# Optimizing a Trainium2 kernel written in Bass

```python
import math
import jax, jax.numpy as jnp
from jax import lax
import numpy as np

D_MODEL = 1024
BATCH = 1
SEQ = 256
DEPTH = 2

N_MIXERS = 2
PLE_DIM = 256
FFN_HIDDEN = ((8 * D_MODEL // 3 + 255) // 256) * 256
DA_HEADS = 8
DA_HEAD_DIM = D_MODEL // (2 * DA_HEADS)
Q_BLOCK = 128
NA_HEADS = 16
NA_HEAD_DIM = D_MODEL // NA_HEADS
GRID_W = 64
NA_KR = 8
NA_KC = 16
NORM_EPS = 1e-6
SUBLN_EPS = 1e-5


def rmsnorm(x, g, eps=NORM_EPS):
    xf = x.astype(jnp.float32)
    y = xf * lax.rsqrt(jnp.mean(xf * xf, axis=-1, keepdims=True) + eps)
    return (y * g.astype(jnp.float32)).astype(x.dtype)

def alibi_slopes(n_heads):
    return jnp.array([2.0 ** (-8.0 * (h + 1) / n_heads) for h in range(n_heads)], dtype=jnp.float32)

def diff_attention(h, w_qkv, w_o, lq1, lk1, lq2, lk2, subln, layer_idx):
    B, S, _ = h.shape
    qkv = h @ w_qkv
    q, k, v = jnp.split(qkv, 3, axis=-1)
    q = q.reshape(B, S, DA_HEADS, 2, DA_HEAD_DIM).transpose(3, 0, 2, 1, 4)
    k = k.reshape(B, S, DA_HEADS, 2, DA_HEAD_DIM).transpose(3, 0, 2, 1, 4)
    v = v.reshape(B, S, DA_HEADS, 2 * DA_HEAD_DIM).transpose(0, 2, 1, 3)
    lam_init = 0.8 - 0.6 * math.exp(-0.3 * layer_idx)
    lam = (jnp.exp(jnp.sum(lq1.astype(jnp.float32) * lk1.astype(jnp.float32)))
           - jnp.exp(jnp.sum(lq2.astype(jnp.float32) * lk2.astype(jnp.float32)))
           + lam_init)
    slopes = alibi_slopes(DA_HEADS)
    scale = DA_HEAD_DIM ** -0.5
    nblk = S // Q_BLOCK
    qb = q.reshape(2, B, DA_HEADS, nblk, Q_BLOCK, DA_HEAD_DIM).transpose(3, 0, 1, 2, 4, 5)
    kpos = jnp.arange(S)

    def block(args):
        qblk, bi = args
        qpos = bi * Q_BLOCK + jnp.arange(Q_BLOCK)
        dist = jnp.abs(qpos[:, None] - kpos[None, :]).astype(jnp.float32)
        bias = -slopes[:, None, None] * dist
        s = jnp.einsum('mbhqd,mbhkd->mbhqk', qblk, k).astype(jnp.float32) * scale + bias
        a = jax.nn.softmax(s, axis=-1)
        a = a[0] - lam * a[1]
        return jnp.einsum('bhqk,bhkd->bhqd', a.astype(v.dtype), v)

    o = lax.map(block, (qb, jnp.arange(nblk)))
    o = o.transpose(1, 0, 3, 2, 4).reshape(B, S, DA_HEADS, 2 * DA_HEAD_DIM)
    o = rmsnorm(o, subln, eps=SUBLN_EPS) * (1.0 - lam_init)
    return o.reshape(B, S, D_MODEL) @ w_o

def neighborhood_attention(h, w_qkv, b_qkv, rpb, w_o):
    B, S, _ = h.shape
    rows = S // GRID_W
    kr = min(NA_KR, rows)
    W = GRID_W
    qkv = h @ w_qkv + b_qkv
    qkv = qkv.reshape(B, rows, W, 3, NA_HEADS, NA_HEAD_DIM).transpose(3, 0, 4, 1, 2, 5)
    q = qkv[0] * (NA_HEAD_DIM ** -0.5)
    k = qkv[1]
    v = qkv[2]
    cols = jnp.arange(W)
    cstart = jnp.clip(cols - NA_KC // 2, 0, W - NA_KC)
    col_mask = (cols[None, :] >= cstart[:, None]) & (cols[None, :] < cstart[:, None] + NA_KC)
    col_off = jnp.clip(cols[None, :] - cols[:, None], -(NA_KC - 1), NA_KC - 1) + (NA_KC - 1)
    rpb_cols = rpb[:, :, col_off]
    key_mask = jnp.tile(col_mask, (1, kr))

    def row_block(r):
        rs = jnp.clip(r - kr // 2, 0, rows - kr)
        kb = lax.dynamic_slice_in_dim(k, rs, kr, axis=2).reshape(B, NA_HEADS, kr * W, NA_HEAD_DIM)
        vb = lax.dynamic_slice_in_dim(v, rs, kr, axis=2).reshape(B, NA_HEADS, kr * W, NA_HEAD_DIM)
        qr = lax.dynamic_index_in_dim(q, r, axis=2, keepdims=False)
        row_off = rs + jnp.arange(kr) - r + (NA_KR - 1)
        bias = jnp.take(rpb_cols, row_off, axis=1)
        bias = bias.transpose(0, 2, 1, 3).reshape(NA_HEADS, W, kr * W).astype(jnp.float32)
        s = jnp.einsum('bhqd,bhkd->bhqk', qr, kb).astype(jnp.float32) + bias
        s = jnp.where(key_mask, s, -jnp.inf)
        a = jax.nn.softmax(s, axis=-1)
        return jnp.einsum('bhqk,bhkd->bhqd', a.astype(vb.dtype), vb)

    o = lax.map(row_block, jnp.arange(rows))
    o = o.transpose(1, 0, 3, 2, 4).reshape(B, S, D_MODEL)
    return o @ w_o

def swiglu(h, w_gate, w_up, w_down):
    return (jax.nn.silu(h @ w_gate) * (h @ w_up)) @ w_down

def first_inputs(seed: int = 0) -> dict:
    key = jax.random.key(seed)
    ks = jax.random.split(key, 24)
    n_a = (DEPTH + 1) // 2
    n_b = DEPTH // 2
    D, F = D_MODEL, FFN_HIDDEN
    f32 = jnp.float32

    def nrm(k, shape, scale):
        return jax.random.normal(k, shape, f32) * scale

    return {
        "x": nrm(ks[0], (BATCH, SEQ, D), 1.0),
        "p": nrm(ks[1], (DEPTH, BATCH, SEQ, PLE_DIM), 1.0),
        "norm_mix": 1.0 + nrm(ks[2], (DEPTH, D), 0.05),
        "norm_ffn": 1.0 + nrm(ks[3], (DEPTH, D), 0.05),
        "norm_ple": 1.0 + nrm(ks[4], (DEPTH, D), 0.05),
        "norm_final": 1.0 + nrm(ks[5], (D,), 0.05),
        "da_w_qkv": nrm(ks[6], (n_a, D, 3 * D), D ** -0.5),
        "da_w_o": nrm(ks[7], (n_a, D, D), D ** -0.5),
        "da_lambda_q1": nrm(ks[8], (n_a, DA_HEAD_DIM), 0.1),
        "da_lambda_k1": nrm(ks[9], (n_a, DA_HEAD_DIM), 0.1),
        "da_lambda_q2": nrm(ks[10], (n_a, DA_HEAD_DIM), 0.1),
        "da_lambda_k2": nrm(ks[11], (n_a, DA_HEAD_DIM), 0.1),
        "da_subln": 1.0 + nrm(ks[12], (n_a, 2 * DA_HEAD_DIM), 0.05),
        "na_w_qkv": nrm(ks[13], (n_b, D, 3 * D), D ** -0.5),
        "na_b_qkv": nrm(ks[14], (n_b, 3 * D), 0.02),
        "na_rpb": nrm(ks[15], (n_b, NA_HEADS, 2 * NA_KR - 1, 2 * NA_KC - 1), 0.5),
        "na_w_o": nrm(ks[16], (n_b, D, D), D ** -0.5),
        "ffn_w_gate": nrm(ks[17], (DEPTH, D, F), D ** -0.5),
        "ffn_w_up": nrm(ks[18], (DEPTH, D, F), D ** -0.5),
        "ffn_w_down": nrm(ks[19], (DEPTH, F, D), F ** -0.5),
        "ple_w_proj": nrm(ks[20], (DEPTH, PLE_DIM, D), PLE_DIM ** -0.5),
        "ple_w_gate": nrm(ks[21], (DEPTH, D, D), D ** -0.5),
    }

def first_block(x, p, norm_mix, norm_ffn, norm_ple, norm_final,
              da_w_qkv, da_w_o, da_lambda_q1, da_lambda_k1, da_lambda_q2, da_lambda_k2, da_subln,
              na_w_qkv, na_b_qkv, na_rpb, na_w_o,
              ffn_w_gate, ffn_w_up, ffn_w_down, ple_w_proj, ple_w_gate):
    h = x
    for i in range(DEPTH):
        hn = rmsnorm(h, norm_mix[i])
        j = i // N_MIXERS
        if i % N_MIXERS == 0:
            mix = diff_attention(hn, da_w_qkv[j], da_w_o[j], da_lambda_q1[j], da_lambda_k1[j],
                                 da_lambda_q2[j], da_lambda_k2[j], da_subln[j], i)
        else:
            mix = neighborhood_attention(hn, na_w_qkv[j], na_b_qkv[j], na_rpb[j], na_w_o[j])
        h = h + mix
        h = h + swiglu(rmsnorm(h, norm_ffn[i]), ffn_w_gate[i], ffn_w_up[i], ffn_w_down[i])
        gate = jax.nn.sigmoid(rmsnorm(h, norm_ple[i]) @ ple_w_gate[i])
        h = h + gate * (p[i] @ ple_w_proj[i])
    return rmsnorm(h, norm_final)


N_HEADS = 16
HEAD_DIM = D_MODEL // N_HEADS
HD = N_HEADS * HEAD_DIM
D_FF = ((8 * D_MODEL + 3 * 256 - 1) // (3 * 256)) * 256
BLOCK_Q = 128
N_A = DEPTH // 2
N_B = DEPTH - N_A
EPS = 1e-6


def rms_norm(x, g):
    xf = x.astype(jnp.float32)
    y = xf * lax.rsqrt(jnp.mean(xf * xf, axis=-1, keepdims=True) + EPS)
    return (y * g.astype(jnp.float32)).astype(x.dtype)

def split_heads(t):
    b, s, _ = t.shape
    return t.reshape(b, s, N_HEADS, HEAD_DIM).transpose(0, 2, 1, 3)

def merge_heads(t):
    b, h, s, d = t.shape
    return t.transpose(0, 2, 1, 3).reshape(b, s, h * d)

def to_blocks(t):
    b, h, s = t.shape[:3]
    t = t.reshape((b, h, s // BLOCK_Q, BLOCK_Q) + t.shape[3:])
    return jnp.moveaxis(t, 2, 0)

def from_blocks(t):
    t = jnp.moveaxis(t, 0, 2)
    b, h, nb, bq, d = t.shape
    return t.reshape(b, h, nb * bq, d)

def stick_breaking_attention(q, k, v):
    s_len = q.shape[2]
    nb = s_len // BLOCK_Q
    kpos = jnp.arange(s_len)
    scale = HEAD_DIM ** -0.5

    def block(args):
        qb, i = args
        tpos = i * BLOCK_Q + jnp.arange(BLOCK_Q)
        z = jnp.einsum('bhqd,bhkd->bhqk', qb, k).astype(jnp.float32) * scale
        strict = kpos[None, :] < tpos[:, None]
        log_one_minus = jnp.where(strict, -jax.nn.softplus(z), 0.0)
        later = lax.cumsum(log_one_minus, axis=3, reverse=True) - log_one_minus
        w = jnp.where(strict, jnp.exp(jax.nn.log_sigmoid(z) + later), 0.0)
        return jnp.einsum('bhqk,bhkd->bhqd', w.astype(v.dtype), v)

    out = lax.map(block, (to_blocks(q), jnp.arange(nb)))
    return from_blocks(out)

def forgetting_attention(q, k, v, f_cum):
    s_len = q.shape[2]
    nb = s_len // BLOCK_Q
    kpos = jnp.arange(s_len)
    scale = HEAD_DIM ** -0.5

    def block(args):
        qb, fb, i = args
        tpos = i * BLOCK_Q + jnp.arange(BLOCK_Q)
        logits = (jnp.einsum('bhqd,bhkd->bhqk', qb, k).astype(jnp.float32) * scale
                  + fb[..., :, None] - f_cum[:, :, None, :])
        causal = kpos[None, :] <= tpos[:, None]
        logits = jnp.where(causal, logits, -jnp.inf)
        probs = jax.nn.softmax(logits, axis=-1)
        return jnp.einsum('bhqk,bhkd->bhqd', probs.astype(v.dtype), v)

    out = lax.map(block, (to_blocks(q), to_blocks(f_cum), jnp.arange(nb)))
    return from_blocks(out)

def swiglu_2(h, w_gu, w_d):
    g, u = jnp.split(h @ w_gu, 2, axis=-1)
    return (jax.nn.silu(g) * u) @ w_d

def second_inputs(seed: int = 0) -> dict:
    key = jax.random.key(seed)
    ks = jax.random.split(key, 20)
    f32 = jnp.float32

    def w(k, shape, fan_in, extra=1.0):
        return jax.random.normal(k, shape, f32) * (fan_in ** -0.5) * extra

    def gain(k, shape):
        return 1.0 + 0.05 * jax.random.normal(k, shape, f32)

    res_scale = (2.0 * DEPTH) ** -0.5
    return {
        'x': jax.random.normal(ks[0], (BATCH, SEQ, D_MODEL), f32),
        'p': jax.random.normal(ks[1], (DEPTH, BATCH, SEQ, PLE_DIM), f32),
        'attn_norm_g': gain(ks[2], (DEPTH, D_MODEL)),
        'sb_w_qkv': w(ks[3], (N_A, D_MODEL, 3 * HD), D_MODEL),
        'sb_w_o': w(ks[4], (N_A, HD, D_MODEL), HD, res_scale),
        'shared_norm_g': gain(ks[5], (D_MODEL,)),
        'shared_w_kvf': w(ks[6], (D_MODEL, 2 * HD + N_HEADS), D_MODEL),
        'shared_b_f': 0.1 * jax.random.normal(ks[7], (N_HEADS,), f32),
        'shared_k_norm_g': gain(ks[8], (HEAD_DIM,)),
        'fox_w_q': w(ks[9], (N_B, D_MODEL, HD), D_MODEL),
        'fox_q_norm_g': gain(ks[10], (N_B, HEAD_DIM)),
        'fox_w_o': w(ks[11], (N_B, HD, D_MODEL), HD, res_scale),
        'ffn_norm_g': gain(ks[12], (DEPTH, D_MODEL)),
        'ffn_w_gu': w(ks[13], (DEPTH, D_MODEL, 2 * D_FF), D_MODEL),
        'ffn_w_d': w(ks[14], (DEPTH, D_FF, D_MODEL), D_FF, res_scale),
        'ple_norm_g': gain(ks[15], (DEPTH, D_MODEL)),
        'ple_w_gate': w(ks[16], (DEPTH, D_MODEL, D_MODEL), D_MODEL),
        'ple_w_proj': w(ks[17], (DEPTH, PLE_DIM, D_MODEL), PLE_DIM, res_scale),
    }

def second_block(x, p, attn_norm_g, sb_w_qkv, sb_w_o, shared_norm_g, shared_w_kvf, shared_b_f,
              shared_k_norm_g, fox_w_q, fox_q_norm_g, fox_w_o, ffn_norm_g, ffn_w_gu, ffn_w_d,
              ple_norm_g, ple_w_gate, ple_w_proj):
    h = x
    k_sh = v_sh = f_cum = None
    for i in range(DEPTH):
        hn = rms_norm(h, attn_norm_g[i])
        if i < N_A:
            q, k, v = jnp.split(hn @ sb_w_qkv[i], 3, axis=-1)
            mix = stick_breaking_attention(split_heads(q), split_heads(k), split_heads(v))
            h = h + merge_heads(mix) @ sb_w_o[i]
        else:
            if i == N_A:
                hs = rms_norm(h, shared_norm_g)
                kvf = hs @ shared_w_kvf
                k_sh = rms_norm(split_heads(kvf[..., :HD]), shared_k_norm_g)
                v_sh = split_heads(kvf[..., HD:2 * HD])
                f_logit = kvf[..., 2 * HD:].astype(jnp.float32) + shared_b_f.astype(jnp.float32)
                f_cum = lax.cumsum(jax.nn.log_sigmoid(f_logit), axis=1).transpose(0, 2, 1)
            j = i - N_A
            q = rms_norm(split_heads(hn @ fox_w_q[j]), fox_q_norm_g[j])
            mix = forgetting_attention(q, k_sh, v_sh, f_cum)
            h = h + merge_heads(mix) @ fox_w_o[j]
        h = h + swiglu_2(rms_norm(h, ffn_norm_g[i]), ffn_w_gu[i], ffn_w_d[i])
        gate = jax.nn.sigmoid(rms_norm(h, ple_norm_g[i]) @ ple_w_gate[i])
        h = h + gate * (p[i] @ ple_w_proj[i])
    return h


def setup_inputs(seed=0):
    out = dict(first_inputs(seed))
    for name, value in second_inputs(seed + 1).items():
        if name != "x":
            out[name + "_2"] = value
    return out


def reference(
    x, p, norm_mix, norm_ffn, norm_ple, norm_final, da_w_qkv, da_w_o, da_lambda_q1,
    da_lambda_k1, da_lambda_q2, da_lambda_k2, da_subln, na_w_qkv, na_b_qkv, na_rpb, na_w_o,
    ffn_w_gate, ffn_w_up, ffn_w_down, ple_w_proj, ple_w_gate, p_2, attn_norm_g_2, sb_w_qkv_2,
    sb_w_o_2, shared_norm_g_2, shared_w_kvf_2, shared_b_f_2, shared_k_norm_g_2, fox_w_q_2,
    fox_q_norm_g_2, fox_w_o_2, ffn_norm_g_2, ffn_w_gu_2, ffn_w_d_2, ple_norm_g_2, ple_w_gate_2,
    ple_w_proj_2,
):
    x = first_block(
        x, p, norm_mix, norm_ffn, norm_ple, norm_final, da_w_qkv, da_w_o, da_lambda_q1,
        da_lambda_k1, da_lambda_q2, da_lambda_k2, da_subln, na_w_qkv, na_b_qkv, na_rpb, na_w_o,
        ffn_w_gate, ffn_w_up, ffn_w_down, ple_w_proj, ple_w_gate,
    )
    return second_block(
        x, p_2, attn_norm_g_2, sb_w_qkv_2, sb_w_o_2, shared_norm_g_2, shared_w_kvf_2,
        shared_b_f_2, shared_k_norm_g_2, fox_w_q_2, fox_q_norm_g_2, fox_w_o_2, ffn_norm_g_2,
        ffn_w_gu_2, ffn_w_d_2, ple_norm_g_2, ple_w_gate_2, ple_w_proj_2,
    )


_drawn_inputs = setup_inputs


def setup_inputs(seed=0):
    import zlib

    import numpy as np

    out = dict(_drawn_inputs(seed))
    spreads = {}
    factors = {'norm_ple': 5.791,
     'da_lambda_k1': 8.0,
     'da_lambda_q2': 8.0,
     'na_b_qkv': 3.836,
     'attn_norm_g_2': 2.789,
     'shared_norm_g_2': 3.397,
     'shared_b_f_2': 5.372,
     'shared_k_norm_g_2': 8.0,
     'fox_q_norm_g_2': 8.0,
     'ple_norm_g_2': 8.0}
    for name, (base, spread) in spreads.items():
        noise = np.random.default_rng([zlib.crc32(name.encode()), seed]).standard_normal(out[name].shape)
        drawn = base * np.exp(spread * noise) if base else spread * noise
        out[name] = __import__('jax').numpy.asarray(drawn.astype(out[name].dtype))
    for name, factor in factors.items():
        out[name] = (out[name] * factor).astype(out[name].dtype)
    return out
```

```python
from contextlib import ExitStack

import math

import concourse.bass as bass
from concourse import mybir

F32 = mybir.dt.float32
F32R = mybir.dt.float32r
BF16 = mybir.dt.bfloat16
ALU = mybir.AluOpType
ACT = mybir.ActivationFunctionType
AX_X = mybir.AxisListType.X

P = 128
S = 256
T = S // P
D = 1024
KB = D // P
F = 2816
GC_COLS = 256
NG = F // GC_COLS
PD = 256
HG = 4
L_DA, L_NA, L_SB, L_FX = range(4)
LAYERS = 4
SCALE = 0.125
LAM_INIT = 0.8 - 0.6 * math.exp(-0.3 * 0)
MASKED = -1e30
EPS = 1e-6
SUB_EPS = 1e-5

RING = 6
AHEAD = RING - 1
U_QKV = 0
U_WO = U_QKV + HG * KB
U_GU0 = U_WO + KB
U_FFN = U_GU0 + 4
U_PROJ_A = U_FFN + 6 * (NG - 1)
U_DOWN_LAST = U_PROJ_A + 1
U_PROJ_B = U_DOWN_LAST + 2
U_GATE = U_PROJ_B + 1
UNITS = U_GATE + KB

G_WO, G_DOWN, G_GATE, GROUPS = 4, 5, 6, 7


def count(labels):
    return {x: n + 1 for n, x in enumerate(labels)}


def steps(s):
    j, r = s // KB - 1, s % KB
    if not (0 <= j < HG):
        return []
    table = {0: ["evac"], 1: ["turnqk"], 2: ["scores0"], 3: ["scores1"], 4: ["turnp0"],
             5: ["pv0", "turnp1"], 6: ["pv1"] + (["turno"] if j == HG - 1 else []),
             7: [] if j == HG - 1 else ["turno"]}
    return [(name, j) for name in table[r]]


def keys(L, t):
    return P if L >= L_SB and t == 0 else S


def p_blocks(L, t):
    n = keys(L, t) // P
    if L == L_DA:
        return [(0, b, k) for b in range(2) for k in range(n)]
    return [(q, b, k) for q in range(2) for b in range(2) for k in range(n)]


def turn_events():
    ev = []
    for L in range(LAYERS):
        for s in range(UNITS):
            if s == 0:
                ev += [("x", L, 0, q) for q in range(4)]
            if L == L_FX and s == 1:
                ev.append(("flog", L))
            if L == L_FX and s == 3:
                ev.append(("flogT", L))
            if L == L_FX and s == 5:
                ev.append(("fcum", L))
            for name, j in steps(s):
                if name == "turnqk":
                    ev += [("qk", L, j, t) for t in range(T)]
                elif name.startswith("turnp"):
                    t = int(name[-1])
                    ev += [("p", L, j, t, n) for n in range(len(p_blocks(L, t)) // 4)]
                elif name.startswith("pv"):
                    ev.append(("pv", L, j, int(name[-1])))
                elif name == "turno":
                    ev.append(("o", L, j))
            if s == U_GU0:
                ev += [("x", L, 1, q) for q in range(4)]
            if s == U_GU0 + 2:
                ev.append(("side", L))
            if U_FFN <= s < U_PROJ_A and (s - U_FFN) % 6 == 1:
                ev += [("g", L, (s - U_FFN) // 6, t) for t in range(T)]
            if s == U_PROJ_A:
                ev += [("g", L, NG - 1, t) for t in range(T)]
            if s == U_GATE:
                ev += [("x", L, 2, q) for q in range(4)]
    return ev


EV_LIST = turn_events()
EV = {x: n for n, x in enumerate(EV_LIST)}
SPLIT = count([x for x in EV_LIST if x[0] in ("x", "o", "g", "side")])
NORMS = [(L, n) for L in range(2) for n in range(3)] + [(1, 3)] + [(L, n) for L in range(2, 4) for n in range(3)]
NORM = count(NORMS)
ATT = count([(L, j, t) for L in range(LAYERS) for j in range(HG) for t in range(T)])
SOFT = count([(L, j, t) for L in (L_DA, L_NA, L_FX) for j in range(HG) for t in range(T)])

GAIN_MIX, GAIN_FFN, GAIN_PLE = [0, 8, 48, 56], [16, 24, 64, 72], [32, 40, 80, 88]
GAIN_SHARED, GAIN_SUB, GAIN_K, GAIN_Q, GAIN_ROWS = 96, 104, 105, 106, 107


def halves(q):
    return q // 2, q % 2


def unit_parts(L, s):
    if s < U_WO:
        kb = s % KB
        if L == L_FX:
            return [(0, 256, GAIN_MIX[L] + kb), (256, 768, GAIN_SHARED + kb)]
        return [(0, 768, GAIN_MIX[L] + kb)]
    if s < U_GU0:
        return [(0, 1024, GAIN_SUB if L == L_DA else None)]
    if s < U_PROJ_A:
        b = s - U_GU0 if s < U_FFN else (s - U_FFN) % 6
        if b < 4:
            return [(0, 512, GAIN_FFN[L] + 2 * b), (512, 1024, GAIN_FFN[L] + 2 * b + 1)]
        return [(0, 1024, None)]
    if s < U_GATE:
        return [(0, 1024, None)]
    return [(0, 1024, GAIN_PLE[L] + s - U_GATE)]


def build(nc, a, out):
    ctx = ExitStack()
    with ctx:
        def sb(name, shape, dt=F32):
            return ctx.enter_context(nc.sbuf_tensor(name, shape, dt))

        def ps(name, shape):
            return ctx.enter_context(nc.psum_tensor(name, shape, F32))

        def sem(name):
            return ctx.enter_context(nc.semaphore(name))

        raw = sb("raw", [P, RING, 1024])
        whi = sb("whi", [P, RING, 1024], F32R)
        wlo = sb("wlo", [P, RING, 1024], F32R)
        h = sb("h", [P, T, D])
        xhi = sb("xhi", [P, KB, S], F32R)
        xlo = sb("xlo", [P, KB, S], F32R)
        ohi = sb("ohi", [P, KB, S], F32R)
        olo = sb("olo", [P, KB, S], F32R)
        ghi = sb("ghi", [P, 2, S], F32R)
        glo = sb("glo", [P, 2, S], F32R)
        phi = sb("phi", [P, 2, S], F32R)
        plo = sb("plo", [P, 2, S], F32R)
        side = sb("side", [P, T, PD])
        qkv = sb("qkv", [P, 2, T, 768])
        qkT = sb("qkT", [P, 4, S])
        z = sb("z", [P, T, 1024])
        aT = sb("aT", [P, T, 1024])
        bias = sb("bias", [P, T, HG, 1024])
        o = sb("o", [P, T, 256])
        nab = sb("nab", [P, 2, 768])
        fin_gain = sb("fin_gain", [P, D])
        ident = sb("ident", [P, P])
        gain_rows = sb("gain_rows", [P, P])
        gain = sb("gain", [P, GAIN_ROWS])
        junk = sb("junk", [P, D], BF16)
        ss = sb("ss", [P, len(NORMS), T])
        rstd = sb("rstd", [P, len(NORMS), T])
        powm = sb("powm", [P, 16])
        mx = sb("mx", [P, T, 4])
        sums = sb("sums", [P, T, 4])
        rsum = sb("rsum", [P, T, 4])
        lamc = sb("lamc", [P, T, 2])
        ss_o = sb("ss_o", [P, T, 2])
        r_o = sb("r_o", [P, T, 2])
        ss_h = sb("ss_h", [P, T, 8])
        r_h = sb("r_h", [P, T, 8])
        lam_in = sb("lam_in", [P, 4, 64])
        lam = sb("lam", [P, 4])
        strict = sb("strict", [P, S])
        incl = sb("incl", [P, P])
        window = sb("window", [P, 64])
        wf = sb("wf", [P, KB, 16])
        wfg = sb("wfg", [P, KB, 16])
        wfhi = sb("wfhi", [P, KB, 16], F32R)
        wflo = sb("wflo", [P, KB, 16], F32R)
        bf = sb("bf", [P, 16])
        f = sb("f", [P, T, 16])
        f2 = sb("f2", [P, T, 16])
        fT, nfcT = o[0:16, 0, :], o[0:16, 1, :]
        ones_sb = sb("ones_sb", [P, 1])
        dist = nab[:, :, 0:S]
        nfc = sb("nfc", [P, T, 16])
        rpb_rows = nab[0:120, 0, S:S + 62].rearrange("p (i c) -> p i c", i=2)
        rpb_back = nab[0:120, 1, S:S + 62].rearrange("p (i c) -> p i c", i=2)
        rpb_dram = nc.dram_tensor("rpb_scratch", (120, 2, 31), F32, kind="Internal").ap()
        nfc_dram = nc.dram_tensor("nfc_scratch", (16, S), F32, kind="Internal").ap()

        acc = [ps(f"acc{b}", [P, 512]) for b in range(4)]
        sc = ps("sc", [P, 2, 512])
        tb = [ps(f"turn{b}", [P, 512]) for b in range(2)]

        weights_in = [sem(f"weights_in{i}") for i in range(RING)]
        hi_done, lo_done, unit_done = sem("hi_done"), sem("lo_done"), sem("unit_done")
        acc_done = sem("acc_done")
        bank_out = [sem(f"bank_out{b}") for b in range(4)]
        gu_done, gu_out = sem("gu_done"), sem("gu_out")
        sig_done, gmid = sem("sig_done"), sem("gmid")
        proj_out, gate_sig = sem("proj_out"), sem("gate_sig")
        turned = sem("turned")
        turn_hi = sem("turn_hi")
        turn_out = [sem(f"turn_out{b}") for b in range(2)]
        x_in, gains_in, side_in, misc_in, nab_in = (sem("x_in"), sem("gains_in"), sem("side_in"), sem("misc_in"),
                                                    [sem(f"nab_in{i}") for i in range(2)])
        gains_turned, gains_ready = sem("gains_turned"), sem("gains_ready")
        consts = sem("consts")
        ss_ready, rstd_ready, fin_ready = sem("ss_ready"), sem("rstd_ready"), sem("fin_ready")
        scores_done, z_ready, mx_ready, e_ready = (sem("scores_done"), sem("z_ready"), sem("mx_ready"),
                                                   sem("e_ready"))
        a_ready, sp_ready, arg_ready = sem("a_ready"), sem("sp_ready"), sem("arg_ready")
        so_ready, ro_ready = sem("so_ready"), sem("ro_ready")
        rpb_load, rpb_store = sem("rpb_load"), sem("rpb_store")
        bias_ready, rpb_in = sem("bias_ready"), sem("rpb_in")
        sq_ready, sh_ready, rh_ready, qk_ready = (sem("sq_ready"), sem("sh_ready"), sem("rh_ready"),
                                                  sem("qk_ready"))
        lam_dot, lam_exp = sem("lam_dot"), sem("lam_exp")
        wf_g, wf_hi, wf_ready = sem("wf_g"), sem("wf_hi"), sem("wf_ready")
        f_ready, f_sp, nfc_ready, nfc_store, nfc_load = (sem("f_ready"), sem("f_sp"), sem("nfc_ready"),
                                                         sem("nfc_store"), sem("nfc_load"))
        act_link, dve_link, pool_link = sem("act_link"), sem("dve_link"), sem("pool_link")
        out_ready, out_stored = sem("out_ready"), sem("out_stored")

        def acc_wait(eng, L, g, b, last):
            if b < 3:
                eng.wait_ge(acc_done, 3 * (GROUPS * L + g) + b + 1)
            else:
                eng.wait_ge(unit_done, UNITS * L + last + 1)

        def wait_out(eng, e):
            eng.wait_ge(turn_out[e % 2], e // 2 + 1)

        def rs(L, n, t):
            i = NORM[(L, n)] - 1
            return rstd[:, i, t:t + 1]

        qkv_w = [a["da_w_qkv"][0], a["na_w_qkv"][0], a["sb_w_qkv_2"][0]]
        wo_w = [a["da_w_o"][0], a["na_w_o"][0], a["sb_w_o_2"][0], a["fox_w_o_2"][0]]

        def gate_up(L):
            if L < 2:
                return a["ffn_w_gate"][L], a["ffn_w_up"][L], 0
            return a["ffn_w_gu_2"][L - 2], a["ffn_w_gu_2"][L - 2], F

        down_w = [a["ffn_w_down"][0], a["ffn_w_down"][1], a["ffn_w_d_2"][0], a["ffn_w_d_2"][1]]
        proj_w = [a["ple_w_proj"][0], a["ple_w_proj"][1], a["ple_w_proj_2"][0], a["ple_w_proj_2"][1]]
        pgate_w = [a["ple_w_gate"][0], a["ple_w_gate"][1], a["ple_w_gate_2"][0], a["ple_w_gate_2"][1]]
        side_x = [a["p"][0, 0], a["p"][1, 0], a["p_2"][0, 0], a["p_2"][1, 0]]

        block = ctx.enter_context(nc.Block())

        @block.sync
        def _(sp):
            def load(u, parts, turns=0):
                if not isinstance(turns, int) or u >= RING:
                    sp.wait_ge(lo_done, turns * 6 + (u - RING + 1))
                for dst, src, n in parts:
                    sp.dma_start(dst, src).then_inc(weights_in[u % RING], 16 * n)

            def rows(w, kb, c0, c1):
                return w[kb * P:(kb + 1) * P, c0:c1]

            def gu_parts(L, u, b, c0):
                gate, up, at = gate_up(L)
                dst = raw[:, u % RING, :].rearrange("p (k s c) -> p s k c", k=2, s=2)
                parts = []
                for sx, (w, off) in enumerate(((gate, 0), (up, at))):
                    src = w[2 * b * P:(2 * b + 2) * P, bass.ds(c0 + off, GC_COLS)]
                    parts.append((dst[:, sx], src.rearrange("(k p) c -> p k c", p=P), 1))
                return parts

            for L in range(LAYERS):
                base = UNITS * L
                for s in range(U_QKV, U_WO):
                    u, j, kb = base + s, s // KB, s % KB
                    dst = raw[:, u % RING, 0:768].rearrange("p (s c) -> p s c", s=3)
                    if L == L_FX:
                        kv = rows(a["shared_w_kvf_2"], kb, 0, 2 * D).rearrange("p (s c) -> p s c", s=2)
                        load(u, [(raw[:, u % RING, 0:256], rows(a["fox_w_q_2"][0], kb, j * 256, j * 256 + 256), 1),
                                 (dst[:, 1:3], kv[:, :, j * 256:j * 256 + 256], 1)])
                    else:
                        w = rows(qkv_w[L], kb, 0, 3 * D).rearrange("p (s c) -> p s c", s=3)
                        load(u, [(dst, w[:, :, j * 256:j * 256 + 256], 2)])
                for kb in range(KB):
                    u = base + U_WO + kb
                    load(u, [(raw[:, u % RING, :], rows(wo_w[L], kb, 0, D), 2)])
                for b in range(4):
                    u = base + U_GU0 + b
                    load(u, gu_parts(L, u, b, 0))
                with sp.Fori(0, NG - 1) as i:
                    for b in range(4):
                        u = base + U_FFN + b
                        load(u, gu_parts(L, u, b, i * GC_COLS + GC_COLS), i)
                    for b in range(2):
                        u = base + U_FFN + 4 + b
                        src = down_w[L].rearrange("(g k p) c -> g k p c", k=2, p=P)[bass.ds(i, 1), b]
                        load(u, [(raw[:, u % RING, :], src.rearrange("g p c -> p (g c)"), 2)], i)

                def proj_parts(u, half):
                    dst = raw[:, u % RING, :].rearrange("p (k c) -> p k c", k=2)
                    return [(dst, proj_w[L][:, half * 512:half * 512 + 512].rearrange("(k p) c -> p k c", p=P), 2)]

                u = base + U_PROJ_A
                load(u, proj_parts(u, 0))
                for b in range(2):
                    u = base + U_DOWN_LAST + b
                    load(u, [(raw[:, u % RING, :], rows(down_w[L], 2 * (NG - 1) + b, 0, D), 2)])
                u = base + U_PROJ_B
                load(u, proj_parts(u, 1))
                for kb in range(KB):
                    u = base + U_GATE + kb
                    load(u, [(raw[:, u % RING, :], rows(pgate_w[L], kb, 0, D), 2)])
            for q in range(4):
                hf, t = halves(q)
                sp.wait_ge(bank_out[q], GROUPS * LAYERS)
                sp.dma_start(out[0, t * P:(t + 1) * P, hf * 512:hf * 512 + 512],
                             h[:, t, hf * 512:hf * 512 + 512]).then_inc(out_stored, 16)
            sp.wait_ge(out_stored, 64)

        @block.gpsimd
        def _(pool):
            links = [0]

            def link(ins):
                links[0] += 1
                ins.then_inc(pool_link, 1)
                pool.wait_ge(pool_link, links[0])

            link(pool.memset(ident[:, :], 0.0))
            pool.affine_select(out=ident[:, :], in_=ident[:, :], compare_op=ALU.not_equal, fill=1.0, base=0,
                               pattern=[[-1, P]], channel_multiplier=1).then_inc(consts, 1)
            link(pool.memset(powm[:, :], -0.5))
            for t in range(T):
                link(pool.iota(dist[:, t, :], pattern=[[-1, S]], base=t * P, channel_multiplier=1,
                               allow_small_or_imprecise_dtypes=True))
                link(pool.tensor_scalar(o[:, t, :], dist[:, t, :], -1.0, 0.0, ALU.mult, ALU.max))
                link(pool.tensor_scalar(dist[:, t, :], dist[:, t, :], 0.0, 1.0, ALU.max, ALU.mult))
                link(pool.tensor_tensor(dist[:, t, :], dist[:, t, :], o[:, t, :], ALU.add))
            for j in range(HG):
                for blk in range(2):
                    slope = 2.0 ** -(2 * j + blk + 1)
                    for t in range(T):
                        for par in range(2):
                            at = par * 512 + blk * 256
                            last = pool.tensor_scalar(bias[:, t, j, at:at + S], dist[:, t, :], -slope, 1.0,
                                                      ALU.mult, ALU.mult)
                last.then_inc(bias_ready, 1)
            link(pool.memset(strict[:, :], 0.0))
            link(pool.affine_select(out=strict[:, P:S], in_=strict[:, P:S], compare_op=ALU.is_gt, fill=MASKED,
                                    base=0, pattern=[[-1, P]], channel_multiplier=1))
            link(pool.memset(incl[:, :], 0.0))
            link(pool.affine_select(out=incl[:, :], in_=incl[:, :], compare_op=ALU.is_ge, fill=MASKED,
                                    base=0, pattern=[[-1, P]], channel_multiplier=1))
            pool.dma_start(rpb_rows[:, :, :], a["na_rpb"].rearrange("l h (r i) c -> (l h r i) c", i=1)
                           .rearrange("(p i) c -> p i c", i=2)).then_inc(rpb_load, 16)
            pool.wait_ge(rpb_load, 16)
            link(pool.tensor_scalar(rpb_back[:, :, :], rpb_rows[:, :, ::-1], 1.0, 1.0, ALU.mult, ALU.mult))
            pool.dma_start(rpb_dram[:, :, :], rpb_back[:, :, :]).then_inc(rpb_store, 16)
            link(pool.memset(window[:, :], 0.0))
            for r in range(2):
                w = window[64 * r:64 * r + 64]
                link(pool.affine_select(out=w[:, 0:48], in_=w[:, 0:48], compare_op=ALU.is_ge, fill=MASKED,
                                        base=8, pattern=[[1, 48]], channel_multiplier=-1))
                link(pool.affine_select(out=w[:, 16:64], in_=w[:, 16:64], compare_op=ALU.is_gt, fill=MASKED,
                                        base=8 - 16, pattern=[[-1, 48]], channel_multiplier=1))

            def rms(dst, src, n, width, eps, ready):
                link(pool.tensor_scalar(dst, src, 1.0 / width, eps, ALU.mult, ALU.add))
                pool.tensor_tensor(dst, dst, powm[:, 0:n], ALU.pow).then_inc(ready, 1)

            def norm(L, n):
                i = NORM[(L, n)] - 1
                pool.wait_ge(ss_ready, 2 * (i + 1))
                rms(rstd[:, i, :], ss[:, i, :], 2, D, EPS, rstd_ready)

            def load_side(L):
                if L:
                    pool.wait_ge(turned, EV[("side", L - 1)] + 1)
                pool.dma_start(side[:, :, :], side_x[L].rearrange("(t p) c -> p t c", p=P)).then_inc(side_in, 16)

            def load_nab(j):
                src = a["na_b_qkv"].rearrange("a (s c) -> a s c", s=3)[:, :, j * 256:j * 256 + 256]
                pool.dma_start(nab[:, j % 2, :].rearrange("p (s c) -> p s c", s=3),
                               src.to_broadcast([P, 3, 256])).then_inc(nab_in[j % 2], 16)

            for L in range(LAYERS):
                load_side(L)
                norm(L, 0)
                if L == L_FX:
                    pool.wait_ge(nfc_ready, 1)
                    pool.dma_start(nfc_dram[:, :], nfcT).then_inc(nfc_store, 16)
                    pool.wait_ge(nfc_store, 16)
                    pool.dma_start(bias[:, 1, :, :].rearrange("p j c -> p (j c)"),
                                   nfc_dram.rearrange("h (a c) -> a (h c)", a=1).to_broadcast([P, 16 * S]))\
                        .then_inc(nfc_load, 16)
                    pool.wait_ge(nfc_load, 16)
                    src = bias[:, 1, :, :].rearrange("p j (x c) -> p (j x) c", c=S)
                    dst = bias[:, 0, :, :].rearrange("p j (x c) -> p (j x) c", c=S)
                    m = incl[:, :].unsqueeze(1).to_broadcast([P, 16, P])
                    pool.tensor_tensor(dst[:, :, 0:P], src[:, :, 0:P], m, ALU.add)
                    pool.tensor_tensor(src[:, :, P:S], src[:, :, P:S], m, ALU.add).then_inc(bias_ready, 1)
                for s in range(U_GU0):
                    if L == L_NA and s < U_WO and s % KB == 0:
                        if s // KB >= 2:
                            pool.wait_ge(bank_out[3], GROUPS * L + s // KB - 1)
                        load_nab(s // KB)
                    for name, j in steps(s):
                        if L == L_FX and name == "evac":
                            for t in range(T):
                                pool.wait_ge(bank_out[t], GROUPS * L + j + 1)
                                pool.wait_ge(bank_out[2 + t], GROUPS * L + j + 1)
                                x = qkv[:, j % 2, t, 0:512]
                                pool.tensor_tensor(z[:, t, 0:512], x, x, ALU.mult).then_inc(sq_ready, 1)
                            for t in range(T):
                                pool.wait_ge(sh_ready, 2 * j + t + 1)
                                rms(r_h[:, t, :], ss_h[:, t, :], 8, 64, EPS, rh_ready)
                        if L == L_DA and name.startswith("pv"):
                            t = int(name[-1])
                            pool.wait_ge(so_ready, 2 * j + t + 1)
                            rms(r_o[:, t, :], ss_o[:, t, :], 2, 128, SUB_EPS, ro_ready)
                norm(L, 1)
                if L == L_DA:
                    pool.wait_ge(rpb_store, 16)
                    pool.wait_ge(z_ready, ATT[(L_DA, HG - 1, T - 1)])
                    for t in range(T):
                        for r2 in range(2):
                            for j in range(HG):
                                for x in range(4):
                                    par, blk = x // 2, x % 2
                                    head = 4 * j + 2 * blk + par
                                    src = bass.AP(tensor=rpb_dram.tensor,
                                                  offset=(head * 15 + 7 - 2 * t - r2) * 31 + 15 - 63,
                                                  ap=[[1, 64], [31, 4], [1, 64]])
                                    dst = bias[64 * r2:64 * r2 + 64, t, j, x * 256:x * 256 + 256]
                                    pool.dma_start(dst.rearrange("p (r c) -> p r c", c=64), src)\
                                        .then_inc(rpb_in, 16)
                    pool.wait_ge(rpb_in, 16 * 64)
                    for t in range(T):
                        b = bias[:, t, :, :].rearrange("p j (r c) -> p (j r) c", c=64)
                        pool.tensor_tensor(b, b, window[:, ::-1].unsqueeze(1).to_broadcast([P, 64, 64]), ALU.add)\
                            .then_inc(bias_ready, 1)
                norm(L, 2)
                if L == 1:
                    norm(L, 3)

        @block.scalar
        def _(act):
            links = [0]

            def link(ins):
                links[0] += 1
                ins.then_inc(act_link, 1)
                act.wait_ge(act_link, links[0])

            for t in range(T):
                act.dma_start(h[:, t, :], a["x"][0, t * P:(t + 1) * P, :]).then_inc(x_in, 16)
            vecs = [("norm_mix", 0, 16), ("norm_ffn", 16, 16), ("norm_ple", 32, 16), ("attn_norm_g_2", 48, 16),
                    ("ffn_norm_g_2", 64, 16), ("ple_norm_g_2", 80, 16)]
            for name, r, n in vecs:
                act.dma_start(gain_rows[r:r + n, :], a[name].rearrange("l (k p) -> (l k) p", p=P))\
                    .then_inc(gains_in, 16)
            act.dma_start(gain_rows[96:104, :], a["shared_norm_g_2"].rearrange("(k p) -> k p", p=P))\
                .then_inc(gains_in, 16)
            act.dma_start(gain_rows[104:105, :], a["da_subln"]).then_inc(gains_in, 16)
            for i in range(2):
                act.dma_start(gain_rows[105:106, 64 * i:64 * i + 64],
                              a["shared_k_norm_g_2"].rearrange("(a p) -> a p", a=1)).then_inc(gains_in, 16)
                act.dma_start(gain_rows[106:107, 64 * i:64 * i + 64], a["fox_q_norm_g_2"]).then_inc(gains_in, 16)
            for i, name in enumerate(("da_lambda_q1", "da_lambda_k1", "da_lambda_q2", "da_lambda_k2")):
                act.dma_start(lam_in[:, i, :], a[name].to_broadcast([P, 64])).then_inc(misc_in, 16)
            act.dma_start(fin_gain[:, :], a["norm_final"].rearrange("(a p) -> a p", a=1).to_broadcast([P, D]))\
                .then_inc(misc_in, 16)
            act.dma_start(wf[:, :, :], a["shared_w_kvf_2"][:, 2 * D:2 * D + 16].rearrange("(k p) c -> p k c", p=P))\
                .then_inc(misc_in, 16)
            act.dma_start(bf[:, :], a["shared_b_f_2"].rearrange("(a p) -> a p", a=1).to_broadcast([P, 16]))\
                .then_inc(misc_in, 16)

            def split(u, parts, turns=0):
                act.wait_ge(weights_in[u % RING], turns * 32 + 32 * (u // RING + 1))
                if not isinstance(turns, int) or u >= RING:
                    act.wait_ge(unit_done, turns * 6 + (u - RING + 1))
                for c0, c1, g in parts:
                    scale = 1.0 if g is None else gain[:, g:g + 1]
                    ins = act.activation(whi[:, u % RING, c0:c1], raw[:, u % RING, c0:c1], ACT.Copy, scale=scale)
                ins.then_inc(hi_done, 1)

            def split_ahead(L, s):
                u = UNITS * L + s + AHEAD
                if u < LAYERS * UNITS:
                    split(u, unit_parts(u // UNITS, u % UNITS))

            def norm(L, n):
                i = NORM[(L, n)] - 1
                for t in range(T):
                    if 2 * i + t:
                        act.wait_ge(ss_ready, 2 * i + t)
                    act.activation(junk[:, :], h[:, t, :], ACT.Square, accum_out=ss[:, i, t:t + 1])\
                        .then_inc(ss_ready, 1)

            def turn_x(L, n):
                for q in range(4):
                    hf, t = halves(q)
                    e = EV[("x", L, n, q)]
                    act.wait_ge(turned, e + 1)
                    act.activation(xhi[:, 4 * hf:4 * hf + 4, t * P:(t + 1) * P],
                                   tb[e % 2][:, :].rearrange("p (k c) -> p k c", k=4), ACT.Copy).then_inc(turn_hi, 1)
                norm(L, n)

            def attention(L, name, j):
                t = int(name[-1]) if name[-1] in "01" else 0
                B = j % 2
                kk = keys(L, t)
                zt = z[:, t, :].rearrange("p (x c) -> p x c", c=S)[:, :, 0:kk]
                if name == "evac":
                    if L == L_NA:
                        return
                    act.wait_ge(rstd_ready, NORM[(L, 0)])
                    at = 256 if L == L_FX else 0
                    for t in range(T):
                        acc_wait(act, L, j, t, KB * j + KB - 1)
                        act.activation(qkv[:, B, t, at:at + 512], acc[t][:, :], ACT.Copy, scale=rs(L, 0, t))\
                            .then_inc(bank_out[t], 1)
                elif name == "turnqk":
                    for t in range(T):
                        e = EV[("qk", L, j, t)]
                        act.wait_ge(turned, e + 1)
                        src = tb[e % 2][:, :].rearrange("p (k c) -> p k c", k=4)
                        dst = qkT[:, :, t * P:(t + 1) * P]
                        if L == L_FX:
                            act.activation(dst[:, 0:2], src[:, 0:2], ACT.Copy, scale=gain[:, GAIN_Q:GAIN_Q + 1])
                            ins = act.activation(dst[:, 2:4], src[:, 2:4], ACT.Copy,
                                                 scale=gain[:, GAIN_K:GAIN_K + 1])
                        else:
                            ins = act.activation(dst, src, ACT.Copy)
                        ins.then_inc(turn_out[e % 2], 1)
                elif name.startswith("scores"):
                    if L == L_SB:
                        act.wait_ge(z_ready, ATT[(L, j, t)])
                        tmp = aT[:, t, :].rearrange("p (x c) -> p x c", c=S)[:, :, 0:kk]
                        link(act.activation(tmp, zt, ACT.Abs))
                        link(act.activation(tmp, tmp, ACT.Exp, scale=-1.0))
                        act.activation(tmp, tmp, ACT.Ln, bias=1.0).then_inc(sp_ready, 1)
                        if t == 1:
                            stick(j, 0)
                    else:
                        act.wait_ge(mx_ready, SOFT[(L, j, t)])
                        for x in range(4):
                            ins = act.activation(zt[:, x, :], zt[:, x, :], ACT.Exp, bias=mx[:, t, x:x + 1],
                                                 accum_out=sums[:, t, x:x + 1])
                        ins.then_inc(e_ready, 1)
                elif name.startswith("turnp"):
                    e = EV[("p", L, j, t, 0)]
                    act.wait_ge(turned, e + 1)
                    act.activation(aT[:, t, 0:512], tb[e % 2][:, :], ACT.Copy).then_inc(turn_out[e % 2], 1)
                    if L == L_SB and t == 0:
                        stick(j, 1)
                elif name.startswith("pv"):
                    e = EV[("pv", L, j, t)]
                    if L == L_DA:
                        act.wait_ge(turned, e + 1)
                        for x in range(2):
                            ins = act.activation(aT[:, t, x * P:(x + 1) * P], tb[e % 2][:, x * P:(x + 1) * P], ACT.Square,
                                                 accum_out=ss_o[:, t, x:x + 1])
                        ins.then_inc(so_ready, 1)
                    if L == L_SB:
                        act.wait_ge(turned, e + 1)
                        act.activation(o[:, t, :], tb[e % 2][:, 0:256], ACT.Copy).then_inc(turn_out[e % 2], 1)
                elif name == "turno":
                    e = EV[("o", L, j)]
                    act.wait_ge(turned, e + 1)
                    act.activation(ohi[:, 2 * j:2 * j + 2, :], tb[e % 2][:, :].rearrange("p (k c) -> p k c", k=2),
                                   ACT.Copy).then_inc(turn_hi, 1)

            def stick(j, t):
                kk = keys(L_SB, t)
                zt = z[:, t, :].rearrange("p (x c) -> p x c", c=S)[:, :, 0:kk]
                act.wait_ge(arg_ready, 2 * j + t + 1)
                act.activation(zt, zt, ACT.Exp).then_inc(e_ready, 1)

            def hidden_sig(L, t, g):
                act.activation(aT[:, 0, t * 256:t * 256 + 256], sc[:, t, 0:256], ACT.Sigmoid, scale=rs(L, 1, t))\
                    .then_inc(sig_done, 1)

            act.wait_ge(gains_ready, 1)
            for u in range(AHEAD):
                split(u, unit_parts(0, u))
            for L in range(LAYERS):
                base = UNITS * L
                for s in range(U_FFN):
                    if s == 0:
                        turn_x(L, 0)
                    if s == U_GU0:
                        turn_x(L, 1)
                    for name, j in steps(s):
                        attention(L, name, j)
                    if L == L_DA and s == 2:
                        act.wait_ge(lam_dot, 2)
                        act.activation(lam[:, 2:4], lam[:, 0:2], ACT.Exp).then_inc(lam_exp, 1)
                    if L == L_SB and s == 2:
                        act.wait_ge(wf_g, 1)
                        act.activation(wfhi[:, :, :], wfg[:, :, :], ACT.Copy).then_inc(wf_hi, 1)
                    if L == L_FX and s == 2:
                        wait_out(act, EV[("flog", L)])
                        link(act.activation(f2[:, :, :], f[:, :, :], ACT.Abs))
                        link(act.activation(f2[:, :, :], f2[:, :, :], ACT.Exp, scale=-1.0))
                        act.activation(f2[:, :, :], f2[:, :, :], ACT.Ln, bias=1.0).then_inc(f_sp, 1)
                    if s == U_GU0 + 2:
                        e = EV[("side", L)]
                        act.wait_ge(turned, e + 1)
                        act.activation(phi[:, :, :], tb[e % 2][:, :].rearrange("p (k c) -> p k c", k=2), ACT.Copy)\
                            .then_inc(turn_hi, 1)
                    split_ahead(L, s)

                g0 = 13 * L
                act.wait_ge(rstd_ready, NORM[(L, 1)])
                act.wait_ge(gu_done, g0 + 1)
                hidden_sig(L, 0, 0)
                act.wait_ge(unit_done, base + U_GU0 + 4)
                hidden_sig(L, 1, 0)

                def ffn_body(i, peeled):
                    for b in range(6):
                        if b == 1:
                            for t in range(T):
                                e = EV[("g", L, 0, t)]
                                act.wait_ge(turned, i * 2 + (e + 1))
                                act.activation(ghi[:, :, t * P:(t + 1) * P],
                                               tb[e % 2][:, 0:256].rearrange("p (k c) -> p k c", k=2),
                                               ACT.Copy).then_inc(turn_hi, 1)
                        if b == 4:
                            act.wait_ge(gu_done, i + (g0 + 2))
                            hidden_sig(L, 0, i)
                            act.wait_ge(unit_done, i * 6 + (base + U_FFN + 4))
                            hidden_sig(L, 1, i)
                        if peeled:
                            split_ahead(L, U_FFN + 6 * i + b)
                        else:
                            u = base + U_FFN + b + AHEAD
                            split(u, unit_parts(L, U_FFN + b + AHEAD), i)

                with act.Fori(0, NG - 2) as i:
                    ffn_body(i, False)
                ffn_body(NG - 2, True)

                for s in range(U_PROJ_A, UNITS):
                    if s == U_PROJ_A:
                        for t in range(T):
                            e = EV[("g", L, NG - 1, t)]
                            act.wait_ge(turned, e + 1)
                            act.activation(ghi[:, :, t * P:(t + 1) * P],
                                           tb[e % 2][:, 0:256].rearrange("p (k c) -> p k c", k=2),
                                           ACT.Copy).then_inc(turn_hi, 1)
                    if s in (U_DOWN_LAST, U_GATE):
                        hf = 0 if s == U_DOWN_LAST else 1
                        for t in range(T):
                            if t == 0:
                                act.wait_ge(gu_done, g0 + 12 + hf)
                            else:
                                act.wait_ge(unit_done, base + (U_PROJ_B if hf else U_PROJ_A) + 1)
                            act.activation(z[:, t, hf * 512:hf * 512 + 512], sc[:, t, :], ACT.Copy)\
                                .then_inc(proj_out, 1)
                    if s == U_GATE:
                        turn_x(L, 2)
                    split_ahead(L, s)
                act.wait_ge(rstd_ready, NORM[(L, 2)])
                for q in range(4):
                    hf, t = halves(q)
                    acc_wait(act, L, G_GATE, q, UNITS - 1)
                    act.activation(aT[:, t, hf * 512:hf * 512 + 512], acc[q][:, :], ACT.Sigmoid,
                                   scale=rs(L, 2, t)).then_inc(gate_sig, 1)
                if L == 1:
                    for q in range(4):
                        act.wait_ge(bank_out[q], GROUPS * L + G_GATE + 1)
                    norm(L, 3)

        @block.vector
        def _(dve):
            links = [0]

            def link(ins):
                links[0] += 1
                ins.then_inc(dve_link, 1)
                dve.wait_ge(dve_link, links[0])

            def split(u, parts, turns=0):
                dve.wait_ge(hi_done, turns * 6 + (u + 1))
                for c0, c1, g in parts:
                    w, hi, lo = (x[:, u % RING, c0:c1] for x in (raw, whi, wlo))
                    if g is None:
                        ins = dve.tensor_tensor(lo, w, hi.bitcast(F32), ALU.subtract)
                    else:
                        ins = dve.scalar_tensor_tensor(out=lo, in0=w, scalar=gain[:, g:g + 1],
                                                       in1=hi.bitcast(F32), op0=ALU.mult, op1=ALU.subtract)
                ins.then_inc(lo_done, 1)

            def split_ahead(L, s):
                u = UNITS * L + s + AHEAD
                if u < LAYERS * UNITS:
                    split(u, unit_parts(u // UNITS, u % UNITS))

            def lo_half(label, lo, hi, src, e, turns=0, per=0):
                dve.wait_ge(turn_hi, turns * per + SPLIT[label])
                dve.tensor_tensor(lo, src, hi.bitcast(F32), ALU.subtract).then_inc(turn_out[e % 2], 1)

            def turn_x(L, n):
                for q in range(4):
                    hf, t = halves(q)
                    e = EV[("x", L, n, q)]
                    at = (slice(None), slice(4 * hf, 4 * hf + 4), slice(t * P, (t + 1) * P))
                    lo_half(("x", L, n, q), xlo[at], xhi[at],
                            tb[e % 2][:, :].rearrange("p (k c) -> p k c", k=4), e)

            def add_to_h(L, g, last):
                for q in range(4):
                    hf, t = halves(q)
                    acc_wait(dve, L, g, q, last)
                    hq = h[:, t, hf * 512:hf * 512 + 512]
                    dve.tensor_tensor(hq, acc[q][:, :], hq, ALU.add).then_inc(bank_out[q], 1)

            def scores(L, j, t):
                kk = keys(L, t)
                zt = z[:, t, :].rearrange("p (x c) -> p x c", c=S)[:, :, 0:kk]
                src = sc[:, :, :].rearrange("p q (b c) -> p (q b) c", c=S)[:, :, 0:kk]
                if L == L_DA:
                    dve.wait_ge(bias_ready, j + 1)
                elif L in (L_NA, L_SB):
                    dve.wait_ge(bias_ready, HG + T)
                elif L == L_FX:
                    dve.wait_ge(bias_ready, HG + T + 1)
                if L == L_SB:
                    m = strict[:, S - kk:S] if t == 0 else strict[:, :]
                    add = m.unsqueeze(1).to_broadcast([P, 4, kk])
                else:
                    add = bias[:, t, j, :].rearrange("p (x c) -> p x c", c=S)[:, :, 0:kk]
                dve.wait_ge(scores_done, ATT[(L, j, t)])
                if L == L_NA:
                    add = bias[:, t, j, :].rearrange("p (x c) -> p x c", c=64)[:, :, ::-1]
                    src = sc[:, :, :].rearrange("p q (x c) -> p (q x) c", c=64)
                    zt = z[:, t, :].rearrange("p (x c) -> p x c", c=64)
                dve.scalar_tensor_tensor(out=zt, in0=src, scalar=SCALE, in1=add, op0=ALU.mult,
                                         op1=ALU.add).then_inc(z_ready, 1)
                if L == L_SB:
                    return
                dve.wait_ge(z_ready, ATT[(L, j, t)])
                zt = z[:, t, :].rearrange("p (x c) -> p x c", c=S)[:, :, 0:kk]
                red = dve.tensor_reduce(mx[:, t, :], zt, AX_X, ALU.max, negate=True)
                if L == L_FX:
                    link(red)
                    fq = nfc[:, t, 4 * j:4 * j + 4]
                    link(dve.tensor_tensor(mx[:, t, :], mx[:, t, :], fq, ALU.add))
                    red = dve.tensor_tensor(mx[:, t, :], mx[:, t, :], fq, ALU.subtract)
                red.then_inc(mx_ready, 1)

            def after_exp(L, j, t):
                kk = keys(L, t)
                if L == L_SB:
                    zt = z[:, t, :].rearrange("p (x c) -> p x c", c=S)[:, :, 0:kk]
                    tmp = aT[:, t, :].rearrange("p (x c) -> p x c", c=S)[:, :, 0:kk]
                    dve.wait_ge(sp_ready, 2 * j + t + 1)
                    link(dve.scalar_tensor_tensor(out=tmp, in0=zt, scalar=0.0, in1=tmp, op0=ALU.max, op1=ALU.add))
                    for x in range(4):
                        back = tmp[:, x, ::-1]
                        ins = dve.tensor_tensor_scan(back, ones_sb[:, 0:1].to_broadcast([P, kk]), back, 0.0,
                                                     ALU.mult, ALU.add)
                    link(ins)
                    dve.tensor_tensor(zt, zt, tmp, ALU.subtract).then_inc(arg_ready, 1)
                    return
                dve.wait_ge(e_ready, ATT[(L, j, t)])
                link(dve.reciprocal(rsum[:, t, :], sums[:, t, :]))
                if L == L_DA:
                    link(dve.tensor_scalar(lamc[:, t, :], rsum[:, t, 2:4], lam[:, 1:2], None, ALU.mult))
                    for b in range(2):
                        e0, e1 = (z[:, t, q * 512 + b * 256:q * 512 + b * 256 + 256] for q in range(2))
                        link(dve.tensor_scalar(e1, e1, lamc[:, t, b:b + 1], None, ALU.mult))
                        ins = dve.scalar_tensor_tensor(out=e0, in0=e0, scalar=rsum[:, t, b:b + 1], in1=e1,
                                                       op0=ALU.mult, op1=ALU.add)
                    ins.then_inc(a_ready, 1)

            def attention(L, name, j):
                t = int(name[-1]) if name[-1] in "01" else 0
                B = j % 2
                last = KB * j + KB - 1
                if name == "evac":
                    dve.wait_ge(rstd_ready, NORM[(L, 0)])
                    if L == L_NA:
                        dve.wait_ge(nab_in[B], 16 * (j // 2 + 1))
                        for b in range(4):
                            half, t = b // 2, b % 2
                            c0, c1 = (0, 512) if half == 0 else (512, 768)
                            acc_wait(dve, L, j, b, last)
                            dve.scalar_tensor_tensor(out=qkv[:, B, t, c0:c1], in0=acc[b][:, 0:c1 - c0],
                                                     scalar=rs(L, 0, t), in1=nab[:, B, c0:c1], op0=ALU.mult,
                                                     op1=ALU.add).then_inc(bank_out[b], 1)
                    else:
                        at = 0 if L == L_FX else 512
                        for t in range(T):
                            acc_wait(dve, L, j, 2 + t, last)
                            dve.tensor_scalar(qkv[:, B, t, at:at + 256], acc[2 + t][:, 0:256], rs(L, 0, t), None,
                                              ALU.mult).then_inc(bank_out[2 + t], 1)
                    if L == L_FX:
                        for t in range(T):
                            dve.wait_ge(sq_ready, 2 * j + t + 1)
                            dve.tensor_reduce(ss_h[:, t, :], z[:, t, 0:512].rearrange("p (x c) -> p x c", c=64),
                                              AX_X, ALU.add).then_inc(sh_ready, 1)
                        for t in range(T):
                            dve.wait_ge(rh_ready, 2 * j + t + 1)
                            x = qkv[:, B, t, 0:512].rearrange("p (x c) -> p x c", c=64)
                            dve.tensor_tensor(x, x, r_h[:, t, :].unsqueeze(2).to_broadcast([P, 8, 64]), ALU.mult)\
                                .then_inc(qk_ready, 1)
                elif name == "scores0":
                    scores(L, j, 0)
                elif name == "scores1":
                    scores(L, j, 1)
                    after_exp(L, j, 0)
                elif name.startswith("turnp"):
                    if t == 0:
                        after_exp(L, j, 1)
                    if ("p", L, j, t, 1) in EV:
                        e = EV[("p", L, j, t, 1)]
                        dve.wait_ge(turned, e + 1)
                        dve.tensor_copy(aT[:, t, 512:1024], tb[e % 2][:, :]).then_inc(turn_out[e % 2], 1)
                elif name.startswith("pv"):
                    e = EV[("pv", L, j, t)]
                    src = tb[e % 2]
                    if L == L_DA:
                        dve.wait_ge(ro_ready, 2 * j + t + 1)
                        dve.tensor_tensor(o[:, t, :].rearrange("p (x c) -> p x c", x=2),
                                          src[:, 0:256].rearrange("p (x c) -> p x c", x=2),
                                          r_o[:, t, :].unsqueeze(2).to_broadcast([P, 2, P]), ALU.mult)\
                            .then_inc(turn_out[e % 2], 1)
                    elif L != L_SB:
                        dve.wait_ge(turned, e + 1)
                        r = rsum[:, t, :].rearrange("p (q b) -> p b q", q=2)
                        dve.tensor_tensor(o[:, t, :].rearrange("p (b q c) -> p b q c", b=2, q=2),
                                          src[:, 0:256].rearrange("p (b q c) -> p b q c", b=2, q=2),
                                          r.unsqueeze(3).to_broadcast([P, 2, 2, 64]), ALU.mult)\
                            .then_inc(turn_out[e % 2], 1)
                elif name == "turno":
                    e = EV[("o", L, j)]
                    at = (slice(None), slice(2 * j, 2 * j + 2))
                    lo_half(("o", L, j), olo[at], ohi[at], tb[e % 2][:, :].rearrange("p (k c) -> p k c", k=2), e)

            def hidden(L, wait_base, turns=0, per=0):
                for t in range(T):
                    sg = aT[:, 0, t * 256:t * 256 + 256]
                    dve.wait_ge(sig_done, turns * per + (wait_base + t + 1))
                    dve.scalar_tensor_tensor(out=sg, in0=sc[:, t, 256:512], scalar=rs(L, 1, t), in1=sg,
                                             op0=ALU.mult, op1=ALU.mult).then_inc(gmid, 1)
                for t in range(T):
                    sg = aT[:, 0, t * 256:t * 256 + 256]
                    dve.wait_ge(gmid, turns * per + (wait_base + t + 1))
                    dve.scalar_tensor_tensor(out=aT[:, 1, t * 256:t * 256 + 256], in0=sc[:, t, 0:256],
                                             scalar=rs(L, 1, t), in1=sg, op0=ALU.mult, op1=ALU.mult)\
                        .then_inc(gu_out, 1)

            dve.memset(ones_sb[:, :], 1.0).then_inc(consts, 1)
            dve.wait_ge(gains_turned, 1)
            link(dve.tensor_copy(gain[:, :], tb[0][:, 0:GAIN_ROWS]))
            dve.tensor_scalar(gain[:, GAIN_SUB:GAIN_SUB + 1], gain[:, GAIN_SUB:GAIN_SUB + 1], 1.0 - LAM_INIT, None,
                              ALU.mult).then_inc(gains_ready, 1)
            dve.wait_ge(gains_ready, 1)
            for u in range(AHEAD):
                split(u, unit_parts(0, u))
            for L in range(LAYERS):
                base = UNITS * L
                for s in range(U_FFN):
                    if s == 0:
                        turn_x(L, 0)
                    if s == U_GU0:
                        add_to_h(L, G_WO, U_GU0 - 1)
                        turn_x(L, 1)
                    for name, j in steps(s):
                        attention(L, name, j)
                    if L == L_DA and s == 1:
                        dve.wait_ge(misc_in, 16 * 7)
                        for i in range(2):
                            dve.tensor_tensor_reduce(out=lam_in[:, 2 * i, :], in0=lam_in[:, 2 * i, :],
                                                     in1=lam_in[:, 2 * i + 1, :], scale=1.0, scalar=0.0,
                                                     op0=ALU.mult, op1=ALU.add, accum_out=lam[:, i:i + 1])\
                                .then_inc(lam_dot, 1)
                    if L == L_DA and s == 3:
                        dve.wait_ge(lam_exp, 1)
                        link(dve.tensor_tensor(lam[:, 0:1], lam[:, 3:4], lam[:, 2:3], ALU.subtract))
                        link(dve.tensor_scalar(lam[:, 1:2], lam[:, 0:1], -LAM_INIT, None, ALU.add))
                    if L == L_SB and s == 1:
                        dst = wfg[:, :, :].rearrange("p k (j q b) -> p q (k j) b", q=2, b=2)
                        src = wf[:, :, :].rearrange("p k (j b q) -> p q (k j) b", q=2, b=2)
                        for kb in range(KB):
                            for q in range(2):
                                gg = gain[:, GAIN_SHARED + kb:GAIN_SHARED + kb + 1]
                                ins = dve.tensor_scalar(dst[:, q, 4 * kb:4 * kb + 4], src[:, q, 4 * kb:4 * kb + 4],
                                                        gg, None, ALU.mult)
                        ins.then_inc(wf_g, 1)
                    if L == L_SB and s == 3:
                        dve.wait_ge(wf_hi, 1)
                        dve.tensor_tensor(wflo[:, :, :], wfg[:, :, :], wfhi[:, :, :].bitcast(F32), ALU.subtract)\
                            .then_inc(wf_ready, 1)
                    if L == L_FX and s == 1:
                        e = EV[("flog", L)]
                        dve.wait_ge(rstd_ready, NORM[(L, 0)])
                        dve.wait_ge(turned, e + 1)
                        bp = bf[:, :].rearrange("p (j b q) -> p q j b", q=2, b=2)
                        for t in range(T):
                            for q in range(2):
                                fd = f[:, t, :].rearrange("p (j q b) -> p q j b", q=2, b=2)[:, q]
                                fs = tb[e % 2][:, 16 * t:16 * t + 16].rearrange("p (j q b) -> p q j b", q=2, b=2)[:, q]
                                ins = dve.scalar_tensor_tensor(out=fd, in0=fs, scalar=rs(L, 0, t), in1=bp[:, q],
                                                               op0=ALU.mult, op1=ALU.add)
                        ins.then_inc(turn_out[e % 2], 1)
                    if L == L_FX and s == 2:
                        dve.wait_ge(f_sp, 1)
                        link(dve.tensor_scalar(f[:, :, :], f[:, :, :], 0.0, None, ALU.min))
                        dve.tensor_tensor(f2[:, :, :], f2[:, :, :], f[:, :, :], ALU.subtract).then_inc(f_ready, 1)
                    if L == L_FX and s == 3:
                        e = EV[("flogT", L)]
                        dve.wait_ge(turned, e + 1)
                        dve.tensor_copy(fT, tb[e % 2][0:16, 0:S]).then_inc(turn_out[e % 2], 1)
                        wait_out(dve, e)
                        dve.wait_ge(consts, 2)
                        dve.tensor_tensor_scan(nfcT, ones_sb[0:16, 0:1].to_broadcast([16, S]), fT, 0.0, ALU.mult, ALU.add)\
                            .then_inc(nfc_ready, 1)
                    if L == L_FX and s == 5:
                        e = EV[("fcum", L)]
                        dve.wait_ge(turned, e + 1)
                        ins = dve.tensor_copy(nfc[:, :, :], tb[e % 2][:, 0:32].rearrange("p (t c) -> p t c", t=T))
                        ins.then_inc(turn_out[e % 2], 1)
                        wait_out(dve, e)
                    if s == U_GU0 + 2:
                        e = EV[("side", L)]
                        lo_half(("side", L), plo[:, :, :], phi[:, :, :],
                                tb[e % 2][:, :].rearrange("p (k c) -> p k c", k=2), e)
                    split_ahead(L, s)

                dve.wait_ge(rstd_ready, NORM[(L, 1)])
                hidden(L, 2 * NG * L)

                def ffn_body(i, peeled):
                    for b in range(6):
                        if b == 1:
                            for t in range(T):
                                e = EV[("g", L, 0, t)]
                                at = (slice(None), slice(None), slice(t * P, (t + 1) * P))
                                lo_half(("g", L, 0, t), glo[at], ghi[at],
                                        tb[e % 2][:, 0:256].rearrange("p (k c) -> p k c", k=2), e, i, 2)
                        if b == 4:
                            hidden(L, 2 * NG * L + 2, i, 2)
                        if peeled:
                            split_ahead(L, U_FFN + 6 * i + b)
                        else:
                            split(base + U_FFN + b + AHEAD, unit_parts(L, U_FFN + b + AHEAD), i)

                with dve.Fori(0, NG - 2) as i:
                    ffn_body(i, False)
                ffn_body(NG - 2, True)

                for s in range(U_PROJ_A, UNITS):
                    if s == U_PROJ_A:
                        for t in range(T):
                            e = EV[("g", L, NG - 1, t)]
                            at = (slice(None), slice(None), slice(t * P, (t + 1) * P))
                            lo_half(("g", L, NG - 1, t), glo[at], ghi[at],
                                    tb[e % 2][:, 0:256].rearrange("p (k c) -> p k c", k=2), e)
                    if s == U_PROJ_B:
                        add_to_h(L, G_DOWN, U_PROJ_B - 1)
                    if s == U_GATE:
                        turn_x(L, 2)
                    split_ahead(L, s)
                for q in range(4):
                    hf, t = halves(q)
                    c = slice(hf * 512, hf * 512 + 512)
                    dve.wait_ge(gate_sig, 4 * L + q + 1)
                    dve.wait_ge(proj_out, 4 * L + q + 1)
                    link(dve.tensor_tensor(aT[:, t, c], aT[:, t, c], z[:, t, c], ALU.mult))
                    dve.tensor_tensor(h[:, t, c], h[:, t, c], aT[:, t, c], ALU.add).then_inc(bank_out[q], 1)
                if L == 1:
                    dve.wait_ge(rstd_ready, NORM[(1, 3)])
                    dve.wait_ge(misc_in, 16 * 7)
                    for q in range(4):
                        hf, t = halves(q)
                        c = slice(hf * 512, hf * 512 + 512)
                        dve.scalar_tensor_tensor(out=h[:, t, c], in0=h[:, t, c], scalar=rs(1, 3, t),
                                                 in1=fin_gain[:, c], op0=ALU.mult, op1=ALU.mult)\
                            .then_inc(fin_ready, 1)

        @block.tensor
        def _(pe):
            def use(e, turns=0):
                if e >= 2:
                    pe.wait_ge(turn_out[e % 2], turns + e // 2)

            def ready(u, turns=0):
                pe.wait_ge(lo_done, turns * 6 + (u + 1))

            def three(dst, xh, xl, wh, wl, first, last):
                pe.matmul(dst, xh, wh, start=first, stop=False)
                pe.matmul(dst, xh, wl, start=False, stop=False)
                return pe.matmul(dst, xl, wh, start=False, stop=last)

            def wide_unit(L, s, kb, xh, xl, first, last, g, segs, turns=0, tiles=None):
                u = UNITS * L + s
                ready(u, turns)
                for b in range(4):
                    seg, t = b // 2, b % 2
                    if first and GROUPS * L + g:
                        pe.wait_ge(bank_out[b], GROUPS * L + g)
                    c0, c1 = segs[seg]
                    ins = three(acc[b][:, 0:c1 - c0], xh[:, kb, t * P:(t + 1) * P], xl[:, kb, t * P:(t + 1) * P],
                                whi[:, u % RING, c0:c1], wlo[:, u % RING, c0:c1], first, last)
                    if last and b < 3:
                        ins.then_inc(acc_done, 1)
                ins.then_inc(unit_done, 1)

            def gu_unit(L, s, b, turns=0):
                u = UNITS * L + s
                ready(u, turns)
                for t in range(T):
                    if b == 0:
                        if s == U_GU0:
                            pe.wait_ge(z_ready, ATT[(L, HG - 1, T - 1)])
                        else:
                            pe.wait_ge(gu_out, turns * 2 + (2 * NG * L + t + 1))
                    for k in range(2):
                        ins = three(sc[:, t, :], xhi[:, 2 * b + k, t * P:(t + 1) * P],
                                    xlo[:, 2 * b + k, t * P:(t + 1) * P],
                                    whi[:, u % RING, 512 * k:512 * k + 512],
                                    wlo[:, u % RING, 512 * k:512 * k + 512], b == 0 and k == 0, b == 3 and k == 1)
                    if b == 3 and t == 0:
                        ins.then_inc(gu_done, 1)
                ins.then_inc(unit_done, 1)

            def proj_unit(L, s, half):
                u = UNITS * L + s
                ready(u)
                for t in range(T):
                    if half == 0:
                        pe.wait_ge(gu_out, 2 * NG * L + 2 * (NG - 1) + t + 1)
                    else:
                        pe.wait_ge(proj_out, 4 * L + t + 1)
                    for k in range(2):
                        ins = three(sc[:, t, :], phi[:, k, t * P:(t + 1) * P], plo[:, k, t * P:(t + 1) * P],
                                    whi[:, u % RING, 512 * k:512 * k + 512],
                                    wlo[:, u % RING, 512 * k:512 * k + 512], k == 0, k == 1)
                    if t == 0:
                        ins.then_inc(gu_done, 1)
                ins.then_inc(unit_done, 1)

            def turn(e, blocks, width=P):
                for n, src in enumerate(blocks):
                    rows, cols = src.shape[0], src.shape[1]
                    ins = pe.transpose(tb[e % 2][0:cols, n * rows:(n + 1) * rows], src, ident[0:rows, 0:rows])
                ins.then_inc(turned, 1)

            def turn_x(L, n, h_ready):
                for q in range(4):
                    hf, t = halves(q)
                    e = EV[("x", L, n, q)]
                    use(e)
                    h_ready(q)
                    turn(e, [h[:, t, (4 * hf + k) * P:(4 * hf + k + 1) * P] for k in range(4)])

            def attention(L, name, j):
                t = int(name[-1]) if name[-1] in "01" else 0
                B = j % 2
                if name == "turnqk":
                    for t in range(T):
                        e = EV[("qk", L, j, t)]
                        use(e)
                        if L == L_FX:
                            pe.wait_ge(qk_ready, 2 * j + t + 1)
                        else:
                            pe.wait_ge(bank_out[t], GROUPS * L + j + 1)
                        turn(e, [qkv[:, B, t, k * P:(k + 1) * P] for k in range(4)])
                elif name.startswith("scores"):
                    for tt in range(T):
                        wait_out(pe, EV[("qk", L, j, tt)])
                    n = ATT[(L, j, t)] - 1
                    if n:
                        pe.wait_ge(z_ready, n)
                    if L and j == 0 and t == 0:
                        pe.wait_ge(proj_out, 4 * L)
                    kk = keys(L, t)
                    for q in range(2):
                        for b in range(2):
                            ins = pe.matmul(sc[:, q, b * S:b * S + kk], qkT[64 * q:64 * q + 64, b, t * P:(t + 1) * P],
                                            qkT[64 * q:64 * q + 64, 2 + b, 0:kk], start=True, stop=True)
                    ins.then_inc(scores_done, 1)
                elif name.startswith("turnp"):
                    if L == L_DA:
                        pe.wait_ge(a_ready, 2 * j + t + 1)
                    else:
                        pe.wait_ge(e_ready, ATT[(L, j, t)])
                    blocks = p_blocks(L, t)
                    for n in range(len(blocks) // 4):
                        e = EV[("p", L, j, t, n)]
                        use(e)
                        turn(e, [z[:, t, q * 512 + b * 256 + k * P:q * 512 + b * 256 + (k + 1) * P]
                                 for q, b, k in blocks[4 * n:4 * n + 4]])
                elif name.startswith("pv"):
                    e = EV[("pv", L, j, t)]
                    use(e)
                    blocks = p_blocks(L, t)
                    for n in range(len(blocks) // 4):
                        wait_out(pe, EV[("p", L, j, t, n)])
                    nk = keys(L, t) // P
                    for kt in range(nk):
                        if L == L_FX:
                            pe.wait_ge(bank_out[kt], GROUPS * L + j + 1)
                        else:
                            pe.wait_ge(bank_out[2 + kt], GROUPS * L + j + 1)
                    for n, (q, b, k) in enumerate(blocks):
                        w = P if L == L_DA else 64
                        c = b * P + (0 if L == L_DA else 64 * q)
                        ins = pe.matmul(tb[e % 2][:, c:c + w], aT[:, t, n * P:(n + 1) * P],
                                        qkv[:, B, k, 512 + c:512 + c + w], start=(k == 0), stop=(k == nk - 1))
                    ins.then_inc(turned, 1)
                elif name == "turno":
                    e = EV[("o", L, j)]
                    use(e)
                    for t in range(T):
                        wait_out(pe, EV[("pv", L, j, t)])
                    turn(e, [o[:, t, k * P:(k + 1) * P] for k in range(2) for t in range(T)])

            def turn_g(L, g, wait, turns=0):
                for t in range(T):
                    e = EV[("g", L, g, t)]
                    use(e, turns)
                    pe.wait_ge(gu_out, turns * 2 + (wait + t + 1))
                    turn(e, [aT[:, 1, t * 256 + k * P:t * 256 + (k + 1) * P] for k in range(2)])

            def down_unit(L, s, b, g, first, last, turns=0):
                if b == 0:
                    for t in range(T):
                        e = EV[("g", L, g, t)]
                        pe.wait_ge(turn_out[e % 2], turns + (e // 2 + 1))
                wide_unit(L, s, b, ghi, glo, first, last, G_DOWN, [(0, 512), (512, 1024)], turns)

            pe.wait_ge(gains_in, 16 * 12)
            pe.wait_ge(consts, 2)
            pe.transpose(tb[0][:, 0:GAIN_ROWS], gain_rows[0:GAIN_ROWS, :], ident[0:GAIN_ROWS, 0:GAIN_ROWS])\
                .then_inc(gains_turned, 1)
            pe.wait_ge(gains_ready, 1)

            for L in range(LAYERS):
                def h_start(q):
                    if L == 0:
                        pe.wait_ge(x_in, 32)
                    elif L == 2:
                        pe.wait_ge(fin_ready, q + 1)
                    else:
                        pe.wait_ge(bank_out[q], GROUPS * L)
                for s in range(U_FFN):
                    if s == 0:
                        turn_x(L, 0, h_start)
                    if s == U_GU0:
                        turn_x(L, 1, lambda q: pe.wait_ge(bank_out[q], GROUPS * L + G_WO + 1))
                    if L == L_FX and s == 1:
                        e = EV[("flog", L)]
                        use(e)
                        pe.wait_ge(wf_ready, 1)
                        wait_out(pe, EV[("x", L, 0, 2)])
                        wait_out(pe, EV[("x", L, 0, 3)])
                        for t in range(T):
                            for kb in range(KB):
                                c = slice(t * P, (t + 1) * P)
                                ins = three(tb[e % 2][:, 16 * t:16 * t + 16], xhi[:, kb, c], xlo[:, kb, c],
                                            wfhi[:, kb, :], wflo[:, kb, :], kb == 0, kb == KB - 1)
                        ins.then_inc(turned, 1)
                    if L == L_FX and s == 3:
                        e = EV[("flogT", L)]
                        use(e)
                        pe.wait_ge(f_ready, 1)
                        turn(e, [f2[:, t, :] for t in range(T)])
                    if L == L_FX and s == 5:
                        e = EV[("fcum", L)]
                        use(e)
                        pe.wait_ge(nfc_ready, 1)
                        turn(e, [nfcT[:, t * P:(t + 1) * P] for t in range(T)])
                    for name, j in steps(s):
                        attention(L, name, j)
                    if s == U_GU0 + 2:
                        e = EV[("side", L)]
                        use(e)
                        pe.wait_ge(side_in, 16 * (L + 1))
                        turn(e, [side[:, t, k * P:(k + 1) * P] for k in range(2) for t in range(T)])
                    if s < U_WO:
                        kb = s % KB
                        if s in (0, 4):
                            for q in range(2):
                                wait_out(pe, EV[("x", L, 0, q + (2 if s else 0))])
                        segs = [(256, 768), (0, 256)] if L == L_FX else [(0, 512), (512, 768)]
                        wide_unit(L, s, kb, xhi, xlo, kb == 0, kb == KB - 1, s // KB, segs)
                    elif s < U_GU0:
                        kb = s - U_WO
                        wait_out(pe, EV[("o", L, kb // 2)])
                        wide_unit(L, s, kb, ohi, olo, kb == 0, kb == KB - 1, G_WO, [(0, 512), (512, 1024)])
                    else:
                        if s in (U_GU0, U_GU0 + 2):
                            for q in range(2):
                                wait_out(pe, EV[("x", L, 1, q + (2 if s > U_GU0 else 0))])
                        gu_unit(L, s, s - U_GU0)

                def ffn_body(i, first):
                    for b in range(4):
                        if b == 1:
                            turn_g(L, 0, 2 * NG * L, i)
                        gu_unit(L, U_FFN + b, b, i)
                    for b in range(2):
                        down_unit(L, U_FFN + 4 + b, b, 0, first and b == 0, False, i)

                ffn_body(0, True)
                with pe.Fori(1, NG - 1) as i:
                    ffn_body(i, False)
                turn_g(L, NG - 1, 2 * NG * L + 2 * (NG - 1))
                proj_unit(L, U_PROJ_A, 0)
                for b in range(2):
                    down_unit(L, U_DOWN_LAST + b, b, NG - 1, False, b == 1)
                proj_unit(L, U_PROJ_B, 1)
                turn_x(L, 2, lambda q: pe.wait_ge(bank_out[q], GROUPS * L + G_DOWN + 1))
                for kb in range(KB):
                    if kb in (0, 4):
                        for q in range(2):
                            wait_out(pe, EV[("x", L, 2, q + (2 if kb else 0))])
                    wide_unit(L, U_GATE + kb, kb, xhi, xlo, kb == 0, kb == KB - 1, G_GATE, [(0, 512), (512, 1024)])


_INS = ['x', 'p', 'norm_mix', 'norm_ffn', 'norm_ple', 'norm_final', 'da_w_qkv', 'da_w_o', 'da_lambda_q1',
        'da_lambda_k1', 'da_lambda_q2', 'da_lambda_k2', 'da_subln', 'na_w_qkv', 'na_b_qkv', 'na_rpb', 'na_w_o',
        'ffn_w_gate', 'ffn_w_up', 'ffn_w_down', 'ple_w_proj', 'ple_w_gate', 'p_2', 'attn_norm_g_2', 'sb_w_qkv_2',
        'sb_w_o_2', 'shared_norm_g_2', 'shared_w_kvf_2', 'shared_b_f_2', 'shared_k_norm_g_2', 'fox_w_q_2',
        'fox_q_norm_g_2', 'fox_w_o_2', 'ffn_norm_g_2', 'ffn_w_gu_2', 'ffn_w_d_2', 'ple_norm_g_2', 'ple_w_gate_2',
        'ple_w_proj_2']


def kernel(**inputs):
    import numpy as _np
    import concourse.bacc as _bacc
    from concourse import mybir as _mybir
    from concourse.bass_utils import run_bass_kernel_spmd as _run

    nc = _bacc.Bacc("TRN2", target_bir_lowering=False, num_devices=1)
    arrays, args = {}, {}
    for name in _INS:
        x = _np.ascontiguousarray(inputs[name])
        arrays[f"in_{name}"] = x
        args[name] = nc.dram_tensor(f"in_{name}", x.shape, _mybir.dt.from_np(x.dtype), kind="ExternalInput").ap()
    out = nc.dram_tensor("out", (1, S, D), _mybir.dt.float32, kind="ExternalOutput").ap()
    build(nc, args, out)
    r = _run(nc, [arrays], core_ids=[0])
    return r.results[0]["out"]
```

```python
from contextlib import ExitStack

import math

import concourse.bass as bass
from concourse import mybir

F32 = mybir.dt.float32
F32R = mybir.dt.float32r
BF16 = mybir.dt.bfloat16
ALU = mybir.AluOpType
ACT = mybir.ActivationFunctionType
AX_X = mybir.AxisListType.X

P = 128
S = 256
T = S // P
D = 1024
KB = D // P
F = 2816
GC_COLS = 256
NG = F // GC_COLS
PD = 256
HG = 4
L_DA, L_NA, L_SB, L_FX = range(4)
LAYERS = 4
SCALE = 0.125
LAM_INIT = 0.8 - 0.6 * math.exp(-0.3 * 0)
MASKED = -1e30
EPS = 1e-6
SUB_EPS = 1e-5

RING = 6
AHEAD = RING - 2
U_QKV = 0
QK_UNITS, V_UNITS = KB // 2, KB // 4
GROUP_UNITS = QK_UNITS + V_UNITS
U_WO = U_QKV + HG * GROUP_UNITS
U_GU0 = U_WO + KB
U_FFN = U_GU0 + 4
U_PROJ_A = U_FFN + 6 * (NG - 1)
U_DOWN_LAST = U_PROJ_A + 1
U_PROJ_B = U_DOWN_LAST + 2
U_GATE = U_PROJ_B + 1
UNITS = U_GATE + KB

G_WO, G_DOWN, G_GATE, GROUPS = 4, 5, 6, 7


def count(labels):
    return {x: n + 1 for n, x in enumerate(labels)}


PE_STEPS = {
    L_DA: [["evacqk"], ["turnqk"], ["scores0"], ["scores1"], [], ["turnp0"], ["pv0", "turnp1"], ["pv1"], ["turno"]],
    L_NA: [["evacqk"], ["turnqk"], ["scores0"], ["scores1"], ["turnp0"], ["pv0", "turnp1"], ["pv1"], ["turno"]],
    L_SB: [["evacqk"], ["turnqk"], ["scores0"], ["scores1"], [], ["turnp0"], ["pv0", "turnp1"], ["pv1"], ["turno"]],
    L_FX: [["evacqk"], [], ["turnqk"], ["scores0"], ["scores1"], ["turnp0"], ["pv0", "turnp1"], ["pv1"], ["turno"]],
}
ACT_STEPS = {
    L_DA: [["evacqk"], ["turnqk"], [], ["exp0"], ["exp1"], ["turnp0"], ["|", "pv0", "turnp1"], ["pv1"], ["turno"]],
    L_NA: [["evacqk"], ["turnqk"], [], ["exp0"], ["turnp0", "exp1"], ["|", "turnp1"], [], ["turno"]],
    L_SB: [["evacqk"], ["turnqk"], [], ["exp0"], ["exp1"], ["turnp0"], ["|", "pv0", "turnp1"], ["pv1"], ["turno"]],
    L_FX: [["evacqk"], [], ["turnqk"], [], ["exp0"], ["turnp0", "exp1"], ["|", "turnp1"], [], ["turno"]],
}
DVE_STEPS = {
    L_DA: [["|"], ["|"], ["evacv", "scores0"], ["scores1"], ["post0"], ["post1"], ["|", "turnp1", "pv0"], ["pv1"],
           ["turno"]],
    L_NA: [["evacqk"], ["|"], ["evacv", "scores0"], ["scores1"], ["turnp0", "post0"],
           ["pv0", "|", "turnp1", "post1"], ["pv1"], ["turno"]],
    L_SB: [["|"], ["|"], ["evacv", "scores0"], ["scores1"], ["post0"], ["post1", "turnp0"], ["|", "turnp1", "pv0"],
           ["pv1"], ["turno"]],
    L_FX: [["evacqk"], ["headnorm"], ["evacv"], ["scores0"], ["scores1"], ["turnp0", "post0"],
           ["pv0", "|", "turnp1", "post1"], ["pv1"], ["turno"]],
}


def steps(tables, L, s):
    found = []
    for j in range(HG):
        r = s - GROUP_UNITS * j - QK_UNITS
        if 0 <= r < len(tables[L]):
            found += [(name, j) for name in tables[L][r]]
    return found


def around_split(tables, L, s):
    before, after = [], []
    for j in range(HG):
        names = [x for x, g in steps(tables, L, s) if g == j]
        at = names.index("|") if "|" in names else len(names)
        before += [(x, j) for x in names[:at]]
        after += [(x, j) for x in names[at + 1:]]
    return before, after


def keys(L, t):
    return P if L >= L_SB and t == 0 else S


def p_blocks(L, t):
    n = keys(L, t) // P
    if L == L_DA:
        return [(0, b, k) for b in range(2) for k in range(n)]
    return [(q, b, k) for q in range(2) for b in range(2) for k in range(n)]


def turn_events():
    ev = []
    for L in range(LAYERS):
        for s in range(UNITS):
            if s == 0:
                ev += [("x", L, 0, q) for q in range(4)]
            if L == L_FX and s == 1:
                ev.append(("flog", L))
            if L == L_FX and s == 3:
                ev.append(("flogT", L))
            if L == L_FX and s == 4:
                ev.append(("fcum", L))
            for name, j in steps(PE_STEPS, L, s):
                if name == "turnqk":
                    ev += [("qk", L, j, t) for t in range(T)]
                elif name.startswith("turnp"):
                    t = int(name[-1])
                    ev += [("p", L, j, t, n) for n in range(len(p_blocks(L, t)) // 4)]
                elif name.startswith("pv"):
                    ev.append(("pv", L, j, int(name[-1])))
                elif name == "turno":
                    ev.append(("o", L, j))
            if s == U_GU0:
                ev += [("x", L, 1, q) for q in range(4)]
            if s == U_GU0 + 2:
                ev.append(("side", L))
            if U_FFN <= s < U_PROJ_A and (s - U_FFN) % 6 == 1:
                ev += [("g", L, (s - U_FFN) // 6, t) for t in range(T)]
            if s == U_PROJ_A:
                ev += [("g", L, NG - 1, t) for t in range(T)]
            if s == U_GATE:
                ev += [("x", L, 2, q) for q in range(4)]
    return ev


EV_LIST = turn_events()
EV = {x: n for n, x in enumerate(EV_LIST)}
SPLIT = count([x for x in EV_LIST if x[0] in ("x", "o", "g", "side")])
NORMS = [(L, n) for L in range(2) for n in range(3)] + [(1, 3)] + [(L, n) for L in range(2, 4) for n in range(3)]
NORM = count(NORMS)
ATT = count([(L, j, t) for L in range(LAYERS) for j in range(HG) for t in range(T)])
SOFT = count([(L, j, t) for L in (L_DA, L_NA, L_FX) for j in range(HG) for t in range(T)])

GAIN_MIX, GAIN_FFN, GAIN_PLE = [0, 8, 48, 56], [16, 24, 64, 72], [32, 40, 80, 88]
GAIN_SHARED, GAIN_SUB, GAIN_K, GAIN_Q, GAIN_ROWS = 96, 104, 105, 106, 107


def halves(q):
    return q // 2, q % 2


def unit_parts(L, s):
    if s < U_WO:
        b = s % GROUP_UNITS
        kv_gain = GAIN_SHARED if L == L_FX else GAIN_MIX[L]
        if b >= QK_UNITS:
            return [(256 * k, 256 * k + 256, kv_gain + 4 * (b - QK_UNITS) + k) for k in range(4)]
        if L == L_FX:
            return [(512 * k + 256 * x, 512 * k + 256 * x + 256, g + 2 * b + k)
                    for k in range(2) for x, g in enumerate((GAIN_MIX[L], GAIN_SHARED))]
        return [(512 * k, 512 * k + 512, GAIN_MIX[L] + 2 * b + k) for k in range(2)]
    if s < U_GU0:
        return [(0, 1024, GAIN_SUB if L == L_DA else None)]
    if s < U_PROJ_A:
        b = s - U_GU0 if s < U_FFN else (s - U_FFN) % 6
        if b < 4:
            return [(0, 512, GAIN_FFN[L] + 2 * b), (512, 1024, GAIN_FFN[L] + 2 * b + 1)]
        return [(0, 1024, None)]
    if s < U_GATE:
        return [(0, 1024, None)]
    return [(0, 1024, GAIN_PLE[L] + s - U_GATE)]


def build(nc, a, out):
    ctx = ExitStack()
    with ctx:
        def sb(name, shape, dt=F32):
            return ctx.enter_context(nc.sbuf_tensor(name, shape, dt))

        def ps(name, shape):
            return ctx.enter_context(nc.psum_tensor(name, shape, F32))

        def sem(name):
            return ctx.enter_context(nc.semaphore(name))

        raw = sb("raw", [P, RING, 1024])
        whi = sb("whi", [P, RING, 1024], F32R)
        wlo = sb("wlo", [P, RING, 1024], F32R)
        h = sb("h", [P, T, D])
        xhi = sb("xhi", [P, KB, S], F32R)
        xlo = sb("xlo", [P, KB, S], F32R)
        ohi = sb("ohi", [P, KB, S], F32R)
        olo = sb("olo", [P, KB, S], F32R)
        ghi = sb("ghi", [P, 2, S], F32R)
        glo = sb("glo", [P, 2, S], F32R)
        phi = sb("phi", [P, 2, S], F32R)
        plo = sb("plo", [P, 2, S], F32R)
        side = sb("side", [P, T, PD])
        qkv = sb("qkv", [P, 2, T, 768])
        qkT = sb("qkT", [P, 4, S])
        z = sb("z", [P, T, 1024])
        aT = sb("aT", [P, T, 1024])
        bias = sb("bias", [P, T, HG, 1024])
        o = sb("o", [P, T, 256])
        nab = sb("nab", [P, 2, 768])
        fin_gain = sb("fin_gain", [P, D])
        ident = sb("ident", [P, P])
        gain_rows = sb("gain_rows", [P, P])
        gain = sb("gain", [P, GAIN_ROWS])
        junk = sb("junk", [P, D], BF16)
        ss = sb("ss", [P, len(NORMS), T])
        rstd = sb("rstd", [P, len(NORMS), T])
        powm = sb("powm", [P, 16])
        mx = sb("mx", [P, T, 4])
        sums = sb("sums", [P, T, 4])
        rsum = sb("rsum", [P, T, 4])
        lamc = sb("lamc", [P, T, 2])
        ss_o = sb("ss_o", [P, T, 2])
        r_o = sb("r_o", [P, T, 2])
        ss_h = sb("ss_h", [P, T, 8])
        r_h = sb("r_h", [P, T, 8])
        lam_in = sb("lam_in", [P, 4, 64])
        lam = sb("lam", [P, 4])
        strict = sb("strict", [P, S])
        incl = sb("incl", [P, P])
        window = sb("window", [P, 64])
        wf = sb("wf", [P, KB, 16])
        wfg = sb("wfg", [P, KB, 16])
        wfhi = sb("wfhi", [P, KB, 16], F32R)
        wflo = sb("wflo", [P, KB, 16], F32R)
        bf = sb("bf", [P, 16])
        f = sb("f", [P, T, 16])
        f2 = sb("f2", [P, T, 16])
        fT, nfcT = o[0:16, 0, :], o[0:16, 1, :]
        ones_sb, zeros_sb = sb("ones_sb", [P, 1]), sb("zeros_sb", [P, 1])
        dist = nab[:, :, 0:S]
        nfc = sb("nfc", [P, T, 16])
        rpb_rows = nab[0:120, 0, S:S + 62].rearrange("p (i c) -> p i c", i=2)
        rpb_back = nab[0:120, 1, S:S + 62].rearrange("p (i c) -> p i c", i=2)
        rpb_dram = nc.dram_tensor("rpb_scratch", (120, 2, 31), F32, kind="Internal").ap()
        nfc_dram = nc.dram_tensor("nfc_scratch", (16, S), F32, kind="Internal").ap()

        acc = [ps(f"acc{b}", [P, 512]) for b in range(4)]
        sc = ps("sc", [P, 2, 512])
        tb = [ps(f"turn{b}", [P, 512]) for b in range(2)]

        weights_in = [sem(f"weights_in{i}") for i in range(RING)]
        hi_done, lo_done, unit_done = sem("hi_done"), sem("lo_done"), sem("unit_done")
        acc_done = sem("acc_done")
        bank_out = [sem(f"bank_out{b}") for b in range(4)]
        gu_done, gu_out = sem("gu_done"), sem("gu_out")
        sig_done, gmid = sem("sig_done"), sem("gmid")
        gated = sem("gated")
        proj_out, gate_sig = sem("proj_out"), sem("gate_sig")
        turned = sem("turned")
        turn_hi = sem("turn_hi")
        turn_out = [sem(f"turn_out{b}") for b in range(2)]
        x_in, gains_in, side_in, misc_in, nab_in = (sem("x_in"), sem("gains_in"), sem("side_in"), sem("misc_in"),
                                                    [sem(f"nab_in{i}") for i in range(2)])
        first_gains_in = sem("first_gains_in")
        gains_turned, gains_ready = sem("gains_turned"), sem("gains_ready")
        consts = sem("consts")
        ss_ready, rstd_ready, fin_ready = sem("ss_ready"), sem("rstd_ready"), sem("fin_ready")
        scores_done, z_ready, mx_ready, e_ready = (sem("scores_done"), sem("z_ready"), sem("mx_ready"),
                                                   sem("e_ready"))
        a_ready, sp_ready, arg_ready = sem("a_ready"), sem("sp_ready"), sem("arg_ready")
        so_ready, ro_ready = sem("so_ready"), sem("ro_ready")
        rpb_load, rpb_store = sem("rpb_load"), sem("rpb_store")
        bias_ready, rpb_in = sem("bias_ready"), sem("rpb_in")
        sq_ready, sh_ready, rh_ready, qk_ready = (sem("sq_ready"), sem("sh_ready"), sem("rh_ready"),
                                                  sem("qk_ready"))
        lam_dot, lam_exp = sem("lam_dot"), sem("lam_exp")
        wf_g, wf_hi, wf_ready = sem("wf_g"), sem("wf_hi"), sem("wf_ready")
        f_ready, f_sp, nfc_ready, nfc_store, nfc_load = (sem("f_ready"), sem("f_sp"), sem("nfc_ready"),
                                                         sem("nfc_store"), sem("nfc_load"))
        act_link, dve_link, pool_link = sem("act_link"), sem("dve_link"), sem("pool_link")
        out_ready, out_stored = sem("out_ready"), sem("out_stored")

        def acc_wait(eng, L, g, b, last):
            if g < HG:
                done, own = 2 * g + b // 2 + 1, b % 2 == 0
            else:
                done, own = 2 * HG + 3 * (g - HG) + b + 1, b < 3
            if own:
                eng.wait_ge(acc_done, (2 * HG + 3 * (GROUPS - HG)) * L + done)
            else:
                eng.wait_ge(unit_done, UNITS * L + last + 1)

        def wait_out(eng, e):
            eng.wait_ge(turn_out[e % 2], e // 2 + 1)

        def rs(L, n, t):
            i = NORM[(L, n)] - 1
            return rstd[:, i, t:t + 1]

        qkv_cols = [[(w, x * D) for x in range(3)] for w in (a["da_w_qkv"][0], a["na_w_qkv"][0], a["sb_w_qkv_2"][0])]
        qkv_cols.append([(a["fox_w_q_2"][0], 0), (a["shared_w_kvf_2"], 0), (a["shared_w_kvf_2"], D)])
        wo_w = [a["da_w_o"][0], a["na_w_o"][0], a["sb_w_o_2"][0], a["fox_w_o_2"][0]]

        def gate_up(L):
            if L < 2:
                return a["ffn_w_gate"][L], a["ffn_w_up"][L], 0
            return a["ffn_w_gu_2"][L - 2], a["ffn_w_gu_2"][L - 2], F

        down_w = [a["ffn_w_down"][0], a["ffn_w_down"][1], a["ffn_w_d_2"][0], a["ffn_w_d_2"][1]]
        proj_w = [a["ple_w_proj"][0], a["ple_w_proj"][1], a["ple_w_proj_2"][0], a["ple_w_proj_2"][1]]
        pgate_w = [a["ple_w_gate"][0], a["ple_w_gate"][1], a["ple_w_gate_2"][0], a["ple_w_gate_2"][1]]
        side_x = [a["p"][0, 0], a["p"][1, 0], a["p_2"][0, 0], a["p_2"][1, 0]]

        block = ctx.enter_context(nc.Block())

        @block.sync
        def _(sp):
            def load(u, parts, turns=0):
                if not isinstance(turns, int) or u >= RING:
                    sp.wait_ge(lo_done, turns * 6 + (u - RING + 1))
                for dst, src, n in parts:
                    sp.dma_start(dst, src).then_inc(weights_in[u % RING], 16 * n)

            def rows(w, kb, c0, c1):
                return w[kb * P:(kb + 1) * P, c0:c1]

            def gu_parts(L, u, b, c0):
                gate, up, at = gate_up(L)
                dst = raw[:, u % RING, :].rearrange("p (k s c) -> p s k c", k=2, s=2)
                parts = []
                for sx, (w, off) in enumerate(((gate, 0), (up, at))):
                    src = w[2 * b * P:(2 * b + 2) * P, bass.ds(c0 + off, GC_COLS)]
                    parts.append((dst[:, sx], src.rearrange("(k p) c -> p k c", p=P), 1))
                return parts

            for L in range(LAYERS):
                base = UNITS * L
                q_w, k_w, v_w = qkv_cols[L]
                for s in range(U_QKV, U_WO):
                    u, j, b = base + s, s // GROUP_UNITS, s % GROUP_UNITS
                    if b < QK_UNITS:
                        dst = raw[:, u % RING, :].rearrange("p (k s c) -> p s k c", k=2, s=2)
                        load(u, [(dst[:, x], w[2 * b * P:(2 * b + 2) * P, at + j * 256:at + j * 256 + 256]
                                  .rearrange("(k p) c -> p k c", p=P), 1) for x, (w, at) in enumerate((q_w, k_w))])
                    else:
                        w, at = v_w
                        v_rows = w[4 * (b - QK_UNITS) * P:4 * (b - QK_UNITS + 1) * P, at + j * 256:at + j * 256 + 256]
                        load(u, [(raw[:, u % RING, :].rearrange("p (k c) -> p k c", k=4),
                                  v_rows.rearrange("(k p) c -> p k c", p=P), 2)])
                for kb in range(KB):
                    u = base + U_WO + kb
                    load(u, [(raw[:, u % RING, :], rows(wo_w[L], kb, 0, D), 2)])
                for b in range(4):
                    u = base + U_GU0 + b
                    load(u, gu_parts(L, u, b, 0))
                with sp.Fori(0, NG - 1) as i:
                    for b in range(4):
                        u = base + U_FFN + b
                        load(u, gu_parts(L, u, b, i * GC_COLS + GC_COLS), i)
                    for b in range(2):
                        u = base + U_FFN + 4 + b
                        src = down_w[L].rearrange("(g k p) c -> g k p c", k=2, p=P)[bass.ds(i, 1), b]
                        load(u, [(raw[:, u % RING, :], src.rearrange("g p c -> p (g c)"), 2)], i)

                def proj_parts(u, half):
                    dst = raw[:, u % RING, :].rearrange("p (k c) -> p k c", k=2)
                    return [(dst, proj_w[L][:, half * 512:half * 512 + 512].rearrange("(k p) c -> p k c", p=P), 2)]

                u = base + U_PROJ_A
                load(u, proj_parts(u, 0))
                for b in range(2):
                    u = base + U_DOWN_LAST + b
                    load(u, [(raw[:, u % RING, :], rows(down_w[L], 2 * (NG - 1) + b, 0, D), 2)])
                u = base + U_PROJ_B
                load(u, proj_parts(u, 1))
                for kb in range(KB):
                    u = base + U_GATE + kb
                    load(u, [(raw[:, u % RING, :], rows(pgate_w[L], kb, 0, D), 2)])
            for q in range(4):
                hf, t = halves(q)
                sp.wait_ge(bank_out[q], GROUPS * LAYERS)
                sp.dma_start(out[0, t * P:(t + 1) * P, hf * 512:hf * 512 + 512],
                             h[:, t, hf * 512:hf * 512 + 512]).then_inc(out_stored, 16)
            sp.wait_ge(out_stored, 64)

        @block.gpsimd
        def _(pool):
            links = [0]

            def link(ins):
                links[0] += 1
                ins.then_inc(pool_link, 1)
                pool.wait_ge(pool_link, links[0])

            link(pool.memset(ident[:, :], 0.0))
            pool.affine_select(out=ident[:, :], in_=ident[:, :], compare_op=ALU.not_equal, fill=1.0, base=0,
                               pattern=[[-1, P]], channel_multiplier=1).then_inc(consts, 1)
            link(pool.memset(powm[:, :], -0.5))
            for t in range(T):
                link(pool.iota(dist[:, t, :], pattern=[[-1, S]], base=t * P, channel_multiplier=1,
                               allow_small_or_imprecise_dtypes=True))
                link(pool.tensor_scalar(o[:, t, :], dist[:, t, :], -1.0, 0.0, ALU.mult, ALU.max))
                link(pool.tensor_scalar(dist[:, t, :], dist[:, t, :], 0.0, 1.0, ALU.max, ALU.mult))
                link(pool.tensor_tensor(dist[:, t, :], dist[:, t, :], o[:, t, :], ALU.add))
            for j in range(HG):
                for blk in range(2):
                    slope = 2.0 ** -(2 * j + blk + 1)
                    for t in range(T):
                        for par in range(2):
                            at = par * 512 + blk * 256
                            last = pool.tensor_scalar(bias[:, t, j, at:at + S], dist[:, t, :], -slope, 1.0 / SCALE,
                                                      ALU.mult, ALU.mult)
                last.then_inc(bias_ready, 1)
            link(pool.memset(strict[:, :], 0.0))
            link(pool.affine_select(out=strict[:, P:S], in_=strict[:, P:S], compare_op=ALU.is_gt, fill=MASKED,
                                    base=0, pattern=[[-1, P]], channel_multiplier=1))
            link(pool.memset(incl[:, :], 0.0))
            link(pool.affine_select(out=incl[:, :], in_=incl[:, :], compare_op=ALU.is_ge, fill=MASKED,
                                    base=0, pattern=[[-1, P]], channel_multiplier=1))
            pool.dma_start(rpb_rows[:, :, :], a["na_rpb"].rearrange("l h (r i) c -> (l h r i) c", i=1)
                           .rearrange("(p i) c -> p i c", i=2)).then_inc(rpb_load, 16)
            pool.wait_ge(rpb_load, 16)
            link(pool.tensor_scalar(rpb_back[:, :, :], rpb_rows[:, :, ::-1], 1.0, 1.0 / SCALE, ALU.mult, ALU.mult))
            pool.dma_start(rpb_dram[:, :, :], rpb_back[:, :, :]).then_inc(rpb_store, 16)
            link(pool.memset(window[:, :], 0.0))
            for r in range(2):
                w = window[64 * r:64 * r + 64]
                link(pool.affine_select(out=w[:, 0:48], in_=w[:, 0:48], compare_op=ALU.is_ge, fill=MASKED,
                                        base=8, pattern=[[1, 48]], channel_multiplier=-1))
                link(pool.affine_select(out=w[:, 16:64], in_=w[:, 16:64], compare_op=ALU.is_gt, fill=MASKED,
                                        base=8 - 16, pattern=[[-1, 48]], channel_multiplier=1))

            def rms(dst, src, n, width, eps, ready):
                link(pool.tensor_scalar(dst, src, 1.0 / width, eps, ALU.mult, ALU.add))
                pool.tensor_tensor(dst, dst, powm[:, 0:n], ALU.pow).then_inc(ready, 1)

            def norm(L, n):
                i = NORM[(L, n)] - 1
                pool.wait_ge(ss_ready, 2 * (i + 1))
                rms(rstd[:, i, :], ss[:, i, :], 2, D, EPS, rstd_ready)

            def load_side(L):
                if L:
                    pool.wait_ge(turned, EV[("side", L - 1)] + 1)
                pool.dma_start(side[:, :, :], side_x[L].rearrange("(t p) c -> p t c", p=P)).then_inc(side_in, 16)

            def forget_bias(j):
                src = bias[:, 1, j, :].rearrange("p (x c) -> p x c", c=S)
                dst = bias[:, 0, j, :].rearrange("p (x c) -> p x c", c=S)
                m = incl[:, :].unsqueeze(1).to_broadcast([P, 4, P])
                pool.tensor_tensor(dst[:, :, 0:P], src[:, :, 0:P], m, ALU.add)
                pool.tensor_tensor(src[:, :, P:S], src[:, :, P:S], m, ALU.add).then_inc(bias_ready, 1)

            def load_nab(j):
                src = a["na_b_qkv"].rearrange("a (s c) -> a s c", s=3)[:, :, j * 256:j * 256 + 256]
                pool.dma_start(nab[:, j % 2, :].rearrange("p (s c) -> p s c", s=3),
                               src.to_broadcast([P, 3, 256])).then_inc(nab_in[j % 2], 16)

            for L in range(LAYERS):
                load_side(L)
                norm(L, 0)
                if L == L_FX:
                    pool.wait_ge(nfc_ready, 1)
                    pool.dma_start(nfc_dram[:, :], nfcT).then_inc(nfc_store, 16)
                    pool.wait_ge(nfc_store, 16)
                    pool.dma_start(bias[:, 1, :, :].rearrange("p j c -> p (j c)"),
                                   nfc_dram.rearrange("h (a c) -> a (h c)", a=1).to_broadcast([P, 16 * S]))\
                        .then_inc(nfc_load, 16)
                    pool.wait_ge(nfc_load, 16)
                    forget_bias(0)
                for s in range(U_GU0):
                    if L == L_NA and s < U_WO and s % GROUP_UNITS == 0:
                        j = s // GROUP_UNITS
                        if j >= 2:
                            pool.wait_ge(bank_out[3], GROUPS * L + j - 1)
                        load_nab(j)
                    for name, j in steps(PE_STEPS, L, s):
                        if L == L_FX and name == "evacqk":
                            for t in range(T):
                                pool.wait_ge(sh_ready, 2 * j + t + 1)
                                rms(r_h[:, t, :], ss_h[:, t, :], 8, 64, EPS, rh_ready)
                            if j + 1 < HG:
                                forget_bias(j + 1)
                        if L == L_DA and name.startswith("pv"):
                            t = int(name[-1])
                            pool.wait_ge(so_ready, 2 * j + t + 1)
                            rms(r_o[:, t, :], ss_o[:, t, :], 2, 128, SUB_EPS, ro_ready)
                norm(L, 1)
                if L == L_DA:
                    pool.wait_ge(rpb_store, 16)
                    pool.wait_ge(z_ready, ATT[(L_DA, HG - 1, T - 1)])
                    for t in range(T):
                        for r2 in range(2):
                            for j in range(HG):
                                for x in range(4):
                                    par, blk = x // 2, x % 2
                                    head = 4 * j + 2 * blk + par
                                    src = bass.AP(tensor=rpb_dram.tensor,
                                                  offset=(head * 15 + 7 - 2 * t - r2) * 31 + 15 - 63,
                                                  ap=[[1, 64], [31, 4], [1, 64]])
                                    dst = bias[64 * r2:64 * r2 + 64, t, j, x * 256:x * 256 + 256]
                                    pool.dma_start(dst.rearrange("p (r c) -> p r c", c=64), src)\
                                        .then_inc(rpb_in, 16)
                    pool.wait_ge(rpb_in, 16 * 64)
                    for t in range(T):
                        b = bias[:, t, :, :].rearrange("p j (r c) -> p (j r) c", c=64)
                        pool.tensor_tensor(b, b, window[:, ::-1].unsqueeze(1).to_broadcast([P, 64, 64]), ALU.add)\
                            .then_inc(bias_ready, 1)
                norm(L, 2)
                if L == 1:
                    norm(L, 3)

        @block.scalar
        def _(act):
            links = [0]

            def link(ins):
                links[0] += 1
                ins.then_inc(act_link, 1)
                act.wait_ge(act_link, links[0])

            for t in range(T):
                act.dma_start(h[:, t, :], a["x"][0, t * P:(t + 1) * P, :]).then_inc(x_in, 16)
            act.dma_start(gain_rows[0:16, :], a["norm_mix"].rearrange("l (k p) -> (l k) p", p=P))\
                .then_inc(first_gains_in, 16)
            vecs = [("norm_ffn", 16, 16), ("norm_ple", 32, 16), ("attn_norm_g_2", 48, 16),
                    ("ffn_norm_g_2", 64, 16), ("ple_norm_g_2", 80, 16)]
            for name, r, n in vecs:
                act.dma_start(gain_rows[r:r + n, :], a[name].rearrange("l (k p) -> (l k) p", p=P))\
                    .then_inc(gains_in, 16)
            act.dma_start(gain_rows[96:104, :], a["shared_norm_g_2"].rearrange("(k p) -> k p", p=P))\
                .then_inc(gains_in, 16)
            act.dma_start(gain_rows[104:105, :], a["da_subln"]).then_inc(gains_in, 16)
            for i in range(2):
                act.dma_start(gain_rows[105:106, 64 * i:64 * i + 64],
                              a["shared_k_norm_g_2"].rearrange("(a p) -> a p", a=1)).then_inc(gains_in, 16)
                act.dma_start(gain_rows[106:107, 64 * i:64 * i + 64], a["fox_q_norm_g_2"]).then_inc(gains_in, 16)
            for i, name in enumerate(("da_lambda_q1", "da_lambda_k1", "da_lambda_q2", "da_lambda_k2")):
                act.dma_start(lam_in[:, i, :], a[name].to_broadcast([P, 64])).then_inc(misc_in, 16)
            act.dma_start(fin_gain[:, :], a["norm_final"].rearrange("(a p) -> a p", a=1).to_broadcast([P, D]))\
                .then_inc(misc_in, 16)
            act.dma_start(wf[:, :, :], a["shared_w_kvf_2"][:, 2 * D:2 * D + 16].rearrange("(k p) c -> p k c", p=P))\
                .then_inc(misc_in, 16)
            act.dma_start(bf[:, :], a["shared_b_f_2"].rearrange("(a p) -> a p", a=1).to_broadcast([P, 16]))\
                .then_inc(misc_in, 16)

            def split(u, parts, turns=0):
                act.wait_ge(weights_in[u % RING], turns * 32 + 32 * (u // RING + 1))
                if not isinstance(turns, int) or u >= RING:
                    act.wait_ge(unit_done, turns * 6 + (u - RING + 1))
                for c0, c1, g in parts:
                    scale = 1.0 if g is None else gain[:, g:g + 1]
                    ins = act.activation(whi[:, u % RING, c0:c1], raw[:, u % RING, c0:c1], ACT.Copy, scale=scale)
                ins.then_inc(hi_done, 1)

            def split_ahead(L, s):
                u = UNITS * L + s + AHEAD
                if u < LAYERS * UNITS:
                    split(u, unit_parts(u // UNITS, u % UNITS))

            def norm(L, n):
                i = NORM[(L, n)] - 1
                for t in range(T):
                    if 2 * i + t:
                        act.wait_ge(ss_ready, 2 * i + t)
                    act.activation(junk[:, :], h[:, t, :], ACT.Square, accum_out=ss[:, i, t:t + 1])\
                        .then_inc(ss_ready, 1)

            def turn_x(L, n):
                for q in range(4):
                    hf, t = halves(q)
                    e = EV[("x", L, n, q)]
                    act.wait_ge(turned, e + 1)
                    act.activation(xhi[:, 4 * hf:4 * hf + 4, t * P:(t + 1) * P],
                                   tb[e % 2][:, :].rearrange("p (k c) -> p k c", k=4), ACT.Copy).then_inc(turn_hi, 1)
                norm(L, n)

            def attention(L, name, j):
                t = int(name[-1]) if name[-1] in "01" else 0
                B = j % 2
                kk = keys(L, t)
                zt = z[:, t, :].rearrange("p (x c) -> p x c", c=S)[:, :, 0:kk]
                if name == "evacqk":
                    if L == L_NA:
                        return
                    act.wait_ge(rstd_ready, NORM[(L, 0)])
                    for t in range(T):
                        acc_wait(act, L, j, t, GROUP_UNITS * j + QK_UNITS - 1)
                        act.activation(qkv[:, B, t, 0:512], acc[t][:, :], ACT.Copy, scale=rs(L, 0, t))\
                            .then_inc(bank_out[t], 1)
                    if L == L_FX:
                        for t in range(T):
                            act.wait_ge(bank_out[t], GROUPS * L + j + 1)
                            act.activation(nab[:, t, 0:512], qkv[:, B, t, 0:512], ACT.Square).then_inc(sq_ready, 1)
                elif name == "turnqk":
                    for t in range(T):
                        e = EV[("qk", L, j, t)]
                        act.wait_ge(turned, e + 1)
                        src = tb[e % 2][:, :].rearrange("p (k c) -> p k c", k=4)
                        dst = qkT[:, :, t * P:(t + 1) * P]
                        if L == L_FX:
                            act.activation(dst[:, 0:2], src[:, 0:2], ACT.Copy, scale=gain[:, GAIN_Q:GAIN_Q + 1])
                            ins = act.activation(dst[:, 2:4], src[:, 2:4], ACT.Copy,
                                                 scale=gain[:, GAIN_K:GAIN_K + 1])
                        else:
                            ins = act.activation(dst, src, ACT.Copy)
                        ins.then_inc(turn_out[e % 2], 1)
                elif name.startswith("exp"):
                    if L == L_SB:
                        act.wait_ge(z_ready, ATT[(L, j, t)])
                        tmp = aT[:, t, :].rearrange("p (x c) -> p x c", c=S)[:, :, 0:kk]
                        act.activation(tmp, zt, ACT.Sigmoid, scale=-1.0)
                        act.activation(zt, zt, ACT.Sigmoid).then_inc(sp_ready, 1)
                    else:
                        if L == L_FX:
                            act.wait_ge(mx_ready, 2 * j + t + 1)
                        else:
                            act.wait_ge(z_ready, ATT[(L, j, t)])
                        for x in range(4):
                            ins = act.activation(zt[:, x, :], zt[:, x, :], ACT.Exp, bias=mx[:, t, x:x + 1],
                                                 scale=-1.0, accum_out=sums[:, t, x:x + 1])
                        ins.then_inc(e_ready, 1)
                elif name.startswith("turnp"):
                    e = EV[("p", L, j, t, 0)]
                    act.wait_ge(turned, e + 1)
                    act.activation(aT[:, t, 0:512], tb[e % 2][:, :], ACT.Copy).then_inc(turn_out[e % 2], 1)
                elif name.startswith("pv"):
                    e = EV[("pv", L, j, t)]
                    if L == L_DA:
                        act.wait_ge(turned, e + 1)
                        for x in range(2):
                            ins = act.activation(aT[:, t, x * P:(x + 1) * P], tb[e % 2][:, x * P:(x + 1) * P], ACT.Square,
                                                 accum_out=ss_o[:, t, x:x + 1])
                        ins.then_inc(so_ready, 1)
                    if L == L_SB:
                        act.wait_ge(turned, e + 1)
                        act.activation(o[:, t, :], tb[e % 2][:, 0:256], ACT.Copy).then_inc(turn_out[e % 2], 1)
                elif name == "turno":
                    e = EV[("o", L, j)]
                    act.wait_ge(turned, e + 1)
                    act.activation(ohi[:, 2 * j:2 * j + 2, :], tb[e % 2][:, :].rearrange("p (k c) -> p k c", k=2),
                                   ACT.Copy).then_inc(turn_hi, 1)

            def hidden_sig(L, t, g):
                act.activation(aT[:, 0, t * 256:t * 256 + 256], sc[:, t, 0:256], ACT.Sigmoid, scale=rs(L, 1, t))\
                    .then_inc(sig_done, 1)

            act.wait_ge(gains_ready, 1)
            for u in range(AHEAD):
                split(u, unit_parts(0, u))
            for L in range(LAYERS):
                base = UNITS * L
                for s in range(U_FFN):
                    if s == 0:
                        turn_x(L, 0)
                    if s == U_GU0:
                        turn_x(L, 1)
                    before, after = around_split(ACT_STEPS, L, s)
                    for name, j in before:
                        attention(L, name, j)
                    split_ahead(L, s)
                    for name, j in after:
                        attention(L, name, j)
                    if L == L_DA and s == 0:
                        act.wait_ge(gains_ready, 2)
                    if L == L_DA and s == 2:
                        act.wait_ge(lam_dot, 2)
                        act.activation(lam[:, 2:4], lam[:, 0:2], ACT.Exp).then_inc(lam_exp, 1)
                    if L == L_SB and s == 2:
                        act.wait_ge(wf_g, 1)
                        act.activation(wfhi[:, :, :], wfg[:, :, :], ACT.Copy).then_inc(wf_hi, 1)
                    if L == L_FX and s == 2:
                        wait_out(act, EV[("flog", L)])
                        link(act.activation(f2[:, :, :], f[:, :, :], ACT.Abs))
                        link(act.activation(f2[:, :, :], f2[:, :, :], ACT.Exp, scale=-1.0))
                        act.activation(f2[:, :, :], f2[:, :, :], ACT.Ln, bias=1.0).then_inc(f_sp, 1)
                    if s == U_GU0 + 2:
                        e = EV[("side", L)]
                        act.wait_ge(turned, e + 1)
                        act.activation(phi[:, :, :], tb[e % 2][:, :].rearrange("p (k c) -> p k c", k=2), ACT.Copy)\
                            .then_inc(turn_hi, 1)

                g0 = 13 * L
                act.wait_ge(rstd_ready, NORM[(L, 1)])
                act.wait_ge(gu_done, g0 + 1)
                hidden_sig(L, 0, 0)
                act.wait_ge(unit_done, base + U_GU0 + 4)
                hidden_sig(L, 1, 0)

                def ffn_body(i, peeled):
                    for b in range(6):
                        if b == 1:
                            for t in range(T):
                                e = EV[("g", L, 0, t)]
                                act.wait_ge(turned, i * 2 + (e + 1))
                                act.activation(ghi[:, :, t * P:(t + 1) * P],
                                               tb[e % 2][:, 0:256].rearrange("p (k c) -> p k c", k=2),
                                               ACT.Copy).then_inc(turn_hi, 1)
                        if b == 4:
                            act.wait_ge(gu_done, i + (g0 + 2))
                            hidden_sig(L, 0, i)
                            act.wait_ge(unit_done, i * 6 + (base + U_FFN + 4))
                            hidden_sig(L, 1, i)
                        if peeled:
                            split_ahead(L, U_FFN + 6 * i + b)
                        else:
                            u = base + U_FFN + b + AHEAD
                            split(u, unit_parts(L, U_FFN + b + AHEAD), i)

                with act.Fori(0, NG - 2) as i:
                    ffn_body(i, False)
                ffn_body(NG - 2, True)

                for s in range(U_PROJ_A, UNITS):
                    if s == U_PROJ_A:
                        for t in range(T):
                            e = EV[("g", L, NG - 1, t)]
                            act.wait_ge(turned, e + 1)
                            act.activation(ghi[:, :, t * P:(t + 1) * P],
                                           tb[e % 2][:, 0:256].rearrange("p (k c) -> p k c", k=2),
                                           ACT.Copy).then_inc(turn_hi, 1)
                    if s in (U_DOWN_LAST, U_GATE):
                        hf = 0 if s == U_DOWN_LAST else 1
                        for t in range(T):
                            if t == 0:
                                act.wait_ge(gu_done, g0 + 12 + hf)
                            else:
                                act.wait_ge(unit_done, base + (U_PROJ_B if hf else U_PROJ_A) + 1)
                            act.activation(z[:, t, hf * 512:hf * 512 + 512], sc[:, t, :], ACT.Copy)\
                                .then_inc(proj_out, 1)
                    if s == U_GATE:
                        turn_x(L, 2)
                    split_ahead(L, s)
                act.wait_ge(rstd_ready, NORM[(L, 2)])
                for q in range(4):
                    hf, t = halves(q)
                    acc_wait(act, L, G_GATE, q, UNITS - 1)
                    act.activation(aT[:, t, hf * 512:hf * 512 + 512], acc[q][:, :], ACT.Sigmoid,
                                   scale=rs(L, 2, t)).then_inc(gate_sig, 1)
                if L == 1:
                    for q in range(4):
                        act.wait_ge(bank_out[q], GROUPS * L + G_GATE + 1)
                    norm(L, 3)

        @block.vector
        def _(dve):
            links = [0]

            def link(ins):
                links[0] += 1
                ins.then_inc(dve_link, 1)
                dve.wait_ge(dve_link, links[0])

            def split(u, parts, turns=0):
                dve.wait_ge(hi_done, turns * 6 + (u + 1))
                for c0, c1, g in parts:
                    w, hi, lo = (x[:, u % RING, c0:c1] for x in (raw, whi, wlo))
                    if g is None:
                        ins = dve.tensor_tensor(lo, w, hi.bitcast(F32), ALU.subtract)
                    else:
                        ins = dve.scalar_tensor_tensor(out=lo, in0=w, scalar=gain[:, g:g + 1],
                                                       in1=hi.bitcast(F32), op0=ALU.mult, op1=ALU.subtract)
                ins.then_inc(lo_done, 1)

            def split_ahead(L, s):
                u = UNITS * L + s + AHEAD
                if u < LAYERS * UNITS:
                    split(u, unit_parts(u // UNITS, u % UNITS))

            def lo_half(label, lo, hi, src, e, turns=0, per=0):
                dve.wait_ge(turn_hi, turns * per + SPLIT[label])
                dve.tensor_tensor(lo, src, hi.bitcast(F32), ALU.subtract).then_inc(turn_out[e % 2], 1)

            def turn_x(L, n):
                for q in range(4):
                    hf, t = halves(q)
                    e = EV[("x", L, n, q)]
                    at = (slice(None), slice(4 * hf, 4 * hf + 4), slice(t * P, (t + 1) * P))
                    lo_half(("x", L, n, q), xlo[at], xhi[at],
                            tb[e % 2][:, :].rearrange("p (k c) -> p k c", k=4), e)

            def add_to_h(L, g, last):
                for q in range(4):
                    hf, t = halves(q)
                    acc_wait(dve, L, g, q, last)
                    hq = h[:, t, hf * 512:hf * 512 + 512]
                    dve.tensor_tensor(hq, acc[q][:, :], hq, ALU.add).then_inc(bank_out[q], 1)

            def scores(L, j, t):
                kk = keys(L, t)
                zt = z[:, t, :].rearrange("p (x c) -> p x c", c=S)[:, :, 0:kk]
                src = sc[:, :, :].rearrange("p q (b c) -> p (q b) c", c=S)[:, :, 0:kk]
                if L == L_DA:
                    dve.wait_ge(bias_ready, j + 1)
                elif L in (L_NA, L_SB):
                    dve.wait_ge(bias_ready, HG + T)
                elif L == L_FX:
                    dve.wait_ge(bias_ready, HG + T + j + 1)
                dve.wait_ge(scores_done, ATT[(L, j, t)])
                if L == L_SB:
                    m = strict[:, S - kk:S] if t == 0 else strict[:, :]
                    dve.scalar_tensor_tensor(out=zt, in0=src, scalar=SCALE, in1=m.unsqueeze(1).to_broadcast([P, 4, kk]),
                                             op0=ALU.mult, op1=ALU.add).then_inc(z_ready, 1)
                    return
                for x in range(4):
                    add, to, prod = bias[:, t, j, x * S:x * S + kk], zt[:, x, :], src[:, x, :]
                    if L == L_NA:
                        add, to, prod = (y.rearrange("p (r c) -> p r c", c=64) for y in (add, to, prod))
                        add = add[:, :, ::-1]
                    ins = dve.tensor_tensor_reduce(out=to, in0=prod, in1=add, scale=-SCALE, scalar=3e38, op0=ALU.add,
                                                   op1=ALU.min, accum_out=mx[:, t, x:x + 1])
                ins.then_inc(z_ready, 1)
                if L == L_FX:
                    dve.wait_ge(z_ready, ATT[(L, j, t)])
                    fq = nfc[:, t, 4 * j:4 * j + 4]
                    link(dve.tensor_tensor(mx[:, t, :], mx[:, t, :], fq, ALU.add))
                    dve.tensor_tensor(mx[:, t, :], mx[:, t, :], fq, ALU.subtract).then_inc(mx_ready, 1)

            def after_exp(L, j, t):
                kk = keys(L, t)
                if L == L_SB:
                    zt = z[:, t, :].rearrange("p (x c) -> p x c", c=S)[:, :, 0:kk]
                    tmp = aT[:, t, :].rearrange("p (x c) -> p x c", c=S)[:, :, 0:kk]
                    dve.wait_ge(sp_ready, 2 * j + t + 1)
                    for x in range(4):
                        back = tmp[:, x, ::-1]
                        ins = dve.tensor_tensor_scan(back, back, zeros_sb[:, 0:1].to_broadcast([P, kk]), 1.0,
                                                     ALU.mult, ALU.add)
                    link(ins)
                    dve.tensor_tensor(zt[:, :, 0:kk - 1], zt[:, :, 0:kk - 1], tmp[:, :, 1:kk], ALU.mult)\
                        .then_inc(arg_ready, 1)
                    return
                dve.wait_ge(e_ready, SOFT[(L, j, t)])
                link(dve.reciprocal(rsum[:, t, :], sums[:, t, :]))
                if L == L_DA:
                    link(dve.tensor_scalar(lamc[:, t, :], rsum[:, t, 2:4], lam[:, 1:2], None, ALU.mult))
                    for b in range(2):
                        e0, e1 = (z[:, t, q * 512 + b * 256:q * 512 + b * 256 + 256] for q in range(2))
                        link(dve.tensor_scalar(e1, e1, lamc[:, t, b:b + 1], None, ALU.mult))
                        ins = dve.scalar_tensor_tensor(out=e0, in0=e0, scalar=rsum[:, t, b:b + 1], in1=e1,
                                                       op0=ALU.mult, op1=ALU.add)
                    ins.then_inc(a_ready, 1)

            def attention(L, name, j):
                t = int(name[-1]) if name[-1] in "01" else 0
                B = j % 2
                if name in ("evacqk", "evacv"):
                    dve.wait_ge(rstd_ready, NORM[(L, 0)])
                    half, c0, c1 = (0, 0, 512) if name == "evacqk" else (1, 512, 768)
                    if L == L_NA:
                        dve.wait_ge(nab_in[B], 16 * (j // 2 + 1))
                        for t in range(T):
                            b = 2 * half + t
                            acc_wait(dve, L, j, b, GROUP_UNITS * j + (GROUP_UNITS if half else QK_UNITS) - 1)
                            dve.scalar_tensor_tensor(out=qkv[:, B, t, c0:c1], in0=acc[b][:, 0:c1 - c0],
                                                     scalar=rs(L, 0, t), in1=nab[:, B, c0:c1], op0=ALU.mult,
                                                     op1=ALU.add).then_inc(bank_out[b], 1)
                    elif half:
                        for t in range(T):
                            acc_wait(dve, L, j, 2 + t, GROUP_UNITS * (j + 1) - 1)
                            dve.tensor_scalar(qkv[:, B, t, c0:c1], acc[2 + t][:, 0:256], rs(L, 0, t), None,
                                              ALU.mult).then_inc(bank_out[2 + t], 1)
                    if L == L_FX and not half:
                        for t in range(T):
                            dve.wait_ge(sq_ready, 2 * j + t + 1)
                            dve.tensor_reduce(ss_h[:, t, :], nab[:, t, 0:512].rearrange("p (x c) -> p x c", c=64),
                                              AX_X, ALU.add).then_inc(sh_ready, 1)
                elif name == "headnorm":
                        for t in range(T):
                            dve.wait_ge(rh_ready, 2 * j + t + 1)
                            x = qkv[:, B, t, 0:512].rearrange("p (x c) -> p x c", c=64)
                            dve.tensor_tensor(x, x, r_h[:, t, :].unsqueeze(2).to_broadcast([P, 8, 64]), ALU.mult)\
                                .then_inc(qk_ready, 1)
                elif name == "scores0":
                    scores(L, j, 0)
                elif name == "scores1":
                    scores(L, j, 1)
                elif name.startswith("post"):
                    after_exp(L, j, t)
                elif name.startswith("turnp"):
                    if ("p", L, j, t, 1) in EV:
                        e = EV[("p", L, j, t, 1)]
                        dve.wait_ge(turned, e + 1)
                        dve.tensor_copy(aT[:, t, 512:1024], tb[e % 2][:, :]).then_inc(turn_out[e % 2], 1)
                elif name.startswith("pv"):
                    e = EV[("pv", L, j, t)]
                    src = tb[e % 2]
                    if L == L_DA:
                        dve.wait_ge(ro_ready, 2 * j + t + 1)
                        dve.tensor_tensor(o[:, t, :].rearrange("p (x c) -> p x c", x=2),
                                          src[:, 0:256].rearrange("p (x c) -> p x c", x=2),
                                          r_o[:, t, :].unsqueeze(2).to_broadcast([P, 2, P]), ALU.mult)\
                            .then_inc(turn_out[e % 2], 1)
                    elif L != L_SB:
                        dve.wait_ge(turned, e + 1)
                        r = rsum[:, t, :].rearrange("p (q b) -> p b q", q=2)
                        dve.tensor_tensor(o[:, t, :].rearrange("p (b q c) -> p b q c", b=2, q=2),
                                          src[:, 0:256].rearrange("p (b q c) -> p b q c", b=2, q=2),
                                          r.unsqueeze(3).to_broadcast([P, 2, 2, 64]), ALU.mult)\
                            .then_inc(turn_out[e % 2], 1)
                elif name == "turno":
                    e = EV[("o", L, j)]
                    at = (slice(None), slice(2 * j, 2 * j + 2))
                    lo_half(("o", L, j), olo[at], ohi[at], tb[e % 2][:, :].rearrange("p (k c) -> p k c", k=2), e)

            def hidden(L, wait_base, turns=0, per=0):
                for t in range(T):
                    sg = aT[:, 0, t * 256:t * 256 + 256]
                    dve.wait_ge(sig_done, turns * per + (wait_base + t + 1))
                    dve.scalar_tensor_tensor(out=sg, in0=sc[:, t, 256:512], scalar=rs(L, 1, t), in1=sg,
                                             op0=ALU.mult, op1=ALU.mult).then_inc(gmid, 1)
                for t in range(T):
                    sg = aT[:, 0, t * 256:t * 256 + 256]
                    dve.wait_ge(gmid, turns * per + (wait_base + t + 1))
                    dve.scalar_tensor_tensor(out=aT[:, 1, t * 256:t * 256 + 256], in0=sc[:, t, 0:256],
                                             scalar=rs(L, 1, t), in1=sg, op0=ALU.mult, op1=ALU.mult)\
                        .then_inc(gu_out, 1)

            link(dve.memset(zeros_sb[:, :], 0.0))
            dve.memset(ones_sb[:, :], 1.0).then_inc(consts, 1)
            dve.wait_ge(gains_turned, 1)
            dve.tensor_copy(gain[:, 0:16], tb[0][:, 0:16]).then_inc(gains_ready, 1)
            dve.wait_ge(gains_ready, 1)
            split(0, unit_parts(0, 0))
            dve.wait_ge(gains_turned, 2)
            link(dve.tensor_copy(gain[:, 16:GAIN_ROWS], tb[1][:, 16:GAIN_ROWS]))
            dve.tensor_scalar(gain[:, GAIN_SUB:GAIN_SUB + 1], gain[:, GAIN_SUB:GAIN_SUB + 1], 1.0 - LAM_INIT, None,
                              ALU.mult).then_inc(gains_ready, 1)
            dve.wait_ge(gains_ready, 2)
            for u in range(1, AHEAD):
                split(u, unit_parts(0, u))
            for L in range(LAYERS):
                base = UNITS * L
                for s in range(U_FFN):
                    if s == 0:
                        turn_x(L, 0)
                    if s == U_GU0:
                        add_to_h(L, G_WO, U_GU0 - 1)
                        turn_x(L, 1)
                    before, after = around_split(DVE_STEPS, L, s)
                    for name, j in before:
                        attention(L, name, j)
                    split_ahead(L, s)
                    for name, j in after:
                        attention(L, name, j)
                    if L == L_DA and s == 1:
                        dve.wait_ge(misc_in, 16 * 7)
                        for i in range(2):
                            dve.tensor_tensor_reduce(out=lam_in[:, 2 * i, :], in0=lam_in[:, 2 * i, :],
                                                     in1=lam_in[:, 2 * i + 1, :], scale=1.0, scalar=0.0,
                                                     op0=ALU.mult, op1=ALU.add, accum_out=lam[:, i:i + 1])\
                                .then_inc(lam_dot, 1)
                    if L == L_DA and s == 3:
                        dve.wait_ge(lam_exp, 1)
                        link(dve.tensor_tensor(lam[:, 0:1], lam[:, 3:4], lam[:, 2:3], ALU.subtract))
                        link(dve.tensor_scalar(lam[:, 1:2], lam[:, 0:1], -LAM_INIT, None, ALU.add))
                    if L == L_SB and s == 1:
                        dst = wfg[:, :, :].rearrange("p k (j q b) -> p q (k j) b", q=2, b=2)
                        src = wf[:, :, :].rearrange("p k (j b q) -> p q (k j) b", q=2, b=2)
                        for kb in range(KB):
                            for q in range(2):
                                gg = gain[:, GAIN_SHARED + kb:GAIN_SHARED + kb + 1]
                                ins = dve.tensor_scalar(dst[:, q, 4 * kb:4 * kb + 4], src[:, q, 4 * kb:4 * kb + 4],
                                                        gg, None, ALU.mult)
                        ins.then_inc(wf_g, 1)
                    if L == L_SB and s == 3:
                        dve.wait_ge(wf_hi, 1)
                        dve.tensor_tensor(wflo[:, :, :], wfg[:, :, :], wfhi[:, :, :].bitcast(F32), ALU.subtract)\
                            .then_inc(wf_ready, 1)
                    if L == L_FX and s == 1:
                        e = EV[("flog", L)]
                        dve.wait_ge(rstd_ready, NORM[(L, 0)])
                        dve.wait_ge(turned, e + 1)
                        bp = bf[:, :].rearrange("p (j b q) -> p q j b", q=2, b=2)
                        for t in range(T):
                            for q in range(2):
                                fd = f[:, t, :].rearrange("p (j q b) -> p q j b", q=2, b=2)[:, q]
                                fs = tb[e % 2][:, 16 * t:16 * t + 16].rearrange("p (j q b) -> p q j b", q=2, b=2)[:, q]
                                ins = dve.scalar_tensor_tensor(out=fd, in0=fs, scalar=rs(L, 0, t), in1=bp[:, q],
                                                               op0=ALU.mult, op1=ALU.add)
                        ins.then_inc(turn_out[e % 2], 1)
                    if L == L_FX and s == 2:
                        dve.wait_ge(f_sp, 1)
                        link(dve.tensor_scalar(f[:, :, :], f[:, :, :], 0.0, 1.0 / SCALE, ALU.min, ALU.mult))
                        dve.scalar_tensor_tensor(out=f2[:, :, :], in0=f2[:, :, :], scalar=1.0 / SCALE,
                                                 in1=f[:, :, :], op0=ALU.mult, op1=ALU.subtract).then_inc(f_ready, 1)
                    if L == L_FX and s == 3:
                        e = EV[("flogT", L)]
                        dve.wait_ge(turned, e + 1)
                        dve.tensor_copy(fT, tb[e % 2][0:16, 0:S]).then_inc(turn_out[e % 2], 1)
                        wait_out(dve, e)
                        dve.wait_ge(consts, 2)
                        dve.tensor_tensor_scan(nfcT, ones_sb[0:16, 0:1].to_broadcast([16, S]), fT, 0.0, ALU.mult, ALU.add)\
                            .then_inc(nfc_ready, 1)
                    if L == L_FX and s == 4:
                        e = EV[("fcum", L)]
                        dve.wait_ge(turned, e + 1)
                        ins = dve.tensor_scalar(nfc[:, :, :], tb[e % 2][:, 0:32].rearrange("p (t c) -> p t c", t=T),
                                                SCALE, None, ALU.mult)
                        ins.then_inc(turn_out[e % 2], 1)
                        wait_out(dve, e)
                    if s == U_GU0 + 2:
                        e = EV[("side", L)]
                        lo_half(("side", L), plo[:, :, :], phi[:, :, :],
                                tb[e % 2][:, :].rearrange("p (k c) -> p k c", k=2), e)

                dve.wait_ge(rstd_ready, NORM[(L, 1)])
                hidden(L, 2 * NG * L)

                def ffn_body(i, peeled):
                    for b in range(6):
                        if b == 1:
                            for t in range(T):
                                e = EV[("g", L, 0, t)]
                                at = (slice(None), slice(None), slice(t * P, (t + 1) * P))
                                lo_half(("g", L, 0, t), glo[at], ghi[at],
                                        tb[e % 2][:, 0:256].rearrange("p (k c) -> p k c", k=2), e, i, 2)
                        if b == 4:
                            hidden(L, 2 * NG * L + 2, i, 2)
                        if peeled:
                            split_ahead(L, U_FFN + 6 * i + b)
                        else:
                            split(base + U_FFN + b + AHEAD, unit_parts(L, U_FFN + b + AHEAD), i)

                with dve.Fori(0, NG - 2) as i:
                    ffn_body(i, False)
                ffn_body(NG - 2, True)

                for s in range(U_PROJ_A, UNITS):
                    if s == U_PROJ_A:
                        for t in range(T):
                            e = EV[("g", L, NG - 1, t)]
                            at = (slice(None), slice(None), slice(t * P, (t + 1) * P))
                            lo_half(("g", L, NG - 1, t), glo[at], ghi[at],
                                    tb[e % 2][:, 0:256].rearrange("p (k c) -> p k c", k=2), e)
                    if s == U_PROJ_B:
                        add_to_h(L, G_DOWN, U_PROJ_B - 1)
                    if s == U_GATE:
                        turn_x(L, 2)
                    split_ahead(L, s)
                for q in range(5):
                    if q < 4:
                        hf, t = halves(q)
                        c = slice(hf * 512, hf * 512 + 512)
                        dve.wait_ge(gate_sig, 4 * L + q + 1)
                        dve.wait_ge(proj_out, 4 * L + q + 1)
                        dve.tensor_tensor(aT[:, t, c], aT[:, t, c], z[:, t, c], ALU.mult).then_inc(gated, 1)
                    if q:
                        hf, t = halves(q - 1)
                        c = slice(hf * 512, hf * 512 + 512)
                        dve.wait_ge(gated, 4 * L + q)
                        dve.tensor_tensor(h[:, t, c], h[:, t, c], aT[:, t, c], ALU.add).then_inc(bank_out[q - 1], 1)
                if L == 1:
                    dve.wait_ge(rstd_ready, NORM[(1, 3)])
                    dve.wait_ge(misc_in, 16 * 7)
                    for q in range(4):
                        hf, t = halves(q)
                        c = slice(hf * 512, hf * 512 + 512)
                        dve.scalar_tensor_tensor(out=h[:, t, c], in0=h[:, t, c], scalar=rs(1, 3, t),
                                                 in1=fin_gain[:, c], op0=ALU.mult, op1=ALU.mult)\
                            .then_inc(fin_ready, 1)

        @block.tensor
        def _(pe):
            def use(e, turns=0):
                if e >= 2:
                    pe.wait_ge(turn_out[e % 2], turns + e // 2)

            def ready(u, turns=0):
                pe.wait_ge(lo_done, turns * 6 + (u + 1))

            def three(dst, xh, xl, wh, wl, first, last):
                pe.matmul(dst, xh, wh, start=first, stop=False)
                pe.matmul(dst, xh, wl, start=False, stop=False)
                return pe.matmul(dst, xl, wh, start=False, stop=last)

            def wide_unit(L, s, kb, xh, xl, first, last, g, segs, turns=0, tiles=None):
                u = UNITS * L + s
                ready(u, turns)
                for b in range(4):
                    seg, t = b // 2, b % 2
                    if first and GROUPS * L + g:
                        pe.wait_ge(bank_out[b], GROUPS * L + g)
                    c0, c1 = segs[seg]
                    ins = three(acc[b][:, 0:c1 - c0], xh[:, kb, t * P:(t + 1) * P], xl[:, kb, t * P:(t + 1) * P],
                                whi[:, u % RING, c0:c1], wlo[:, u % RING, c0:c1], first, last)
                    if last and b < 3:
                        ins.then_inc(acc_done, 1)
                ins.then_inc(unit_done, 1)

            def qkv_unit(L, s):
                u, j, b = UNITS * L + s, s // GROUP_UNITS, s % GROUP_UNITS
                ready(u)
                first, last = b in (0, QK_UNITS), b in (QK_UNITS - 1, GROUP_UNITS - 1)
                half, at, blocks = (0, 2 * b, 2) if b < QK_UNITS else (1, 4 * (b - QK_UNITS), 4)
                w = 1024 // blocks
                for t in range(T):
                    bank = 2 * half + t
                    if first and GROUPS * L + j:
                        pe.wait_ge(bank_out[bank], GROUPS * L + j)
                    for k in range(blocks):
                        ins = three(acc[bank][:, 0:w], xhi[:, at + k, t * P:(t + 1) * P],
                                    xlo[:, at + k, t * P:(t + 1) * P], whi[:, u % RING, w * k:w * k + w],
                                    wlo[:, u % RING, w * k:w * k + w], first and k == 0, last and k == blocks - 1)
                    if last and t == 0:
                        ins.then_inc(acc_done, 1)
                ins.then_inc(unit_done, 1)

            def gu_unit(L, s, b, turns=0):
                u = UNITS * L + s
                ready(u, turns)
                for t in range(T):
                    if b == 0:
                        if s == U_GU0:
                            pe.wait_ge(z_ready, ATT[(L, HG - 1, T - 1)])
                        else:
                            pe.wait_ge(gu_out, turns * 2 + (2 * NG * L + t + 1))
                    for k in range(2):
                        ins = three(sc[:, t, :], xhi[:, 2 * b + k, t * P:(t + 1) * P],
                                    xlo[:, 2 * b + k, t * P:(t + 1) * P],
                                    whi[:, u % RING, 512 * k:512 * k + 512],
                                    wlo[:, u % RING, 512 * k:512 * k + 512], b == 0 and k == 0, b == 3 and k == 1)
                    if b == 3 and t == 0:
                        ins.then_inc(gu_done, 1)
                ins.then_inc(unit_done, 1)

            def proj_unit(L, s, half):
                u = UNITS * L + s
                ready(u)
                for t in range(T):
                    if half == 0:
                        pe.wait_ge(gu_out, 2 * NG * L + 2 * (NG - 1) + t + 1)
                    else:
                        pe.wait_ge(proj_out, 4 * L + t + 1)
                    for k in range(2):
                        ins = three(sc[:, t, :], phi[:, k, t * P:(t + 1) * P], plo[:, k, t * P:(t + 1) * P],
                                    whi[:, u % RING, 512 * k:512 * k + 512],
                                    wlo[:, u % RING, 512 * k:512 * k + 512], k == 0, k == 1)
                    if t == 0:
                        ins.then_inc(gu_done, 1)
                ins.then_inc(unit_done, 1)

            def turn(e, blocks, width=P):
                for n, src in enumerate(blocks):
                    rows, cols = src.shape[0], src.shape[1]
                    ins = pe.transpose(tb[e % 2][0:cols, n * rows:(n + 1) * rows], src, ident[0:rows, 0:rows])
                ins.then_inc(turned, 1)

            def turn_x(L, n, h_ready):
                for q in range(4):
                    hf, t = halves(q)
                    e = EV[("x", L, n, q)]
                    use(e)
                    h_ready(q)
                    turn(e, [h[:, t, (4 * hf + k) * P:(4 * hf + k + 1) * P] for k in range(4)])

            def attention(L, name, j):
                t = int(name[-1]) if name[-1] in "01" else 0
                B = j % 2
                if name == "turnqk":
                    for t in range(T):
                        e = EV[("qk", L, j, t)]
                        use(e)
                        if L == L_FX:
                            pe.wait_ge(qk_ready, 2 * j + t + 1)
                        else:
                            pe.wait_ge(bank_out[t], GROUPS * L + j + 1)
                        turn(e, [qkv[:, B, t, k * P:(k + 1) * P] for k in range(4)])
                elif name.startswith("scores"):
                    for tt in range(T):
                        wait_out(pe, EV[("qk", L, j, tt)])
                    n = ATT[(L, j, t)] - 1
                    if n:
                        pe.wait_ge(z_ready, n)
                    if L and j == 0 and t == 0:
                        pe.wait_ge(proj_out, 4 * L)
                    kk = keys(L, t)
                    for q in range(2):
                        for b in range(2):
                            ins = pe.matmul(sc[:, q, b * S:b * S + kk], qkT[64 * q:64 * q + 64, b, t * P:(t + 1) * P],
                                            qkT[64 * q:64 * q + 64, 2 + b, 0:kk], start=True, stop=True)
                    ins.then_inc(scores_done, 1)
                elif name.startswith("turnp"):
                    if L == L_DA:
                        pe.wait_ge(a_ready, 2 * j + t + 1)
                    elif L == L_SB:
                        pe.wait_ge(arg_ready, 2 * j + t + 1)
                    else:
                        pe.wait_ge(e_ready, SOFT[(L, j, t)])
                    blocks = p_blocks(L, t)
                    for n in range(len(blocks) // 4):
                        e = EV[("p", L, j, t, n)]
                        use(e)
                        turn(e, [z[:, t, q * 512 + b * 256 + k * P:q * 512 + b * 256 + (k + 1) * P]
                                 for q, b, k in blocks[4 * n:4 * n + 4]])
                elif name.startswith("pv"):
                    e = EV[("pv", L, j, t)]
                    use(e)
                    blocks = p_blocks(L, t)
                    for n in range(len(blocks) // 4):
                        wait_out(pe, EV[("p", L, j, t, n)])
                    nk = keys(L, t) // P
                    for kt in range(nk):
                        pe.wait_ge(bank_out[2 + kt], GROUPS * L + j + 1)
                    for n, (q, b, k) in enumerate(blocks):
                        w = P if L == L_DA else 64
                        c = b * P + (0 if L == L_DA else 64 * q)
                        ins = pe.matmul(tb[e % 2][:, c:c + w], aT[:, t, n * P:(n + 1) * P],
                                        qkv[:, B, k, 512 + c:512 + c + w], start=(k == 0), stop=(k == nk - 1))
                    ins.then_inc(turned, 1)
                elif name == "turno":
                    e = EV[("o", L, j)]
                    use(e)
                    for t in range(T):
                        wait_out(pe, EV[("pv", L, j, t)])
                    turn(e, [o[:, t, k * P:(k + 1) * P] for k in range(2) for t in range(T)])

            def turn_g(L, g, wait, turns=0):
                for t in range(T):
                    e = EV[("g", L, g, t)]
                    use(e, turns)
                    pe.wait_ge(gu_out, turns * 2 + (wait + t + 1))
                    turn(e, [aT[:, 1, t * 256 + k * P:t * 256 + (k + 1) * P] for k in range(2)])

            def down_unit(L, s, b, g, first, last, turns=0):
                if b == 0:
                    for t in range(T):
                        e = EV[("g", L, g, t)]
                        pe.wait_ge(turn_out[e % 2], turns + (e // 2 + 1))
                wide_unit(L, s, b, ghi, glo, first, last, G_DOWN, [(0, 512), (512, 1024)], turns)

            pe.wait_ge(consts, 2)
            pe.wait_ge(first_gains_in, 16)
            pe.transpose(tb[0][:, 0:16], gain_rows[0:16, :], ident[0:16, 0:16]).then_inc(gains_turned, 1)
            pe.wait_ge(gains_in, 16 * 11)
            pe.transpose(tb[1][:, 0:GAIN_ROWS], gain_rows[0:GAIN_ROWS, :], ident[0:GAIN_ROWS, 0:GAIN_ROWS])\
                .then_inc(gains_turned, 1)
            pe.wait_ge(gains_ready, 2)

            for L in range(LAYERS):
                def h_start(q):
                    if L == 0:
                        pe.wait_ge(x_in, 32)
                    elif L == 2:
                        pe.wait_ge(fin_ready, q + 1)
                    else:
                        pe.wait_ge(bank_out[q], GROUPS * L)
                for s in range(U_FFN):
                    if s == 0:
                        turn_x(L, 0, h_start)
                    if s == U_GU0:
                        turn_x(L, 1, lambda q: pe.wait_ge(bank_out[q], GROUPS * L + G_WO + 1))
                    if L == L_FX and s == 1:
                        e = EV[("flog", L)]
                        use(e)
                        pe.wait_ge(wf_ready, 1)
                        wait_out(pe, EV[("x", L, 0, 2)])
                        wait_out(pe, EV[("x", L, 0, 3)])
                        for t in range(T):
                            for kb in range(KB):
                                c = slice(t * P, (t + 1) * P)
                                ins = three(tb[e % 2][:, 16 * t:16 * t + 16], xhi[:, kb, c], xlo[:, kb, c],
                                            wfhi[:, kb, :], wflo[:, kb, :], kb == 0, kb == KB - 1)
                        ins.then_inc(turned, 1)
                    if L == L_FX and s == 3:
                        e = EV[("flogT", L)]
                        use(e)
                        pe.wait_ge(f_ready, 1)
                        turn(e, [f2[:, t, :] for t in range(T)])
                    if L == L_FX and s == 4:
                        e = EV[("fcum", L)]
                        use(e)
                        pe.wait_ge(nfc_ready, 1)
                        turn(e, [nfcT[:, t * P:(t + 1) * P] for t in range(T)])
                    for name, j in steps(PE_STEPS, L, s):
                        attention(L, name, j)
                    if s == U_GU0 + 2:
                        e = EV[("side", L)]
                        use(e)
                        pe.wait_ge(side_in, 16 * (L + 1))
                        turn(e, [side[:, t, k * P:(k + 1) * P] for k in range(2) for t in range(T)])
                    if s < U_WO:
                        if s in (0, 2):
                            for q in range(2):
                                wait_out(pe, EV[("x", L, 0, q + s)])
                        qkv_unit(L, s)
                    elif s < U_GU0:
                        kb = s - U_WO
                        wait_out(pe, EV[("o", L, kb // 2)])
                        wide_unit(L, s, kb, ohi, olo, kb == 0, kb == KB - 1, G_WO, [(0, 512), (512, 1024)])
                    else:
                        if s in (U_GU0, U_GU0 + 2):
                            for q in range(2):
                                wait_out(pe, EV[("x", L, 1, q + (2 if s > U_GU0 else 0))])
                        gu_unit(L, s, s - U_GU0)

                def ffn_body(i, first):
                    for b in range(4):
                        if b == 1:
                            turn_g(L, 0, 2 * NG * L, i)
                        gu_unit(L, U_FFN + b, b, i)
                    for b in range(2):
                        down_unit(L, U_FFN + 4 + b, b, 0, first and b == 0, False, i)

                ffn_body(0, True)
                with pe.Fori(1, NG - 1) as i:
                    ffn_body(i, False)
                turn_g(L, NG - 1, 2 * NG * L + 2 * (NG - 1))
                proj_unit(L, U_PROJ_A, 0)
                for b in range(2):
                    down_unit(L, U_DOWN_LAST + b, b, NG - 1, False, b == 1)
                proj_unit(L, U_PROJ_B, 1)
                turn_x(L, 2, lambda q: pe.wait_ge(bank_out[q], GROUPS * L + G_DOWN + 1))
                for kb in range(KB):
                    if kb in (0, 4):
                        for q in range(2):
                            wait_out(pe, EV[("x", L, 2, q + (2 if kb else 0))])
                    wide_unit(L, U_GATE + kb, kb, xhi, xlo, kb == 0, kb == KB - 1, G_GATE, [(0, 512), (512, 1024)])


_INS = ['x', 'p', 'norm_mix', 'norm_ffn', 'norm_ple', 'norm_final', 'da_w_qkv', 'da_w_o', 'da_lambda_q1',
        'da_lambda_k1', 'da_lambda_q2', 'da_lambda_k2', 'da_subln', 'na_w_qkv', 'na_b_qkv', 'na_rpb', 'na_w_o',
        'ffn_w_gate', 'ffn_w_up', 'ffn_w_down', 'ple_w_proj', 'ple_w_gate', 'p_2', 'attn_norm_g_2', 'sb_w_qkv_2',
        'sb_w_o_2', 'shared_norm_g_2', 'shared_w_kvf_2', 'shared_b_f_2', 'shared_k_norm_g_2', 'fox_w_q_2',
        'fox_q_norm_g_2', 'fox_w_o_2', 'ffn_norm_g_2', 'ffn_w_gu_2', 'ffn_w_d_2', 'ple_norm_g_2', 'ple_w_gate_2',
        'ple_w_proj_2']


def kernel(**inputs):
    import numpy as _np
    import concourse.bacc as _bacc
    from concourse import mybir as _mybir
    from concourse.bass_utils import run_bass_kernel_spmd as _run

    nc = _bacc.Bacc("TRN2", target_bir_lowering=False, num_devices=1)
    arrays, args = {}, {}
    for name in _INS:
        x = _np.ascontiguousarray(inputs[name])
        arrays[f"in_{name}"] = x
        args[name] = nc.dram_tensor(f"in_{name}", x.shape, _mybir.dt.from_np(x.dtype), kind="ExternalInput").ap()
    out = nc.dram_tensor("out", (1, S, D), _mybir.dt.float32, kind="ExternalOutput").ap()
    build(nc, args, out)
    r = _run(nc, [arrays], core_ids=[0])
    return r.results[0]["out"]
```

```python
from contextlib import ExitStack

import math

import concourse.bass as bass
from concourse import mybir

F32 = mybir.dt.float32
F32R = mybir.dt.float32r
BF16 = mybir.dt.bfloat16
ALU = mybir.AluOpType
ACT = mybir.ActivationFunctionType
AX_X = mybir.AxisListType.X

P = 128
S = 256
T = S // P
D = 1024
KB = D // P
F = 2816
GC_COLS = 256
NG = F // GC_COLS
PD = 256
HG = 4
L_DA, L_NA, L_SB, L_FX = range(4)
LAYERS = 4
SCALE = 0.125
LAM_INIT = 0.8 - 0.6 * math.exp(-0.3 * 0)
MASKED = -1e30
EPS = 1e-6
SUB_EPS = 1e-5

RING = 6
AHEAD = RING - 2
LO_AHEAD = AHEAD - 1
U_QKV = 0
QK_UNITS, V_UNITS = KB // 2, KB // 4
GROUP_UNITS = QK_UNITS + V_UNITS
U_WO = U_QKV + HG * GROUP_UNITS
SIDE_SLOT = U_WO + 6
U_GU0 = U_WO + KB
U_FFN = U_GU0 + 4
U_DOWN_LAST = U_FFN + 6 * (NG - 1)
U_PROJ = U_DOWN_LAST + 2
U_GATE = U_PROJ + 2
UNITS = U_GATE + KB

G_WO, G_DOWN, G_GATE, GROUPS = 4, 5, 6, 7


def count(labels):
    return {x: n + 1 for n, x in enumerate(labels)}


PE_STEPS = {
    L_DA: [["evacqk"], ["turnqk"], ["scores0"], ["scores1"], [], ["turnp0"], ["pv0", "turnp1"], ["pv1"], ["turno"]],
    L_NA: [["evacqk"], ["turnqk"], ["scores0"], ["scores1"], ["turnp0"], ["pv0", "turnp1"], ["pv1"], ["turno"]],
    L_SB: [["evacqk"], ["turnqk"], ["scores0"], ["scores1"], [], ["turnp0"], ["pv0", "turnp1"], ["pv1"], ["turno"]],
    L_FX: [["evacqk"], [], ["turnqk"], ["scores0"], ["scores1"], ["turnp0"], ["pv0", "turnp1"], ["pv1"], ["turno"]],
}
ACT_STEPS = {
    L_DA: [["evacqk"], ["turnqk"], [], ["exp0"], ["exp1"], ["turnp0"], ["pv0", "turnp1"], ["pv1"], ["turno"]],
    L_NA: [["evacqk"], ["turnqk"], [], ["exp0"], ["turnp0", "exp1"], ["turnp1"], [], ["turno"]],
    L_SB: [["evacqk"], ["turnqk"], [], ["exp0"], ["exp1"], ["turnp0"], ["pv0", "turnp1"], ["pv1"], ["turno"]],
    L_FX: [["evacqk"], [], ["turnqk"], [], ["exp0"], ["turnp0", "exp1"], ["turnp1"], [], ["turno"]],
}
DVE_STEPS = {
    L_DA: [[], ["turnqk"], ["evacv", "scores0"], ["scores1"], ["post0"], ["post1"], ["pv0", "turnp1"], ["pv1"],
           ["turno"]],
    L_NA: [["evacqk"], ["turnqk"], ["evacv", "scores0"], ["scores1"], ["turnp0", "post0"],
           ["pv0", "turnp1", "post1"], ["pv1"], ["turno"]],
    L_SB: [[], [], ["evacv", "scores0"], ["scores1"], ["post0"], ["post1", "turnp0"], ["pv0", "turnp1"],
           ["pv1"], ["turno"]],
    L_FX: [["evacqk"], ["headnorm"], ["evacv"], ["scores0"], ["scores1"], ["turnp0", "post0"],
           ["pv0", "turnp1", "post1"], ["pv1"], ["turno"]],
}


def order(L):
    return range(HG)[::-1] if L in (L_DA, L_NA) else range(HG)


def steps(tables, L, s):
    found = []
    for j in order(L):
        r = s - GROUP_UNITS * j - QK_UNITS
        if L == L_FX and j == 0 and r > 0:
            r = r - 1 if r > 1 else -1
        if 0 <= r < len(tables[L]):
            found += [(name, j) for name in tables[L][r]]
    return found


def keys(L, t):
    return P if L >= L_SB and t == 0 else S


def split_scores(L):
    return L < L_SB


def p_blocks(L, t):
    n = keys(L, t) // P
    if L == L_DA:
        return [(0, b, k) for b in range(2) for k in range(n)]
    return [(q, b, k) for q in range(2) for b in range(2) for k in range(n)]


FORGET = {2: "flog", 3: "flogB", 5: "flogT", 6: "fcum"}


def halves_at(r):
    return (2 * r, 2 * r + 1)


def turn_events():
    ev = []
    for L in range(LAYERS):
        for s in range(UNITS):
            if s == 0 and L == 0:
                ev.append(("gain", 0))
            for n, first in enumerate((0, U_GU0, U_GATE - 1)):
                if s in (first, first + 1):
                    ev += [("x", L, n, q) for q in halves_at(s - first)]
            if s == 3 and L == 0:
                ev.append(("gain", 1))
            if L == L_FX and s in FORGET:
                ev.append((FORGET[s], L))
            for name, j in steps(PE_STEPS, L, s):
                if name == "turnqk":
                    ev += [("qk", L, j, t) for t in range(T)]
                elif name.startswith("turnp"):
                    t = int(name[-1])
                    ev += [("p", L, j, t, n) for n in range(len(p_blocks(L, t)) // 4)]
                elif name.startswith("pv"):
                    ev.append(("pv", L, j, int(name[-1])))
                elif name == "turno":
                    ev.append(("o", L, j))
            if s == SIDE_SLOT:
                ev.append(("side", L))
            if U_FFN <= s < U_DOWN_LAST and (s - U_FFN) % 6 == 1:
                ev += [("g", L, (s - U_FFN) // 6, t) for t in range(T)]
            if s == U_DOWN_LAST - 1:
                ev += [("g", L, NG - 1, t) for t in range(T)]
    return ev


EV_LIST = turn_events()
EV = {x: n for n, x in enumerate(EV_LIST)}
SPLIT = count([x for x in EV_LIST if x[0] in ("x", "o", "g", "side") or x[0] == "qk" and split_scores(x[1])])
NORMS = [(L, n) for L in range(2) for n in range(3)] + [(1, 3)] + [(L, n) for L in range(2, 4) for n in range(3)]
NORM = count(NORMS)
SUMS = {x: n for n, x in enumerate(x for x in NORMS if x != (1, 3))}
ATT = count([(L, j, t) for L in range(LAYERS) for j in range(HG) for t in range(T)])
SOFT = count([(L, j, t) for L in (L_DA, L_NA, L_FX) for j in range(HG) for t in range(T)])

GAIN_MIX, GAIN_FFN, GAIN_PLE = [0, 8, 48, 56], [16, 24, 64, 72], [32, 40, 80, 88]
GAIN_SHARED, GAIN_SUB, GAIN_K, GAIN_Q, GAIN_ROWS = 96, 104, 105, 106, 107


def halves(q):
    return q // 2, q % 2


def unit_parts(L, s):
    if s < U_WO:
        b = s % GROUP_UNITS
        kv_gain = GAIN_SHARED if L == L_FX else GAIN_MIX[L]
        if b >= QK_UNITS:
            return [(256 * k, 256 * k + 256, kv_gain + 4 * (b - QK_UNITS) + k) for k in range(4)]
        if L == L_FX:
            return [(512 * k + 256 * x, 512 * k + 256 * x + 256, g + 2 * b + k)
                    for k in range(2) for x, g in enumerate((GAIN_MIX[L], GAIN_SHARED))]
        return [(512 * k, 512 * k + 512, GAIN_MIX[L] + 2 * b + k) for k in range(2)]
    if s < U_GU0:
        return [(0, 1024, GAIN_SUB if L == L_DA else None)]
    if s < U_DOWN_LAST:
        b = s - U_GU0 if s < U_FFN else (s - U_FFN) % 6
        if b < 4:
            return [(0, 512, GAIN_FFN[L] + 2 * b), (512, 1024, GAIN_FFN[L] + 2 * b + 1)]
        return [(0, 1024, None)]
    if s < U_GATE:
        return [(0, 1024, None)]
    return [(0, 1024, GAIN_PLE[L] + s - U_GATE)]


def build(nc, a, out):
    ctx = ExitStack()
    with ctx:
        def sb(name, shape, dt=F32):
            return ctx.enter_context(nc.sbuf_tensor(name, shape, dt))

        def ps(name, shape):
            return ctx.enter_context(nc.psum_tensor(name, shape, F32))

        def sem(name):
            return ctx.enter_context(nc.semaphore(name))

        raw = sb("raw", [P, RING, 1024])
        whi = sb("whi", [P, RING, 1024], F32R)
        wlo = sb("wlo", [P, RING, 1024], F32R)
        h = sb("h", [P, T, D])
        xhi = sb("xhi", [P, KB, S], F32R)
        xlo = sb("xlo", [P, KB, S], F32R)
        ohi = sb("ohi", [P, KB, S], F32R)
        olo = sb("olo", [P, KB, S], F32R)
        split_qg = sb("split_qg", [P, 4, S], F32R)
        ghi, glo = split_qg[:, 0:2, :], split_qg[:, 2:4, :]
        qklo = split_qg
        phi = sb("phi", [P, 2, S], F32R)
        plo = sb("plo", [P, 2, S], F32R)
        side = sb("side", [P, T, PD])
        qkv = sb("qkv", [P, 2, T, 768])
        qkT = sb("qkT", [P, 4, S], F32R)
        z = sb("z", [P, T, 1024])
        aT = sb("aT", [P, T, 1024])
        bias = sb("bias", [P, T, HG, 1024])
        o = sb("o", [P, T, 256])
        nab = sb("nab", [P, 2, 768])
        fin_gain = sb("fin_gain", [P, D])
        qk32 = fin_gain[:, :].rearrange("p (k c) -> p k c", k=4)
        ident = sb("ident", [P, P])
        gain_rows = sb("gain_rows", [P, P])
        gain = sb("gain", [P, GAIN_ROWS])
        junk = sb("junk", [P, D], BF16)
        ss = sb("ss", [P, len(NORMS), T])
        ss4 = sb("ss4", [P, 4])
        rstd = sb("rstd", [P, len(NORMS), T])
        powm = sb("powm", [P, 8])
        mx = sb("mx", [P, T, 4])
        sums = sb("sums", [P, T, 4])
        rsum = sb("rsum", [P, T, 4])
        lamc = sb("lamc", [P, T, 2])
        ss_o = sb("ss_o", [P, T, 2])
        r_o = sb("r_o", [P, T, 2])
        ss_h = sb("ss_h", [P, T, 8])
        r_h = sb("r_h", [P, T, 8])
        lam_in = sb("lam_in", [P, 4, 64])
        lam = sb("lam", [P, 4])
        strict = sb("strict", [P, S])
        incl = sb("incl", [P, P])
        window = sb("window", [P, 64])
        wf = sb("wf", [P, KB, 16])
        wfg = sb("wfg", [P, KB, 16])
        wfhi = sb("wfhi", [P, KB, 16], F32R)
        wflo = sb("wflo", [P, KB, 16], F32R)
        bf = sb("bf", [P, 16])
        f = sb("f", [P, T, 16])
        f2 = sb("f2", [P, T, 16])
        fT, nfcT = o[0:16, 0, :], o[0:16, 1, :]
        ones_sb, zeros_sb, warm = sb("ones_sb", [P, 1]), sb("zeros_sb", [P, 1]), sb("warm", [P, 1])
        dist = nab[:, :, 0:S]
        nfc = sb("nfc", [P, T, 16])
        rpb_rows = nab[0:120, 0, S:S + 62].rearrange("p (i c) -> p i c", i=2)
        rpb_back = nab[0:120, 1, S:S + 62].rearrange("p (i c) -> p i c", i=2)
        rpb_dram = nc.dram_tensor("rpb_scratch", (120, 2, 31), F32, kind="Internal").ap()
        nfc_dram = nc.dram_tensor("nfc_scratch", (16, S), F32, kind="Internal").ap()

        acc = [ps(f"acc{b}", [P, 512]) for b in range(4)]
        sc = ps("sc", [P, 2, 512])
        tb = [ps(f"turn{b}", [P, 512]) for b in range(2)]

        weights_in = [sem(f"weights_in{i}") for i in range(RING)]
        hi_done, lo_done, unit_done = sem("hi_done"), sem("lo_done"), sem("unit_done")
        acc_done = sem("acc_done")
        bank_out = [sem(f"bank_out{b}") for b in range(4)]
        gu_done, gu_out = sem("gu_done"), sem("gu_out")
        sig_done, gmid = sem("sig_done"), sem("gmid")
        gated = sem("gated")
        proj_out, gate_sig = sem("proj_out"), sem("gate_sig")
        turned = sem("turned")
        turn_hi = sem("turn_hi")
        turn_out = [sem(f"turn_out{b}") for b in range(2)]
        x_in, nab_in = [sem(f"x_in{q}") for q in range(4)], [sem(f"nab_in{i}") for i in range(2)]
        gains_in, side_in, misc_in = sem("gains_in"), sem("side_in"), sem("misc_in")
        first_gains_in = sem("first_gains_in")
        gains_ready = sem("gains_ready")
        consts, zero_ready = sem("consts"), sem("zero_ready")
        quarter_ss = sem("quarter_ss")
        ss_ready, rstd_ready, fin_ready = sem("ss_ready"), sem("rstd_ready"), sem("fin_ready")
        scores_done, z_ready, mx_ready, e_ready = (sem("scores_done"), sem("z_ready"), sem("mx_ready"),
                                                   sem("e_ready"))
        a_ready, sp_ready, arg_ready = sem("a_ready"), sem("sp_ready"), sem("arg_ready")
        so_ready, ro_ready = sem("so_ready"), sem("ro_ready")
        rpb_load, rpb_store = sem("rpb_load"), sem("rpb_store")
        bias_ready, rpb_in = sem("bias_ready"), sem("rpb_in")
        sq_ready, sh_ready, rh_ready, qk_ready = (sem("sq_ready"), sem("sh_ready"), sem("rh_ready"),
                                                  sem("qk_ready"))
        lam_dot, lam_exp = sem("lam_dot"), sem("lam_exp")
        wf_g, wf_hi, wf_ready = sem("wf_g"), sem("wf_hi"), sem("wf_ready")
        f_ready, f_sp, nfc_ready, nfc_store, nfc_load = (sem("f_ready"), sem("f_sp"), sem("nfc_ready"),
                                                         sem("nfc_store"), sem("nfc_load"))
        act_link, dve_link, pool_link = sem("act_link"), sem("dve_link"), sem("pool_link")
        out_stored = sem("out_stored")

        def acc_wait(eng, L, g, b, last):
            if g < HG:
                done, own = 2 * g + b // 2 + 1, b % 2 == 0
            else:
                done, own = 2 * HG + 3 * (g - HG) + b + 1, b < 3
            if own:
                eng.wait_ge(acc_done, (2 * HG + 3 * (GROUPS - HG)) * L + done)
            else:
                eng.wait_ge(unit_done, UNITS * L + last + 1)

        def wait_out(eng, e):
            eng.wait_ge(turn_out[e % 2], e // 2 + 1)

        def rs(L, n, t):
            i = NORM[(L, n)] - 1
            return rstd[:, i, t:t + 1]

        qkv_cols = [[(w, x * D) for x in range(3)] for w in (a["da_w_qkv"][0], a["na_w_qkv"][0], a["sb_w_qkv_2"][0])]
        qkv_cols.append([(a["fox_w_q_2"][0], 0), (a["shared_w_kvf_2"], 0), (a["shared_w_kvf_2"], D)])
        wo_w = [a["da_w_o"][0], a["na_w_o"][0], a["sb_w_o_2"][0], a["fox_w_o_2"][0]]

        def gate_up(L):
            if L < 2:
                return a["ffn_w_gate"][L], a["ffn_w_up"][L], 0
            return a["ffn_w_gu_2"][L - 2], a["ffn_w_gu_2"][L - 2], F

        down_w = [a["ffn_w_down"][0], a["ffn_w_down"][1], a["ffn_w_d_2"][0], a["ffn_w_d_2"][1]]
        proj_w = [a["ple_w_proj"][0], a["ple_w_proj"][1], a["ple_w_proj_2"][0], a["ple_w_proj_2"][1]]
        pgate_w = [a["ple_w_gate"][0], a["ple_w_gate"][1], a["ple_w_gate_2"][0], a["ple_w_gate_2"][1]]
        side_x = [a["p"][0, 0], a["p"][1, 0], a["p_2"][0, 0], a["p_2"][1, 0]]

        block = ctx.enter_context(nc.Block())

        @block.sync
        def _(sp):
            def load(u, parts, turns=0):
                if not isinstance(turns, int) or u >= RING:
                    sp.wait_ge(lo_done, turns * 6 + (u - RING + 1))
                for dst, src, n in parts:
                    sp.dma_start(dst, src).then_inc(weights_in[u % RING], 16 * n)

            def rows(w, kb, c0, c1):
                return w[kb * P:(kb + 1) * P, c0:c1]

            def load_misc():
                vecs = [("norm_ffn", 16, 16), ("norm_ple", 32, 16), ("attn_norm_g_2", 48, 16),
                        ("ffn_norm_g_2", 64, 16), ("ple_norm_g_2", 80, 16)]
                for name, r, n in vecs:
                    sp.dma_start(gain_rows[r:r + n, :], a[name].rearrange("l (k p) -> (l k) p", p=P))\
                        .then_inc(gains_in, 16)
                sp.dma_start(gain_rows[96:104, :], a["shared_norm_g_2"].rearrange("(k p) -> k p", p=P))\
                    .then_inc(gains_in, 16)
                sp.dma_start(gain_rows[104:105, :], a["da_subln"]).then_inc(gains_in, 16)
                for i in range(2):
                    sp.dma_start(gain_rows[105:106, 64 * i:64 * i + 64],
                                  a["shared_k_norm_g_2"].rearrange("(a p) -> a p", a=1)).then_inc(gains_in, 16)
                    sp.dma_start(gain_rows[106:107, 64 * i:64 * i + 64], a["fox_q_norm_g_2"]).then_inc(gains_in, 16)
                for i, name in enumerate(("da_lambda_q1", "da_lambda_k1", "da_lambda_q2", "da_lambda_k2")):
                    sp.dma_start(lam_in[:, i, :], a[name].to_broadcast([P, 64])).then_inc(misc_in, 16)
                sp.dma_start(fin_gain[:, :], a["norm_final"].rearrange("(a p) -> a p", a=1).to_broadcast([P, D]))\
                    .then_inc(misc_in, 16)
                sp.dma_start(wf[:, :, :], a["shared_w_kvf_2"][:, 2 * D:2 * D + 16].rearrange("(k p) c -> p k c", p=P))\
                    .then_inc(misc_in, 16)
                sp.dma_start(bf[:, :], a["shared_b_f_2"].rearrange("(a p) -> a p", a=1).to_broadcast([P, 16]))\
                    .then_inc(misc_in, 16)

            def gu_parts(L, u, b, c0):
                gate, up, at = gate_up(L)
                dst = raw[:, u % RING, :].rearrange("p (k s c) -> p s k c", k=2, s=2)
                parts = []
                for sx, (w, off) in enumerate(((gate, 0), (up, at))):
                    src = w[2 * b * P:(2 * b + 2) * P, bass.ds(c0 + off, GC_COLS)]
                    parts.append((dst[:, sx], src.rearrange("(k p) c -> p k c", p=P), 1))
                return parts

            for L in range(LAYERS):
                base = UNITS * L
                q_w, k_w, v_w = qkv_cols[L]
                for s in range(U_QKV, U_WO):
                    u, j, b = base + s, s // GROUP_UNITS, s % GROUP_UNITS
                    if u < 2:
                        for q in halves_at(u):
                            hf, t = halves(q)
                            sp.dma_start(h[:, t, hf * 512:hf * 512 + 512],
                                         a["x"][0, t * P:(t + 1) * P, hf * 512:hf * 512 + 512]).then_inc(x_in[q], 16)
                    if u == RING:
                        load_misc()
                    if b < QK_UNITS:
                        dst = raw[:, u % RING, :].rearrange("p (k s c) -> p s k c", k=2, s=2)
                        load(u, [(dst[:, x], w[2 * b * P:(2 * b + 2) * P, at + j * 256:at + j * 256 + 256]
                                  .rearrange("(k p) c -> p k c", p=P), 1) for x, (w, at) in enumerate((q_w, k_w))])
                    else:
                        w, at = v_w
                        v_rows = w[4 * (b - QK_UNITS) * P:4 * (b - QK_UNITS + 1) * P, at + j * 256:at + j * 256 + 256]
                        load(u, [(raw[:, u % RING, :].rearrange("p (k c) -> p k c", k=4),
                                  v_rows.rearrange("(k p) c -> p k c", p=P), 2)])
                for kb in range(KB):
                    u = base + U_WO + kb
                    load(u, [(raw[:, u % RING, :], rows(wo_w[L], kb, 0, D), 2)])
                for b in range(4):
                    u = base + U_GU0 + b
                    load(u, gu_parts(L, u, b, 0))
                with sp.Fori(0, NG - 1) as i:
                    for b in range(4):
                        u = base + U_FFN + b
                        load(u, gu_parts(L, u, b, i * GC_COLS + GC_COLS), i)
                    for b in range(2):
                        u = base + U_FFN + 4 + b
                        src = down_w[L].rearrange("(g k p) c -> g k p c", k=2, p=P)[bass.ds(i, 1), b]
                        load(u, [(raw[:, u % RING, :], src.rearrange("g p c -> p (g c)"), 2)], i)

                def proj_parts(u, half):
                    dst = raw[:, u % RING, :].rearrange("p (k c) -> p k c", k=2)
                    return [(dst, proj_w[L][:, half * 512:half * 512 + 512].rearrange("(k p) c -> p k c", p=P), 2)]

                for b in range(2):
                    u = base + U_DOWN_LAST + b
                    load(u, [(raw[:, u % RING, :], rows(down_w[L], 2 * (NG - 1) + b, 0, D), 2)])
                for b in range(2):
                    u = base + U_PROJ + b
                    load(u, proj_parts(u, b))
                for kb in range(KB):
                    u = base + U_GATE + kb
                    load(u, [(raw[:, u % RING, :], rows(pgate_w[L], kb, 0, D), 2)])
            for q in range(4):
                hf, t = halves(q)
                sp.wait_ge(bank_out[q], GROUPS * LAYERS)
                sp.dma_start(out[0, t * P:(t + 1) * P, hf * 512:hf * 512 + 512],
                             h[:, t, hf * 512:hf * 512 + 512]).then_inc(out_stored, 16)
            sp.wait_ge(out_stored, 64)

        @block.gpsimd
        def _(pool):
            links = [0]

            def link(ins):
                links[0] += 1
                ins.then_inc(pool_link, 1)
                pool.wait_ge(pool_link, links[0])

            link(pool.memset(ident[:, :], 0.0))
            pool.affine_select(out=ident[:, :], in_=ident[:, :], compare_op=ALU.not_equal, fill=1.0, base=0,
                               pattern=[[-1, P]], channel_multiplier=1).then_inc(consts, 1)
            link(pool.memset(powm[:, :], -0.5))
            for t in range(T):
                link(pool.iota(dist[:, t, :], pattern=[[-1, S]], base=t * P, channel_multiplier=1,
                               allow_small_or_imprecise_dtypes=True))
                link(pool.tensor_scalar(o[:, t, :], dist[:, t, :], -1.0, 0.0, ALU.mult, ALU.max))
                link(pool.tensor_scalar(dist[:, t, :], dist[:, t, :], 0.0, 1.0, ALU.max, ALU.mult))
                link(pool.tensor_tensor(dist[:, t, :], dist[:, t, :], o[:, t, :], ALU.add))
            for j in range(HG):
                for blk in range(2):
                    slope = 2.0 ** -(2 * j + blk + 1)
                    for t in range(T):
                        for par in range(2):
                            at = par * 512 + blk * 256
                            last = pool.tensor_scalar(bias[:, t, j, at:at + S], dist[:, t, :], -slope, 1.0 / SCALE,
                                                      ALU.mult, ALU.mult)
                last.then_inc(bias_ready, 1)
            def rms(dst, src, n, width, eps, ready):
                link(pool.tensor_scalar(dst, src, 1.0 / width, eps, ALU.mult, ALU.add))
                pool.tensor_tensor(dst, dst, powm[:, 0:n], ALU.pow).then_inc(ready, 1)

            def norm(L, n):
                i = NORM[(L, n)] - 1
                pool.wait_ge(ss_ready, 2 * (SUMS[(L, n)] + 1))
                rms(rstd[:, i, :], ss[:, i, :], 2, D, EPS, rstd_ready)

            def load_side(L):
                if L:
                    pool.wait_ge(turned, EV[("side", L - 1)] + 1)
                pool.dma_start(side[:, :, :], side_x[L].rearrange("(t p) c -> p t c", p=P)).then_inc(side_in, 16)

            def head_rms(j):
                for t in range(T):
                    pool.wait_ge(sh_ready, 2 * j + t + 1)
                    rms(r_h[:, t, :], ss_h[:, t, :], 8, 64, EPS, rh_ready)

            def forget_load(j):
                pool.dma_start(bias[:, 1, j, :], nfc_dram[4 * j:4 * j + 4, :].rearrange("h (a c) -> a (h c)", a=1)
                               .to_broadcast([P, 4 * S])).then_inc(nfc_load, 16)

            def forget_bias(j):
                pool.wait_ge(nfc_load, 16 * (j + 1))
                src = bias[:, 1, j, :].rearrange("p (x c) -> p x c", c=S)
                dst = bias[:, 0, j, :].rearrange("p (x c) -> p x c", c=S)
                m = incl[:, :].unsqueeze(1).to_broadcast([P, 4, P])
                pool.tensor_tensor(dst[:, :, 0:P], src[:, :, 0:P], m, ALU.add)
                pool.tensor_tensor(src[:, :, P:S], src[:, :, P:S], m, ALU.add).then_inc(bias_ready, 1)

            def load_nab(j):
                src = a["na_b_qkv"].rearrange("a (s c) -> a s c", s=3)[:, :, j * 256:j * 256 + 256]
                pool.dma_start(nab[:, j % 2, :].rearrange("p (s c) -> p s c", s=3),
                               src.to_broadcast([P, 3, 256])).then_inc(nab_in[j % 2], 16)

            def later_tables():
                link(pool.memset(strict[:, :], 0.0))
                link(pool.affine_select(out=strict[:, P:S], in_=strict[:, P:S], compare_op=ALU.is_gt, fill=MASKED,
                                        base=0, pattern=[[-1, P]], channel_multiplier=1))
                link(pool.memset(incl[:, :], 0.0))
                link(pool.affine_select(out=incl[:, :], in_=incl[:, :], compare_op=ALU.is_ge, fill=MASKED,
                                        base=0, pattern=[[-1, P]], channel_multiplier=1))
                pool.dma_start(rpb_rows[:, :, :], a["na_rpb"].rearrange("l h (r i) c -> (l h r i) c", i=1)
                               .rearrange("(p i) c -> p i c", i=2)).then_inc(rpb_load, 16)
                pool.wait_ge(rpb_load, 16)
                link(pool.tensor_scalar(rpb_back[:, :, :], rpb_rows[:, :, ::-1], 1.0, 1.0 / SCALE, ALU.mult, ALU.mult))
                pool.dma_start(rpb_dram[:, :, :], rpb_back[:, :, :]).then_inc(rpb_store, 16)
                link(pool.memset(window[:, :], 0.0))
                for r in range(2):
                    w = window[64 * r:64 * r + 64]
                    link(pool.affine_select(out=w[:, 0:48], in_=w[:, 0:48], compare_op=ALU.is_ge, fill=MASKED,
                                            base=8, pattern=[[1, 48]], channel_multiplier=-1))
                    link(pool.affine_select(out=w[:, 16:64], in_=w[:, 16:64], compare_op=ALU.is_gt, fill=MASKED,
                                            base=8 - 16, pattern=[[-1, 48]], channel_multiplier=1))

            for L in range(LAYERS):
                norm(L, 0)
                load_side(L)
                if L == L_DA:
                    later_tables()
                if L == L_FX:
                    pool.wait_ge(nfc_ready, 1)
                    pool.dma_start(nfc_dram[:, :], nfcT).then_inc(nfc_store, 16)
                    head_rms(0)
                    pool.wait_ge(nfc_store, 16)
                    forget_load(0)
                for s in range(U_GU0):
                    if L == L_NA and s < U_WO and s % GROUP_UNITS == 0:
                        j = s // GROUP_UNITS
                        if j >= 2:
                            pool.wait_ge(bank_out[3], GROUPS * L + j - 1)
                        load_nab(j)
                    for name, j in steps(PE_STEPS, L, s):
                        if L == L_FX and name == "evacqk":
                            if j:
                                head_rms(j)
                            for n in ([0, 1] if j == 0 else [j + 1] if j + 1 < HG else []):
                                forget_bias(n)
                                if n + 1 < HG:
                                    forget_load(n + 1)
                        if L == L_DA and name.startswith("pv"):
                            t = int(name[-1])
                            pool.wait_ge(so_ready, 2 * j + t + 1)
                            rms(r_o[:, t, :], ss_o[:, t, :], 2, 128, SUB_EPS, ro_ready)
                norm(L, 1)
                if L == L_DA:
                    pool.wait_ge(rpb_store, 16)
                    pool.wait_ge(z_ready, ATT[(L_DA, HG - 1, T - 1)])
                    for t in range(T):
                        for r2 in range(2):
                            for j in range(HG):
                                for x in range(4):
                                    par, blk = x // 2, x % 2
                                    head = 4 * j + 2 * blk + par
                                    src = bass.AP(tensor=rpb_dram.tensor,
                                                  offset=(head * 15 + 7 - 2 * t - r2) * 31 + 15 - 63,
                                                  ap=[[1, 64], [31, 4], [1, 64]])
                                    dst = bias[64 * r2:64 * r2 + 64, t, j, x * 256:x * 256 + 256]
                                    pool.dma_start(dst.rearrange("p (r c) -> p r c", c=64), src)\
                                        .then_inc(rpb_in, 16)
                    pool.wait_ge(rpb_in, 16 * 64)
                    for t in range(T):
                        b = bias[:, t, :, :].rearrange("p j (r c) -> p (j r) c", c=64)
                        pool.tensor_tensor(b, b, window[:, ::-1].unsqueeze(1).to_broadcast([P, 64, 64]), ALU.add)\
                            .then_inc(bias_ready, 1)
                norm(L, 2)
                if L == 1:
                    i = NORM[(1, 3)] - 1
                    pool.wait_ge(quarter_ss, 4)
                    link(pool.tensor_tensor(ss[:, i, :], ss4[:, 0:2], ss4[:, 2:4], ALU.add))
                    rms(rstd[:, i, :], ss[:, i, :], 2, D, EPS, rstd_ready)

        @block.scalar
        def _(act):
            links = [0]

            def link(ins):
                links[0] += 1
                ins.then_inc(act_link, 1)
                act.wait_ge(act_link, links[0])

            act.dma_start(gain_rows[0:16, :], a["norm_mix"].rearrange("l (k p) -> (l k) p", p=P))\
                .then_inc(first_gains_in, 16)
            act.wait_ge(zero_ready, 1)
            act.activation(warm[:, :], zeros_sb[:, :], ACT.Copy)
            def split(u, parts, turns=0):
                act.wait_ge(weights_in[u % RING], turns * 32 + 32 * (u // RING + 1))
                if not isinstance(turns, int) or u >= RING:
                    act.wait_ge(unit_done, turns * 6 + (u - RING + 1))
                for c0, c1, g in parts:
                    scale = 1.0 if g is None else gain[:, g:g + 1]
                    ins = act.activation(whi[:, u % RING, c0:c1], raw[:, u % RING, c0:c1], ACT.Copy, scale=scale)
                ins.then_inc(hi_done, 1)

            def split_ahead(L, s):
                u = UNITS * L + s + AHEAD
                if u < LAYERS * UNITS:
                    split(u, unit_parts(u // UNITS, u % UNITS))

            def norm(L, n):
                i, done = NORM[(L, n)] - 1, 2 * SUMS[(L, n)]
                for t in range(T):
                    if done + t:
                        act.wait_ge(ss_ready, done + t)
                    act.activation(junk[:, :], h[:, t, :], ACT.Square, accum_out=ss[:, i, t:t + 1])\
                        .then_inc(ss_ready, 1)

            def turn_x(L, n, r):
                for q in halves_at(r):
                    hf, t = halves(q)
                    e = EV[("x", L, n, q)]
                    act.wait_ge(turned, e + 1)
                    act.activation(xhi[:, 4 * hf:4 * hf + 4, t * P:(t + 1) * P],
                                   tb[e % 2][:, :].rearrange("p (k c) -> p k c", k=4), ACT.Copy).then_inc(turn_hi, 1)

            def attention(L, name, j):
                t = int(name[-1]) if name[-1] in "01" else 0
                B = j % 2
                kk = keys(L, t)
                zt = z[:, t, :].rearrange("p (x c) -> p x c", c=S)[:, :, 0:kk]
                if name == "evacqk":
                    if L == L_NA:
                        return
                    act.wait_ge(rstd_ready, NORM[(L, 0)])
                    for t in range(T):
                        acc_wait(act, L, j, t, GROUP_UNITS * j + QK_UNITS - 1)
                        act.activation(qkv[:, B, t, 0:512], acc[t][:, :], ACT.Copy, scale=rs(L, 0, t))\
                            .then_inc(bank_out[t], 1)
                    if L == L_FX:
                        for t in range(T):
                            act.wait_ge(bank_out[t], GROUPS * L + j + 1)
                            act.activation(nab[:, t, 0:512], qkv[:, B, t, 0:512], ACT.Square).then_inc(sq_ready, 1)
                elif name == "turnqk":
                    for t in range(T):
                        e = EV[("qk", L, j, t)]
                        act.wait_ge(turned, e + 1)
                        src = tb[e % 2][:, :].rearrange("p (k c) -> p k c", k=4)
                        dst = qkT[:, :, t * P:(t + 1) * P]
                        if split_scores(L):
                            act.activation(dst, src, ACT.Copy).then_inc(turn_hi, 1)
                            continue
                        dst = qk32[:, :, t * P:(t + 1) * P]
                        if L == L_FX:
                            act.activation(dst[:, 0:2], src[:, 0:2], ACT.Copy, scale=gain[:, GAIN_Q:GAIN_Q + 1])
                            ins = act.activation(dst[:, 2:4], src[:, 2:4], ACT.Copy,
                                                 scale=gain[:, GAIN_K:GAIN_K + 1])
                        else:
                            ins = act.activation(dst, src, ACT.Copy)
                        ins.then_inc(turn_out[e % 2], 1)
                elif name.startswith("exp"):
                    if L == L_SB:
                        act.wait_ge(z_ready, ATT[(L, j, t)])
                        tmp = aT[:, t, :].rearrange("p (x c) -> p x c", c=S)[:, :, 0:kk]
                        act.activation(tmp, zt, ACT.Sigmoid, scale=-1.0)
                        act.activation(zt, zt, ACT.Sigmoid).then_inc(sp_ready, 1)
                    else:
                        if L == L_FX:
                            act.wait_ge(mx_ready, 2 * j + t + 1)
                        else:
                            act.wait_ge(z_ready, ATT[(L, j, t)])
                        for x in range(4):
                            ins = act.activation(zt[:, x, :], zt[:, x, :], ACT.Exp, bias=mx[:, t, x:x + 1],
                                                 scale=-1.0, accum_out=sums[:, t, x:x + 1])
                        ins.then_inc(e_ready, 1)
                elif name.startswith("turnp"):
                    e = EV[("p", L, j, t, 0)]
                    act.wait_ge(turned, e + 1)
                    act.activation(aT[:, t, 0:512], tb[e % 2][:, :], ACT.Copy).then_inc(turn_out[e % 2], 1)
                elif name.startswith("pv"):
                    e = EV[("pv", L, j, t)]
                    if L == L_DA:
                        act.wait_ge(turned, e + 1)
                        for x in range(2):
                            ins = act.activation(aT[:, t, x * P:(x + 1) * P], tb[e % 2][:, x * P:(x + 1) * P], ACT.Square,
                                                 accum_out=ss_o[:, t, x:x + 1])
                        ins.then_inc(so_ready, 1)
                    if L == L_SB:
                        act.wait_ge(turned, e + 1)
                        act.activation(o[:, t, :], tb[e % 2][:, 0:256], ACT.Copy).then_inc(turn_out[e % 2], 1)
                elif name == "turno":
                    e = EV[("o", L, j)]
                    act.wait_ge(turned, e + 1)
                    act.activation(ohi[:, 2 * j:2 * j + 2, :], tb[e % 2][:, :].rearrange("p (k c) -> p k c", k=2),
                                   ACT.Copy).then_inc(turn_hi, 1)

            def hidden_sig(L, t, bank):
                act.activation(aT[:, 0, t * 256:t * 256 + 256], bank[:, 0:256], ACT.Sigmoid, scale=rs(L, 1, t))\
                    .then_inc(sig_done, 1)

            wait_out(act, EV[("gain", 0)])
            split(0, unit_parts(0, 0))
            for L in range(LAYERS):
                base = UNITS * L
                for s in range(U_FFN):
                    for n, first in enumerate((0, U_GU0)):
                        if s in (first, first + 1):
                            turn_x(L, n, s - first)
                    if L == 0 and s == 0:
                        for u in range(1, AHEAD):
                            split(u, unit_parts(0, u))
                    for name, j in steps(ACT_STEPS, L, s):
                        attention(L, name, j)
                    split_ahead(L, s)
                    if s in (1, U_GU0 + 1):
                        norm(L, 0 if s == 1 else 1)
                    if L == L_DA and s == 3:
                        wait_out(act, EV[("gain", 1)])
                        act.wait_ge(gains_ready, 1)
                    if L == L_DA and s == 4:
                        act.wait_ge(lam_dot, 2)
                        act.activation(lam[:, 2:4], lam[:, 0:2], ACT.Exp).then_inc(lam_exp, 1)
                    if L == L_SB and s == 2:
                        act.wait_ge(wf_g, 1)
                        act.activation(wfhi[:, :, :], wfg[:, :, :], ACT.Copy).then_inc(wf_hi, 1)
                    if L == L_FX and s == 3:
                        wait_out(act, EV[("flogB", L)])
                        link(act.activation(f2[:, :, :], f[:, :, :], ACT.Abs))
                        link(act.activation(f2[:, :, :], f2[:, :, :], ACT.Exp, scale=-1.0))
                        act.activation(f2[:, :, :], f2[:, :, :], ACT.Ln, bias=1.0).then_inc(f_sp, 1)
                    if s == SIDE_SLOT:
                        e = EV[("side", L)]
                        act.wait_ge(turned, e + 1)
                        act.activation(phi[:, :, :], tb[e % 2][:, :].rearrange("p (k c) -> p k c", k=2), ACT.Copy)\
                            .then_inc(turn_hi, 1)

                g0 = 13 * L
                act.wait_ge(rstd_ready, NORM[(L, 1)])
                act.wait_ge(gu_done, g0 + 1)
                hidden_sig(L, 0, acc[0])
                act.wait_ge(unit_done, base + U_GU0 + 4)
                hidden_sig(L, 1, acc[1])

                def ffn_body(i, peeled):
                    for b in range(6):
                        if b == 1:
                            for t in range(T):
                                e = EV[("g", L, 0, t)]
                                act.wait_ge(turned, i * 2 + (e + 1))
                                act.activation(ghi[:, :, t * P:(t + 1) * P],
                                               tb[e % 2][:, 0:256].rearrange("p (k c) -> p k c", k=2),
                                               ACT.Copy).then_inc(turn_hi, 1)
                        if peeled and b == 5:
                            for t in range(T):
                                e = EV[("g", L, NG - 1, t)]
                                act.wait_ge(turned, e + 1)
                                act.activation(ohi[:, 0:2, t * P:(t + 1) * P],
                                               tb[e % 2][:, 0:256].rearrange("p (k c) -> p k c", k=2),
                                               ACT.Copy).then_inc(turn_hi, 1)
                        if b == 4:
                            act.wait_ge(gu_done, i + (g0 + 2))
                            hidden_sig(L, 0, sc[:, 0, :])
                            act.wait_ge(unit_done, i * 6 + (base + U_FFN + 4))
                            hidden_sig(L, 1, sc[:, 1, :])
                        if peeled:
                            split_ahead(L, U_FFN + 6 * i + b)
                        else:
                            u = base + U_FFN + b + AHEAD
                            split(u, unit_parts(L, U_FFN + b + AHEAD), i)

                with act.Fori(0, NG - 2) as i:
                    ffn_body(i, False)
                ffn_body(NG - 2, True)

                for s in range(U_DOWN_LAST, UNITS):
                    if s in (U_PROJ + 1, U_GATE):
                        hf = s - U_PROJ - 1
                        for t in range(T):
                            if t == 0:
                                act.wait_ge(gu_done, g0 + 12 + hf)
                            else:
                                act.wait_ge(unit_done, base + U_PROJ + hf + 1)
                            act.activation(z[:, t, hf * 512:hf * 512 + 512], sc[:, t, :], ACT.Copy)\
                                .then_inc(proj_out, 1)
                    if s in (U_GATE - 1, U_GATE):
                        turn_x(L, 2, s - U_GATE + 1)
                    split_ahead(L, s)
                    if s == U_GATE:
                        norm(L, 2)
                act.wait_ge(rstd_ready, NORM[(L, 2)])
                for q in range(4):
                    hf, t = halves(q)
                    acc_wait(act, L, G_GATE, q, UNITS - 1)
                    act.activation(aT[:, t, hf * 512:hf * 512 + 512], acc[q][:, :], ACT.Sigmoid,
                                   scale=rs(L, 2, t)).then_inc(gate_sig, 1)
                if L == 1:
                    for q in range(4):
                        hf, t = halves(q)
                        act.wait_ge(bank_out[q], GROUPS * L + G_GATE + 1)
                        if q:
                            act.wait_ge(quarter_ss, q)
                        else:
                            act.wait_ge(ss_ready, 2 * NORM[(L, 2)])
                        act.activation(junk[:, 0:512], h[:, t, hf * 512:hf * 512 + 512], ACT.Square,
                                       accum_out=ss4[:, q:q + 1]).then_inc(quarter_ss, 1)

        @block.vector
        def _(dve):
            links = [0]

            def link(ins):
                links[0] += 1
                ins.then_inc(dve_link, 1)
                dve.wait_ge(dve_link, links[0])

            def split(u, parts, turns=0):
                dve.wait_ge(hi_done, turns * 6 + (u + 1))
                for c0, c1, g in parts:
                    w, hi, lo = (x[:, u % RING, c0:c1] for x in (raw, whi, wlo))
                    if g is None:
                        ins = dve.tensor_tensor(lo, w, hi.bitcast(F32), ALU.subtract)
                    else:
                        ins = dve.scalar_tensor_tensor(out=lo, in0=w, scalar=gain[:, g:g + 1],
                                                       in1=hi.bitcast(F32), op0=ALU.mult, op1=ALU.subtract)
                ins.then_inc(lo_done, 1)

            def split_ahead(L, s):
                u = UNITS * L + s + LO_AHEAD
                if u < LAYERS * UNITS:
                    split(u, unit_parts(u // UNITS, u % UNITS))

            def lo_half(label, lo, hi, src, e, turns=0, per=0):
                dve.wait_ge(turn_hi, turns * per + SPLIT[label])
                dve.tensor_tensor(lo, src, hi.bitcast(F32), ALU.subtract).then_inc(turn_out[e % 2], 1)

            def turn_x(L, n, r):
                for q in halves_at(r):
                    hf, t = halves(q)
                    e = EV[("x", L, n, q)]
                    at = (slice(None), slice(4 * hf, 4 * hf + 4), slice(t * P, (t + 1) * P))
                    lo_half(("x", L, n, q), xlo[at], xhi[at],
                            tb[e % 2][:, :].rearrange("p (k c) -> p k c", k=4), e)

            def add_to_h(L, g, last, quarters):
                for q in quarters:
                    hf, t = halves(q)
                    acc_wait(dve, L, g, q, last)
                    hq = h[:, t, hf * 512:hf * 512 + 512]
                    dve.tensor_tensor(hq, acc[q][:, :], hq, ALU.add).then_inc(bank_out[q], 1)

            def gated_side(L, quarters):
                for q in quarters:
                    hf, t = halves(q)
                    c = slice(hf * 512, hf * 512 + 512)
                    dve.wait_ge(gate_sig, 4 * L + q + 1)
                    dve.wait_ge(proj_out, 4 * L + q + 1)
                    dve.tensor_tensor(aT[:, t, c], aT[:, t, c], z[:, t, c], ALU.mult).then_inc(gated, 1)
                    dve.wait_ge(gated, 4 * L + q + 1)
                    dve.tensor_tensor(h[:, t, c], h[:, t, c], aT[:, t, c], ALU.add).then_inc(bank_out[q], 1)

            def final_norm(quarters):
                for q in quarters:
                    hf, t = halves(q)
                    c = slice(hf * 512, hf * 512 + 512)
                    dve.scalar_tensor_tensor(out=h[:, t, c], in0=h[:, t, c], scalar=rs(1, 3, t),
                                             in1=fin_gain[:, c], op0=ALU.mult, op1=ALU.mult).then_inc(fin_ready, 1)

            def scores(L, j, t):
                kk = keys(L, t)
                zt = z[:, t, :].rearrange("p (x c) -> p x c", c=S)[:, :, 0:kk]
                src = sc[:, :, :].rearrange("p q (b c) -> p (q b) c", c=S)[:, :, 0:kk]
                if L == L_DA:
                    dve.wait_ge(bias_ready, j + 1)
                elif L in (L_NA, L_SB):
                    dve.wait_ge(bias_ready, HG + T)
                elif L == L_FX:
                    dve.wait_ge(bias_ready, HG + T + j + 1)
                dve.wait_ge(scores_done, ATT[(L, j, t)])
                if L == L_SB:
                    m = strict[:, S - kk:S] if t == 0 else strict[:, :]
                    dve.scalar_tensor_tensor(out=zt, in0=src, scalar=SCALE, in1=m.unsqueeze(1).to_broadcast([P, 4, kk]),
                                             op0=ALU.mult, op1=ALU.add).then_inc(z_ready, 1)
                    return
                for x in range(4):
                    add, to, prod = bias[:, t, j, x * S:x * S + kk], zt[:, x, :], src[:, x, :]
                    if L == L_NA:
                        add, to, prod = (y.rearrange("p (r c) -> p r c", c=64) for y in (add, to, prod))
                        add = add[:, :, ::-1]
                    ins = dve.tensor_tensor_reduce(out=to, in0=prod, in1=add, scale=-SCALE, scalar=3e38, op0=ALU.add,
                                                   op1=ALU.min, accum_out=mx[:, t, x:x + 1])
                ins.then_inc(z_ready, 1)
                if L == L_FX:
                    dve.wait_ge(z_ready, ATT[(L, j, t)])
                    fq = nfc[:, t, 4 * j:4 * j + 4]
                    link(dve.tensor_tensor(mx[:, t, :], mx[:, t, :], fq, ALU.add))
                    dve.tensor_tensor(mx[:, t, :], mx[:, t, :], fq, ALU.subtract).then_inc(mx_ready, 1)

            def after_exp(L, j, t):
                kk = keys(L, t)
                if L == L_SB:
                    zt = z[:, t, :].rearrange("p (x c) -> p x c", c=S)[:, :, 0:kk]
                    tmp = aT[:, t, :].rearrange("p (x c) -> p x c", c=S)[:, :, 0:kk]
                    dve.wait_ge(sp_ready, 2 * j + t + 1)
                    for x in range(4):
                        back = tmp[:, x, ::-1]
                        ins = dve.tensor_tensor_scan(back, back, zeros_sb[:, 0:1].to_broadcast([P, kk]), 1.0,
                                                     ALU.mult, ALU.add)
                    link(ins)
                    dve.tensor_tensor(zt[:, :, 0:kk - 1], zt[:, :, 0:kk - 1], tmp[:, :, 1:kk], ALU.mult)\
                        .then_inc(arg_ready, 1)
                    return
                dve.wait_ge(e_ready, SOFT[(L, j, t)])
                link(dve.reciprocal(rsum[:, t, :], sums[:, t, :]))
                if L == L_DA:
                    link(dve.tensor_scalar(lamc[:, t, :], rsum[:, t, 2:4], lam[:, 1:2], None, ALU.mult))
                    for b in range(2):
                        e0, e1 = (z[:, t, q * 512 + b * 256:q * 512 + b * 256 + 256] for q in range(2))
                        link(dve.tensor_scalar(e1, e1, lamc[:, t, b:b + 1], None, ALU.mult))
                        ins = dve.scalar_tensor_tensor(out=e0, in0=e0, scalar=rsum[:, t, b:b + 1], in1=e1,
                                                       op0=ALU.mult, op1=ALU.add)
                    ins.then_inc(a_ready, 1)

            def attention(L, name, j):
                t = int(name[-1]) if name[-1] in "01" else 0
                B = j % 2
                if name in ("evacqk", "evacv"):
                    dve.wait_ge(rstd_ready, NORM[(L, 0)])
                    half, c0, c1 = (0, 0, 512) if name == "evacqk" else (1, 512, 768)
                    if L == L_NA:
                        dve.wait_ge(nab_in[B], 16 * (j // 2 + 1))
                        for t in range(T):
                            b = 2 * half + t
                            acc_wait(dve, L, j, b, GROUP_UNITS * j + (GROUP_UNITS if half else QK_UNITS) - 1)
                            dve.scalar_tensor_tensor(out=qkv[:, B, t, c0:c1], in0=acc[b][:, 0:c1 - c0],
                                                     scalar=rs(L, 0, t), in1=nab[:, B, c0:c1], op0=ALU.mult,
                                                     op1=ALU.add).then_inc(bank_out[b], 1)
                    elif half:
                        for t in range(T):
                            acc_wait(dve, L, j, 2 + t, GROUP_UNITS * (j + 1) - 1)
                            dve.tensor_scalar(qkv[:, B, t, c0:c1], acc[2 + t][:, 0:256], rs(L, 0, t), None,
                                              ALU.mult).then_inc(bank_out[2 + t], 1)
                    if L == L_FX and not half:
                        for t in range(T):
                            dve.wait_ge(sq_ready, 2 * j + t + 1)
                            dve.tensor_reduce(ss_h[:, t, :], nab[:, t, 0:512].rearrange("p (x c) -> p x c", c=64),
                                              AX_X, ALU.add).then_inc(sh_ready, 1)
                elif name == "turnqk":
                    for t in range(T):
                        e, at = EV[("qk", L, j, t)], (slice(None), slice(None), slice(t * P, (t + 1) * P))
                        lo_half(("qk", L, j, t), qklo[at], qkT[at],
                                tb[e % 2][:, :].rearrange("p (k c) -> p k c", k=4), e)
                elif name == "headnorm":
                        for t in range(T):
                            dve.wait_ge(rh_ready, 2 * j + t + 1)
                            x = qkv[:, B, t, 0:512].rearrange("p (x c) -> p x c", c=64)
                            dve.tensor_tensor(x, x, r_h[:, t, :].unsqueeze(2).to_broadcast([P, 8, 64]), ALU.mult)\
                                .then_inc(qk_ready, 1)
                elif name == "scores0":
                    scores(L, j, 0)
                elif name == "scores1":
                    scores(L, j, 1)
                elif name.startswith("post"):
                    after_exp(L, j, t)
                elif name.startswith("turnp"):
                    if ("p", L, j, t, 1) in EV:
                        e = EV[("p", L, j, t, 1)]
                        dve.wait_ge(turned, e + 1)
                        dve.tensor_copy(aT[:, t, 512:1024], tb[e % 2][:, :]).then_inc(turn_out[e % 2], 1)
                elif name.startswith("pv"):
                    e = EV[("pv", L, j, t)]
                    src = tb[e % 2]
                    if L == L_DA:
                        dve.wait_ge(ro_ready, 2 * j + t + 1)
                        dve.tensor_tensor(o[:, t, :].rearrange("p (x c) -> p x c", x=2),
                                          src[:, 0:256].rearrange("p (x c) -> p x c", x=2),
                                          r_o[:, t, :].unsqueeze(2).to_broadcast([P, 2, P]), ALU.mult)\
                            .then_inc(turn_out[e % 2], 1)
                    elif L != L_SB:
                        dve.wait_ge(turned, e + 1)
                        r = rsum[:, t, :].rearrange("p (q b) -> p b q", q=2)
                        dve.tensor_tensor(o[:, t, :].rearrange("p (b q c) -> p b q c", b=2, q=2),
                                          src[:, 0:256].rearrange("p (b q c) -> p b q c", b=2, q=2),
                                          r.unsqueeze(3).to_broadcast([P, 2, 2, 64]), ALU.mult)\
                            .then_inc(turn_out[e % 2], 1)
                elif name == "turno":
                    e = EV[("o", L, j)]
                    at = (slice(None), slice(2 * j, 2 * j + 2))
                    lo_half(("o", L, j), olo[at], ohi[at], tb[e % 2][:, :].rearrange("p (k c) -> p k c", k=2), e)

            def hidden(L, banks, wait_base, turns=0, per=0):
                for t in range(T):
                    sg = aT[:, 0, t * 256:t * 256 + 256]
                    dve.wait_ge(sig_done, turns * per + (wait_base + t + 1))
                    dve.scalar_tensor_tensor(out=sg, in0=banks[t][:, 256:512], scalar=rs(L, 1, t), in1=sg,
                                             op0=ALU.mult, op1=ALU.mult).then_inc(gmid, 1)
                for t in range(T):
                    sg = aT[:, 0, t * 256:t * 256 + 256]
                    dve.wait_ge(gmid, turns * per + (wait_base + t + 1))
                    dve.scalar_tensor_tensor(out=aT[:, 1, t * 256:t * 256 + 256], in0=banks[t][:, 0:256],
                                             scalar=rs(L, 1, t), in1=sg, op0=ALU.mult, op1=ALU.mult)\
                        .then_inc(gu_out, 1)

            dve.memset(zeros_sb[:, :], 0.0).then_inc(zero_ready, 1)
            dve.wait_ge(zero_ready, 1)
            dve.memset(ones_sb[:, :], 1.0).then_inc(consts, 1)
            dve.wait_ge(turned, EV[("gain", 0)] + 1)
            dve.tensor_copy(gain[:, 0:16], tb[0][:, 0:16]).then_inc(turn_out[0], 1)
            wait_out(dve, EV[("gain", 0)])
            split(0, unit_parts(0, 0))
            for L in range(LAYERS):
                base = UNITS * L
                for s in range(U_FFN):
                    if s == U_GU0:
                        add_to_h(L, G_WO, U_GU0 - 1, halves_at(0))
                    for n, first in enumerate((0, U_GU0)):
                        if s in (first, first + 1):
                            turn_x(L, n, s - first)
                    if s == 0 and L in (1, 3):
                        gated_side(L - 1, halves_at(1))
                    if s == 0 and L == 2:
                        final_norm(halves_at(1))
                    if s == U_GU0:
                        add_to_h(L, G_WO, U_GU0 - 1, halves_at(1))
                    if L == 0 and s == 0:
                        for u in range(1, LO_AHEAD):
                            split(u, unit_parts(0, u))
                    if L == L_FX and s == 2:
                        e = EV[("flog", L)]
                        dve.wait_ge(turned, e + 1)
                        dve.tensor_copy(fT, tb[e % 2][0:16, 0:S]).then_inc(turn_out[e % 2], 1)
                    if L == L_FX and s == 3:
                        e = EV[("flogB", L)]
                        dve.wait_ge(rstd_ready, NORM[(L, 0)])
                        dve.wait_ge(turned, e + 1)
                        bp = bf[:, :].rearrange("p (j b q) -> p q j b", q=2, b=2)
                        for t in range(T):
                            for q in range(2):
                                fd = f[:, t, :].rearrange("p (j q b) -> p q j b", q=2, b=2)[:, q]
                                fs = tb[e % 2][:, 16 * t:16 * t + 16].rearrange("p (j q b) -> p q j b", q=2, b=2)[:, q]
                                ins = dve.scalar_tensor_tensor(out=fd, in0=fs, scalar=rs(L, 0, t), in1=bp[:, q],
                                                               op0=ALU.mult, op1=ALU.add)
                        ins.then_inc(turn_out[e % 2], 1)
                    if L == L_FX and s == 5:
                        e = EV[("flogT", L)]
                        dve.wait_ge(turned, e + 1)
                        dve.tensor_copy(fT, tb[e % 2][0:16, 0:S]).then_inc(turn_out[e % 2], 1)
                        wait_out(dve, e)
                        dve.wait_ge(consts, 2)
                        dve.tensor_tensor_scan(nfcT, ones_sb[0:16, 0:1].to_broadcast([16, S]), fT, 0.0, ALU.mult, ALU.add)\
                            .then_inc(nfc_ready, 1)
                    if L == L_FX and s == 6:
                        e = EV[("fcum", L)]
                        dve.wait_ge(turned, e + 1)
                        ins = dve.tensor_scalar(nfc[:, :, :], tb[e % 2][:, 0:32].rearrange("p (t c) -> p t c", t=T),
                                                SCALE, None, ALU.mult)
                        ins.then_inc(turn_out[e % 2], 1)
                        wait_out(dve, e)
                    if L == L_FX and s == 4:
                        dve.wait_ge(f_sp, 1)
                        link(dve.tensor_scalar(f[:, :, :], f[:, :, :], 0.0, 1.0 / SCALE, ALU.min, ALU.mult))
                        dve.scalar_tensor_tensor(out=f2[:, :, :], in0=f2[:, :, :], scalar=1.0 / SCALE,
                                                 in1=f[:, :, :], op0=ALU.mult, op1=ALU.subtract).then_inc(f_ready, 1)
                    for name, j in steps(DVE_STEPS, L, s):
                        attention(L, name, j)
                    split_ahead(L, s)
                    if L == L_DA and s == 3:
                        e = EV[("gain", 1)]
                        dve.wait_ge(turned, e + 1)
                        dve.tensor_copy(gain[:, 16:GAIN_ROWS], tb[e % 2][:, 16:GAIN_ROWS]).then_inc(turn_out[e % 2], 1)
                        wait_out(dve, e)
                        dve.tensor_scalar(gain[:, GAIN_SUB:GAIN_SUB + 1], gain[:, GAIN_SUB:GAIN_SUB + 1],
                                          1.0 - LAM_INIT, None, ALU.mult).then_inc(gains_ready, 1)
                        dve.wait_ge(gains_ready, 1)
                        dve.wait_ge(misc_in, 16 * 7)
                        for i in range(2):
                            dve.tensor_tensor_reduce(out=lam_in[:, 2 * i, :], in0=lam_in[:, 2 * i, :],
                                                     in1=lam_in[:, 2 * i + 1, :], scale=1.0, scalar=0.0,
                                                     op0=ALU.mult, op1=ALU.add, accum_out=lam[:, i:i + 1])\
                                .then_inc(lam_dot, 1)
                    if L == L_DA and s == 5:
                        dve.wait_ge(lam_exp, 1)
                        link(dve.tensor_tensor(lam[:, 0:1], lam[:, 3:4], lam[:, 2:3], ALU.subtract))
                        link(dve.tensor_scalar(lam[:, 1:2], lam[:, 0:1], -LAM_INIT, None, ALU.add))
                    if L == L_SB and s == 1:
                        dst = wfg[:, :, :].rearrange("p k (j q b) -> p q (k j) b", q=2, b=2)
                        src = wf[:, :, :].rearrange("p k (j b q) -> p q (k j) b", q=2, b=2)
                        for kb in range(KB):
                            for q in range(2):
                                gg = gain[:, GAIN_SHARED + kb:GAIN_SHARED + kb + 1]
                                ins = dve.tensor_scalar(dst[:, q, 4 * kb:4 * kb + 4], src[:, q, 4 * kb:4 * kb + 4],
                                                        gg, None, ALU.mult)
                        ins.then_inc(wf_g, 1)
                    if L == L_SB and s == 3:
                        dve.wait_ge(wf_hi, 1)
                        dve.tensor_tensor(wflo[:, :, :], wfg[:, :, :], wfhi[:, :, :].bitcast(F32), ALU.subtract)\
                            .then_inc(wf_ready, 1)
                    if s == SIDE_SLOT:
                        e = EV[("side", L)]
                        lo_half(("side", L), plo[:, :, :], phi[:, :, :],
                                tb[e % 2][:, :].rearrange("p (k c) -> p k c", k=2), e)

                dve.wait_ge(rstd_ready, NORM[(L, 1)])
                hidden(L, acc, 2 * NG * L)

                def ffn_body(i, peeled):
                    for b in range(6):
                        if b == 1:
                            for t in range(T):
                                e = EV[("g", L, 0, t)]
                                at = (slice(None), slice(None), slice(t * P, (t + 1) * P))
                                lo_half(("g", L, 0, t), glo[at], ghi[at],
                                        tb[e % 2][:, 0:256].rearrange("p (k c) -> p k c", k=2), e, i, 2)
                        if peeled and b == 5:
                            for t in range(T):
                                e = EV[("g", L, NG - 1, t)]
                                at = (slice(None), slice(0, 2), slice(t * P, (t + 1) * P))
                                lo_half(("g", L, NG - 1, t), olo[at], ohi[at],
                                        tb[e % 2][:, 0:256].rearrange("p (k c) -> p k c", k=2), e)
                        if b == 4:
                            hidden(L, [sc[:, t, :] for t in range(T)], 2 * NG * L + 2, i, 2)
                        if peeled:
                            split_ahead(L, U_FFN + 6 * i + b)
                        else:
                            split(base + U_FFN + b + LO_AHEAD, unit_parts(L, U_FFN + b + LO_AHEAD), i)

                with dve.Fori(0, NG - 2) as i:
                    ffn_body(i, False)
                ffn_body(NG - 2, True)

                for s in range(U_DOWN_LAST, UNITS):
                    if s == U_PROJ:
                        add_to_h(L, G_DOWN, U_PROJ - 1, range(4))
                    if s in (U_GATE - 1, U_GATE):
                        turn_x(L, 2, s - U_GATE + 1)
                    split_ahead(L, s)
                if L in (0, 2):
                    gated_side(L, halves_at(0))
                else:
                    gated_side(L, range(4))
                if L == 1:
                    dve.wait_ge(rstd_ready, NORM[(1, 3)])
                    dve.wait_ge(misc_in, 16 * 7)
                    final_norm(halves_at(0))

        @block.tensor
        def _(pe):
            def use(e, turns=0):
                if e >= 2:
                    pe.wait_ge(turn_out[e % 2], turns + e // 2)

            def ready(u, turns=0):
                pe.wait_ge(lo_done, turns * 6 + (u + 1))

            def three(dst, xh, xl, wh, wl, first, last):
                pe.matmul(dst, xh, wh, start=first, stop=False)
                pe.matmul(dst, xh, wl, start=False, stop=False)
                return pe.matmul(dst, xl, wh, start=False, stop=last)

            def wide_unit(L, s, kb, xh, xl, first, last, g, turns=0, midway=None):
                u = UNITS * L + s
                ready(u, turns)
                for b in range(4):
                    half, t = halves(b)
                    cols = slice(half * 512, half * 512 + 512)
                    if midway and b == 2:
                        midway()
                    if first and GROUPS * L + g:
                        pe.wait_ge(bank_out[b], GROUPS * L + g)
                    ins = three(acc[b][:, :], xh[:, kb, t * P:(t + 1) * P], xl[:, kb, t * P:(t + 1) * P],
                                whi[:, u % RING, cols], wlo[:, u % RING, cols], first, last)
                    if last and b < 3:
                        ins.then_inc(acc_done, 1)
                ins.then_inc(unit_done, 1)

            def early_turno(L, s):
                return L in (L_SB, L_FX) and s == U_WO + KB - 2

            def x_wait(L, n, s, first, t):
                if s in (first, first + 2):
                    wait_out(pe, EV[("x", L, n, (2 if s > first else 0) + t)])

            def qkv_unit(L, s):
                u, j, b = UNITS * L + s, s // GROUP_UNITS, s % GROUP_UNITS
                ready(u)
                first, last = b in (0, QK_UNITS), b in (QK_UNITS - 1, GROUP_UNITS - 1)
                half, at, blocks = (0, 2 * b, 2) if b < QK_UNITS else (1, 4 * (b - QK_UNITS), 4)
                w = 1024 // blocks
                for t in range(T):
                    bank = 2 * half + t
                    x_wait(L, 0, s, 0, t)
                    if first and GROUPS * L + j:
                        pe.wait_ge(bank_out[bank], GROUPS * L + j)
                    for k in range(blocks):
                        ins = three(acc[bank][:, 0:w], xhi[:, at + k, t * P:(t + 1) * P],
                                    xlo[:, at + k, t * P:(t + 1) * P], whi[:, u % RING, w * k:w * k + w],
                                    wlo[:, u % RING, w * k:w * k + w], first and k == 0, last and k == blocks - 1)
                    if last and t == 0:
                        ins.then_inc(acc_done, 1)
                ins.then_inc(unit_done, 1)

            def gu_unit(L, s, b, turns=0):
                u = UNITS * L + s
                ready(u, turns)
                for t in range(T):
                    dst = acc[t][:, :] if s < U_FFN else sc[:, t, :]
                    x_wait(L, 1, s, U_GU0, t)
                    if b == 0 and s >= U_FFN:
                        if isinstance(turns, int) and turns == 0:
                            pe.wait_ge(z_ready, ATT[(L, HG - 1, T - 1)])
                        else:
                            pe.wait_ge(gu_out, turns * 2 + (2 * NG * L + t + 1))
                    for k in range(2):
                        ins = three(dst, xhi[:, 2 * b + k, t * P:(t + 1) * P],
                                    xlo[:, 2 * b + k, t * P:(t + 1) * P],
                                    whi[:, u % RING, 512 * k:512 * k + 512],
                                    wlo[:, u % RING, 512 * k:512 * k + 512], b == 0 and k == 0, b == 3 and k == 1)
                    if b == 3 and t == 0:
                        ins.then_inc(gu_done, 1)
                ins.then_inc(unit_done, 1)

            def proj_unit(L, s, half):
                u = UNITS * L + s
                ready(u)
                for t in range(T):
                    if half == 0:
                        pe.wait_ge(gu_out, 2 * NG * L + 2 * (NG - 1) + t + 1)
                    else:
                        pe.wait_ge(proj_out, 4 * L + t + 1)
                    for k in range(2):
                        ins = three(sc[:, t, :], phi[:, k, t * P:(t + 1) * P], plo[:, k, t * P:(t + 1) * P],
                                    whi[:, u % RING, 512 * k:512 * k + 512],
                                    wlo[:, u % RING, 512 * k:512 * k + 512], k == 0, k == 1)
                    if t == 0:
                        ins.then_inc(gu_done, 1)
                ins.then_inc(unit_done, 1)

            def turn(e, blocks, width=P):
                for n, src in enumerate(blocks):
                    rows, cols = src.shape[0], src.shape[1]
                    ins = pe.transpose(tb[e % 2][0:cols, n * rows:(n + 1) * rows], src, ident[0:rows, 0:rows])
                ins.then_inc(turned, 1)

            def turn_x(L, n, r, h_ready):
                for q in halves_at(r):
                    hf, t = halves(q)
                    e = EV[("x", L, n, q)]
                    use(e)
                    h_ready(q)
                    turn(e, [h[:, t, (4 * hf + k) * P:(4 * hf + k + 1) * P] for k in range(4)])

            def attention(L, name, j):
                t = int(name[-1]) if name[-1] in "01" else 0
                B = j % 2
                if name == "turnqk":
                    for t in range(T):
                        e = EV[("qk", L, j, t)]
                        use(e)
                        if L == L_FX:
                            pe.wait_ge(qk_ready, 2 * j + t + 1)
                        else:
                            pe.wait_ge(bank_out[t], GROUPS * L + j + 1)
                        turn(e, [qkv[:, B, t, k * P:(k + 1) * P] for k in range(4)])
                elif name.startswith("scores"):
                    for tt in range(T):
                        wait_out(pe, EV[("qk", L, j, tt)])
                    n = ATT[(L, j, t)] - 1
                    if n:
                        pe.wait_ge(z_ready, n)
                    if L and j == 0 and t == 0:
                        pe.wait_ge(proj_out, 4 * L)
                    kk = keys(L, t)
                    for q in range(2):
                        for b in range(2):
                            rows, tile = slice(64 * q, 64 * q + 64), slice(t * P, (t + 1) * P)
                            dst = sc[:, q, b * S:b * S + kk]
                            if split_scores(L):
                                ins = three(dst, qkT[rows, b, tile], qklo[rows, b, tile], qkT[rows, 2 + b, 0:kk],
                                            qklo[rows, 2 + b, 0:kk], True, True)
                            else:
                                ins = pe.matmul(dst, qk32[rows, b, tile], qk32[rows, 2 + b, 0:kk], start=True,
                                                stop=True)
                    ins.then_inc(scores_done, 1)
                elif name.startswith("turnp"):
                    if L == L_DA:
                        pe.wait_ge(a_ready, 2 * j + t + 1)
                    elif L == L_SB:
                        pe.wait_ge(arg_ready, 2 * j + t + 1)
                    else:
                        pe.wait_ge(e_ready, SOFT[(L, j, t)])
                    blocks = p_blocks(L, t)
                    for n in range(len(blocks) // 4):
                        e = EV[("p", L, j, t, n)]
                        use(e)
                        turn(e, [z[:, t, q * 512 + b * 256 + k * P:q * 512 + b * 256 + (k + 1) * P]
                                 for q, b, k in blocks[4 * n:4 * n + 4]])
                elif name.startswith("pv"):
                    e = EV[("pv", L, j, t)]
                    use(e)
                    blocks = p_blocks(L, t)
                    for n in range(len(blocks) // 4):
                        wait_out(pe, EV[("p", L, j, t, n)])
                    nk = keys(L, t) // P
                    for kt in range(nk):
                        pe.wait_ge(bank_out[2 + kt], GROUPS * L + j + 1)
                    for n, (q, b, k) in enumerate(blocks):
                        w = P if L == L_DA else 64
                        c = b * P + (0 if L == L_DA else 64 * q)
                        ins = pe.matmul(tb[e % 2][:, c:c + w], aT[:, t, n * P:(n + 1) * P],
                                        qkv[:, B, k, 512 + c:512 + c + w], start=(k == 0), stop=(k == nk - 1))
                    ins.then_inc(turned, 1)
                elif name == "turno":
                    e = EV[("o", L, j)]
                    use(e)
                    for t in range(T):
                        wait_out(pe, EV[("pv", L, j, t)])
                    turn(e, [o[:, t, k * P:(k + 1) * P] for k in range(2) for t in range(T)])

            def turn_g(L, g, wait, turns=0):
                for t in range(T):
                    e = EV[("g", L, g, t)]
                    use(e, turns)
                    pe.wait_ge(gu_out, turns * 2 + (wait + t + 1))
                    turn(e, [aT[:, 1, t * 256 + k * P:t * 256 + (k + 1) * P] for k in range(2)])

            def down_unit(L, s, b, g, first, last, turns=0):
                gh, gl = (ohi, olo) if last is not None else (ghi, glo)
                if b == 0:
                    for t in range(T):
                        e = EV[("g", L, g, t)]
                        pe.wait_ge(turn_out[e % 2], turns + (e // 2 + 1))
                wide_unit(L, s, b, gh, gl, first, bool(last), G_DOWN, turns)

            pe.wait_ge(consts, 2)
            pe.wait_ge(first_gains_in, 16)
            turn(EV[("gain", 0)], [gain_rows[0:16, :]])

            for L in range(LAYERS):
                def h_start(q):
                    if L == 0:
                        pe.wait_ge(x_in[q], 16)
                    elif L == 2:
                        pe.wait_ge(fin_ready, q + 1)
                    else:
                        pe.wait_ge(bank_out[q], GROUPS * L)
                for s in range(U_FFN):
                    if s in (0, 1):
                        turn_x(L, 0, s, h_start)
                    if s in (U_GU0, U_GU0 + 1):
                        turn_x(L, 1, s - U_GU0, lambda q: pe.wait_ge(bank_out[q], GROUPS * L + G_WO + 1))
                    if L == L_DA and s == 3:
                        use(EV[("gain", 1)])
                        pe.wait_ge(gains_in, 16 * 11)
                        turn(EV[("gain", 1)], [gain_rows[0:GAIN_ROWS, :]])
                    if L == L_FX and s in FORGET:
                        e = EV[(FORGET[s], L)]
                        use(e)
                        if FORGET[s] == "flog":
                            pe.wait_ge(wf_ready, 1)
                            wait_out(pe, EV[("x", L, 0, 2)])
                            wait_out(pe, EV[("x", L, 0, 3)])
                            for kb in range(KB):
                                ins = three(tb[e % 2][0:16, 0:S], wfhi[:, kb, :], wflo[:, kb, :], xhi[:, kb, :],
                                            xlo[:, kb, :], kb == 0, kb == KB - 1)
                            ins.then_inc(turned, 1)
                        elif FORGET[s] == "flogB":
                            wait_out(pe, EV[("flog", L)])
                            turn(e, [fT[:, t * P:(t + 1) * P] for t in range(T)])
                        elif FORGET[s] == "flogT":
                            pe.wait_ge(f_ready, 1)
                            turn(e, [f2[:, t, :] for t in range(T)])
                        else:
                            pe.wait_ge(nfc_ready, 1)
                            turn(e, [nfcT[:, t * P:(t + 1) * P] for t in range(T)])
                    for name, j in steps(PE_STEPS, L, s):
                        if not (name == "turno" and early_turno(L, s)):
                            attention(L, name, j)
                    if s == SIDE_SLOT:
                        e = EV[("side", L)]
                        use(e)
                        pe.wait_ge(side_in, 16 * (L + 1))
                        turn(e, [side[:, t, k * P:(k + 1) * P] for k in range(2) for t in range(T)])
                    if s < U_WO:
                        qkv_unit(L, s)
                    elif s < U_GU0:
                        kb = s - U_WO
                        wait_out(pe, EV[("o", L, kb // 2)])
                        wide_unit(L, s, kb, ohi, olo, kb == 0, kb == KB - 1, G_WO,
                                  midway=(lambda: attention(L, "turno", HG - 1)) if early_turno(L, s + 1) else None)
                    else:
                        gu_unit(L, s, s - U_GU0)

                def ffn_body(i, first=False, last=False):
                    for b in range(4):
                        if b == 1:
                            turn_g(L, 0, 2 * NG * L, i)
                        gu_unit(L, U_FFN + b, b, i)
                    for b in range(2):
                        if last and b == 1:
                            turn_g(L, NG - 1, 2 * NG * L + 2 * (NG - 1))
                        down_unit(L, U_FFN + 4 + b, b, 0, first and b == 0, None, i)

                ffn_body(0, first=True)
                with pe.Fori(1, NG - 2) as i:
                    ffn_body(i)
                ffn_body(NG - 2, last=True)
                for b in range(2):
                    down_unit(L, U_DOWN_LAST + b, b, NG - 1, False, b == 1)
                for b in range(2):
                    proj_unit(L, U_PROJ + b, b)
                    turn_x(L, 2, b, lambda q: pe.wait_ge(bank_out[q], GROUPS * L + G_DOWN + 1))
                for kb in range(KB):
                    if kb in (0, 4):
                        for q in range(2):
                            wait_out(pe, EV[("x", L, 2, q + (2 if kb else 0))])
                    wide_unit(L, U_GATE + kb, kb, xhi, xlo, kb == 0, kb == KB - 1, G_GATE)


_INS = ['x', 'p', 'norm_mix', 'norm_ffn', 'norm_ple', 'norm_final', 'da_w_qkv', 'da_w_o', 'da_lambda_q1',
        'da_lambda_k1', 'da_lambda_q2', 'da_lambda_k2', 'da_subln', 'na_w_qkv', 'na_b_qkv', 'na_rpb', 'na_w_o',
        'ffn_w_gate', 'ffn_w_up', 'ffn_w_down', 'ple_w_proj', 'ple_w_gate', 'p_2', 'attn_norm_g_2', 'sb_w_qkv_2',
        'sb_w_o_2', 'shared_norm_g_2', 'shared_w_kvf_2', 'shared_b_f_2', 'shared_k_norm_g_2', 'fox_w_q_2',
        'fox_q_norm_g_2', 'fox_w_o_2', 'ffn_norm_g_2', 'ffn_w_gu_2', 'ffn_w_d_2', 'ple_norm_g_2', 'ple_w_gate_2',
        'ple_w_proj_2']


def kernel(**inputs):
    import numpy as _np
    import concourse.bacc as _bacc
    from concourse import mybir as _mybir
    from concourse.bass_utils import run_bass_kernel_spmd as _run

    nc = _bacc.Bacc("TRN2", target_bir_lowering=False, num_devices=1)
    arrays, args = {}, {}
    for name in _INS:
        x = _np.ascontiguousarray(inputs[name])
        arrays[f"in_{name}"] = x
        args[name] = nc.dram_tensor(f"in_{name}", x.shape, _mybir.dt.from_np(x.dtype), kind="ExternalInput").ap()
    out = nc.dram_tensor("out", (1, S, D), _mybir.dt.float32, kind="ExternalOutput").ap()
    build(nc, args, out)
    r = _run(nc, [arrays], core_ids=[0])
    return r.results[0]["out"]
```
